# Optimizing a Trainium2 kernel written in Bass

```python
import math
import jax, jax.numpy as jnp
from jax import lax
import numpy as np

D_MODEL = 2048
BATCH = 1
SEQ = 256
DEPTH = 1

A_HEADS = 8
A_EXPAND = 128
A_HEAD_V = 128
A_WIDTH = A_HEADS * A_EXPAND
A_CHUNK = 16
B_GROUPS = ((128, 1), (512, 4), (2048, 16))
B_HEADS_PER_GROUP = 4
B_HEADS = B_HEADS_PER_GROUP * len(B_GROUPS)
B_HEAD_DIM = 64
B_WIDTH = B_HEADS * B_HEAD_DIM
B_OUT = B_HEADS_PER_GROUP * B_HEAD_DIM
C_WIDTH = 768
C_KERNEL = 31
REL_BUCKETS = 32
REL_MAX_DIST = 2048
D_FF = 4 * D_MODEL
N_BRANCH = 3
IN_SPLITS = (A_WIDTH, A_WIDTH, A_HEADS * A_HEAD_V, A_HEADS * A_HEAD_V,
             B_WIDTH, B_WIDTH, B_WIDTH, C_WIDTH, C_WIDTH)
IN_WIDTH = sum(IN_SPLITS)
EPS = 1e-6
MASK_VALUE = -1e30
TINY = 1e-30


def rms_norm(x, w):
    xf = x.astype(jnp.float32)
    y = xf * lax.rsqrt(jnp.mean(xf * xf, axis=-1, keepdims=True) + EPS)
    return (y * w).astype(x.dtype)

def layer_norm(x, g, b):
    xf = x.astype(jnp.float32)
    mu = jnp.mean(xf, axis=-1, keepdims=True)
    var = jnp.mean(jnp.square(xf - mu), axis=-1, keepdims=True)
    return ((xf - mu) * lax.rsqrt(var + EPS) * g + b).astype(x.dtype)

def split_cols(a, sizes):
    idx = [int(v) for v in np.cumsum(sizes)[:-1]]
    return jnp.split(a, idx, axis=-1)

def hgrn2_mixer(q_pre, f_pre, inp, og, lb, norm_w):
    f32 = jnp.float32
    Bsz, S, _ = q_pre.shape
    H, K, V, C = A_HEADS, A_EXPAND, A_HEAD_V, A_CHUNK
    N = S // C

    def chunks(a, d):
        return a.astype(f32).reshape(Bsz, N, C, H, d).transpose(0, 3, 1, 2, 4)

    lb = jnp.maximum(lb.astype(f32), 0.0).reshape(H, K)[None, :, None, None, :]
    z = chunks(f_pre, K)
    log_f = jnp.logaddexp(jnp.log(lb + TINY), jnp.log1p(-lb) + jax.nn.log_sigmoid(z))
    k = (1.0 - lb) * jax.nn.sigmoid(-z)
    q = jax.nn.silu(chunks(q_pre, K))
    v = chunks(inp, V)
    b = jnp.cumsum(log_f, axis=3)
    causal = jnp.tril(jnp.ones((C, C), bool))
    decay = jnp.exp(jnp.where(causal[:, :, None],
                              b[..., :, None, :] - b[..., None, :, :], MASK_VALUE))
    attn = jnp.einsum('bhntk,bhntsk,bhnsk->bhnts', q, decay, k)
    o = jnp.einsum('bhnts,bhnsv->bhntv', attn, v)
    b_last = b[..., -1, :]
    delta = jnp.einsum('bhnck,bhncv->bhnkv', k * jnp.exp(b_last[..., None, :] - b), v)

    def step(state, xs):
        dec, dlt = xs
        return dec[..., None] * state + dlt, state

    _, s_prev = lax.scan(step, jnp.zeros((Bsz, H, K, V), f32),
                         (jnp.moveaxis(jnp.exp(b_last), 2, 0), jnp.moveaxis(delta, 2, 0)))
    s_prev = jnp.moveaxis(s_prev, 0, 2)
    o = o + jnp.einsum('bhnck,bhnkv->bhncv', q * jnp.exp(b), s_prev)
    o = o.transpose(0, 2, 3, 1, 4).reshape(Bsz, S, H, V)
    o = rms_norm(o, norm_w) * jax.nn.silu(og.astype(f32).reshape(Bsz, S, H, V))
    return o.reshape(Bsz, S, H * V).astype(q_pre.dtype)

def t5_bucket(dist):
    exact = REL_BUCKETS // 2
    d = jnp.maximum(dist, 1).astype(jnp.float32)
    large = exact + (jnp.log(d / exact) / math.log(REL_MAX_DIST / exact)
                     * (REL_BUCKETS - exact)).astype(jnp.int32)
    return jnp.where(dist < exact, dist, jnp.clip(large, exact, REL_BUCKETS - 1))

def dilated_window_group(q, k, v, bias_tab, window, dil):
    f32 = jnp.float32
    Bsz, S, H, Dh = q.shape
    J = window // dil
    Q = J
    L = S // dil
    nb = -(-L // Q)
    Lp = nb * Q

    def strided(a):
        a = a.reshape(Bsz, L, dil, H, Dh).transpose(0, 2, 1, 3, 4)
        return jnp.pad(a, ((0, 0), (0, 0), (0, Lp - L), (0, 0), (0, 0)))

    def band(a):
        a = jnp.pad(a, ((0, 0), (0, 0), (Q, 0), (0, 0), (0, 0))).reshape(Bsz, dil, nb + 1, Q, H, Dh)
        return jnp.concatenate([a[:, :, :-1], a[:, :, 1:]], axis=3)

    qb = strided(q).reshape(Bsz, dil, nb, Q, H, Dh)
    kb, vb = band(strided(k)), band(strided(v))
    steps = jnp.arange(Q)[:, None] + Q - jnp.arange(2 * Q)[None, :]
    key_pos = jnp.arange(nb)[:, None] * Q + jnp.arange(2 * Q)[None, :] - Q
    valid = ((steps >= 0) & (steps <= J))[None] & (key_pos >= 0)[:, None, :]
    bias = bias_tab[t5_bucket(jnp.clip(steps, 0, J) * dil)].transpose(2, 0, 1)
    logits = (jnp.einsum('brnqhd,brnkhd->brnhqk', qb, kb).astype(f32) * (Dh ** -0.5)
              + bias.astype(f32))
    logits = jnp.where(valid[None, None, :, None], logits, MASK_VALUE)
    m = jnp.max(logits, axis=-1, keepdims=True)
    p = jnp.exp(logits - m)
    z = jnp.sum(p, axis=-1, keepdims=True)
    o = jnp.einsum('brnhqk,brnkhd->brnqhd', p / z, vb.astype(f32))
    lse = (m + jnp.log(z))[..., 0]
    o = o.reshape(Bsz, dil, Lp, H, Dh)[:, :, :L].transpose(0, 2, 1, 3, 4).reshape(Bsz, S, H, Dh)
    lse = (lse.transpose(0, 1, 2, 4, 3).reshape(Bsz, dil, Lp, H)[:, :, :L]
           .transpose(0, 2, 1, 3).reshape(Bsz, S, H))
    return o, lse

def dilated_attention_mixer(q, k, v, rel_bias):
    Bsz, S, _ = q.shape
    shp = (Bsz, S, B_HEADS, B_HEAD_DIM)
    q, k, v = q.reshape(shp), k.reshape(shp), v.reshape(shp)
    outs, lses = [], []
    for g, (window, dil) in enumerate(B_GROUPS):
        hs = slice(g * B_HEADS_PER_GROUP, (g + 1) * B_HEADS_PER_GROUP)
        o, lse = dilated_window_group(q[:, :, hs], k[:, :, hs], v[:, :, hs],
                                      rel_bias[:, hs], window, dil)
        outs.append(o)
        lses.append(lse)
    alpha = jax.nn.softmax(jnp.stack(lses, axis=0), axis=0)
    out = jnp.sum(alpha[..., None] * jnp.stack(outs, axis=0), axis=0)
    return out.reshape(Bsz, S, B_OUT).astype(q.dtype)

def conv_module(a, gate, conv_w, conv_b, ln_g, ln_b):
    u = a * jax.nn.sigmoid(gate)
    y = lax.conv_general_dilated(u, conv_w[:, None, :], window_strides=(1,),
                                 padding=((C_KERNEL - 1, 0),),
                                 dimension_numbers=('NWC', 'WIO', 'NWC'),
                                 feature_group_count=C_WIDTH) + conv_b
    return jax.nn.silu(layer_norm(y, ln_g, ln_b))

def first_inputs(seed: int = 0) -> dict:
    key = jax.random.key(seed)
    ks = jax.random.split(key, 26)
    f32 = jnp.float32

    def nrm(k, shape, scale):
        return jax.random.normal(k, shape, f32) * scale

    D = D_MODEL
    return {
        "x": nrm(ks[0], (BATCH, SEQ, D), 1.0),
        "c": nrm(ks[1], (BATCH, D), 1.0),
        "rel_bias": nrm(ks[2], (REL_BUCKETS, B_HEADS), 0.5),
        "hgrn_lb_logits": nrm(ks[3], (DEPTH, A_WIDTH), 1.0),
        "w_ada": nrm(ks[4], (DEPTH, D, 6 * D), 0.3 * D ** -0.5),
        "b_ada": nrm(ks[5], (DEPTH, 6 * D), 0.02),
        "mix_norm_pre": 1.0 + nrm(ks[6], (DEPTH, D), 0.05),
        "mix_norm_post": 1.0 + nrm(ks[7], (DEPTH, D), 0.05),
        "w_in": nrm(ks[8], (DEPTH, D, IN_WIDTH), D ** -0.5),
        "w_gate": nrm(ks[9], (DEPTH, D, N_BRANCH * D), D ** -0.5),
        "b_gate": nrm(ks[10], (DEPTH, N_BRANCH * D), 0.02),
        "hgrn_norm_w": 1.0 + nrm(ks[11], (DEPTH, A_HEAD_V), 0.05),
        "conv_w": nrm(ks[12], (DEPTH, C_KERNEL, C_WIDTH), C_KERNEL ** -0.5),
        "conv_b": nrm(ks[13], (DEPTH, C_WIDTH), 0.02),
        "conv_ln_g": 1.0 + nrm(ks[14], (DEPTH, C_WIDTH), 0.05),
        "conv_ln_b": nrm(ks[15], (DEPTH, C_WIDTH), 0.02),
        "w_a_out": nrm(ks[16], (DEPTH, A_HEADS * A_HEAD_V, D), (A_HEADS * A_HEAD_V) ** -0.5),
        "w_b_out": nrm(ks[17], (DEPTH, B_OUT, D), B_OUT ** -0.5),
        "w_c_out": nrm(ks[18], (DEPTH, C_WIDTH, D), C_WIDTH ** -0.5),
        "w_o": nrm(ks[19], (DEPTH, D, D), D ** -0.5),
        "mlp_norm_pre": 1.0 + nrm(ks[20], (DEPTH, D), 0.05),
        "mlp_norm_post": 1.0 + nrm(ks[21], (DEPTH, D), 0.05),
        "w_up": nrm(ks[22], (DEPTH, D, D_FF), D ** -0.5),
        "w_down": nrm(ks[23], (DEPTH, D_FF, D), D_FF ** -0.5),
    }

def first_block(x, c, rel_bias, hgrn_lb_logits, w_ada, b_ada, mix_norm_pre, mix_norm_post,
              w_in, w_gate, b_gate, hgrn_norm_w, conv_w, conv_b, conv_ln_g, conv_ln_b,
              w_a_out, w_b_out, w_c_out, w_o, mlp_norm_pre, mlp_norm_post, w_up, w_down):
    Bsz, S, D = x.shape
    sm = jax.nn.softmax(hgrn_lb_logits.astype(jnp.float32), axis=0)
    lower_bounds = jnp.cumsum(sm, axis=0) - sm[0]
    c_act = jax.nn.silu(c)
    for l in range(DEPTH):
        mod = c_act @ w_ada[l] + b_ada[l]
        sh1, sc1, g1, sh2, sc2, g2 = jnp.split(mod[:, None, :], 6, axis=-1)

        h = rms_norm(x, mix_norm_pre[l]) * (1.0 + sc1) + sh1
        a_q, a_f, a_i, a_g, b_q, b_k, b_v, c_a, c_g = split_cols(h @ w_in[l], IN_SPLITS)
        ya = hgrn2_mixer(a_q, a_f, a_i, a_g, lower_bounds[l], hgrn_norm_w[l])
        yb = dilated_attention_mixer(b_q, b_k, b_v, rel_bias)
        yc = conv_module(c_a, c_g, conv_w[l], conv_b[l], conv_ln_g[l], conv_ln_b[l])
        gates = jax.nn.sigmoid(h @ w_gate[l] + b_gate[l]).reshape(Bsz, S, N_BRANCH, D)
        merged = (gates[:, :, 0] * (ya @ w_a_out[l])
                  + gates[:, :, 1] * (yb @ w_b_out[l])
                  + gates[:, :, 2] * (yc @ w_c_out[l]))
        x = x + g1 * rms_norm(merged @ w_o[l], mix_norm_post[l])

        h = rms_norm(x, mlp_norm_pre[l]) * (1.0 + sc2) + sh2
        y = jnp.square(jax.nn.relu(h @ w_up[l])) @ w_down[l]
        x = x + g2 * rms_norm(y, mlp_norm_post[l])
    return x


CTX_LEN = 256
GRID_W = 64
MIX_WIDTH = D_MODEL
MLSTM_HEAD_DIM = 128
MLSTM_HEADS = (MIX_WIDTH // 2) // MLSTM_HEAD_DIM
MLSTM_WIDTH = MLSTM_HEADS * MLSTM_HEAD_DIM
MLSTM_CHUNK = 128
DIFF_V_DIM = 128
DIFF_QK_DIM = DIFF_V_DIM // 2
DIFF_HEADS = (MIX_WIDTH - MLSTM_WIDTH) // DIFF_V_DIM
DIFF_WIDTH = DIFF_HEADS * DIFF_V_DIM
ROPE_FREQS = DIFF_QK_DIM // 4
ROPE_BASE = 10000.0
Q_BLOCK = 128
D_FF_2 = 5632
CONV_W = 3
N_MOD = 6

OFF_MQ = 0
OFF_MK = MLSTM_WIDTH
OFF_MV = 2 * MLSTM_WIDTH
OFF_MO = 3 * MLSTM_WIDTH
OFF_MG = 4 * MLSTM_WIDTH
OFF_DQ = OFF_MG + 4 * MLSTM_HEADS
OFF_DK = OFF_DQ + DIFF_HEADS * 2 * DIFF_QK_DIM
OFF_DV = OFF_DK + DIFF_HEADS * 2 * DIFF_QK_DIM
IN_COLS = OFF_DV + DIFF_WIDTH


def rmsnorm(a, g):
    a32 = a.astype(jnp.float32)
    y = a32 * lax.rsqrt(jnp.mean(a32 * a32, axis=-1, keepdims=True) + EPS)
    return (y * g.astype(jnp.float32)).astype(a.dtype)

def modulate(h, shift, scale):
    return h * (1 + scale) + shift

def dwconv3(a, w, b):
    ap = jnp.pad(a, ((0, 0), (1, 1), (0, 0)))
    return ap[:, :-2] * w[0] + ap[:, 1:-1] * w[1] + ap[:, 2:] * w[2] + b

def axial_rope_tables(rows, n_lat):
    row = jnp.broadcast_to(jnp.arange(rows, dtype=jnp.float32)[:, None], (rows, GRID_W)).reshape(-1)
    col = jnp.broadcast_to(jnp.arange(GRID_W, dtype=jnp.float32)[None, :], (rows, GRID_W)).reshape(-1)
    inv_freq = ROPE_BASE ** (-jnp.arange(ROPE_FREQS, dtype=jnp.float32) / ROPE_FREQS)
    ang = jnp.stack([row[:, None] * inv_freq, col[:, None] * inv_freq], axis=1)
    ang = jnp.stack([ang, ang], axis=2).reshape(n_lat, 4 * ROPE_FREQS)
    return jnp.cos(ang), jnp.sin(ang)

def rope_2d(x, cos, sin):
    xr = x.reshape(*x.shape[:-1], 2, 2, ROPE_FREQS)
    rot = jnp.stack([-xr[..., 1, :], xr[..., 0, :]], axis=-2).reshape(x.shape)
    return x * cos[:, None, None, :] + rot * sin[:, None, None, :]

def to_mlstm_heads(a):
    B, T, _ = a.shape
    return a.reshape(B, T, MLSTM_HEADS, MLSTM_HEAD_DIM).transpose(0, 2, 1, 3).astype(jnp.float32)

def mlstm_project(p, conv_w, conv_b, b_gate):
    B, T, _ = p.shape
    qk = jax.nn.silu(dwconv3(p[..., OFF_MQ:OFF_MV], conv_w, conv_b))
    q = to_mlstm_heads(qk[..., :MLSTM_WIDTH])
    k = to_mlstm_heads(qk[..., MLSTM_WIDTH:]) * (MLSTM_HEAD_DIM ** -0.5)
    v = to_mlstm_heads(p[..., OFF_MV:OFF_MO])
    g = (p[..., OFF_MG:OFF_DQ].reshape(B, T, 4, MLSTM_HEADS) + b_gate).astype(jnp.float32)
    g = jnp.transpose(g, (2, 0, 3, 1))
    return q, k, v, g[0], jax.nn.log_sigmoid(g[1]), g[2], jax.nn.log_sigmoid(g[3])

def mlstm_chunkwise(q, k, v, i_pre, log_f, state):
    B, H, T, Dh = q.shape
    nc = T // MLSTM_CHUNK

    def to_chunks(a):
        return jnp.moveaxis(a.reshape(B, H, nc, MLSTM_CHUNK, *a.shape[3:]), 2, 0)

    xs = (to_chunks(q), to_chunks(k), to_chunks(v), to_chunks(i_pre), to_chunks(log_f))
    causal = jnp.tril(jnp.ones((MLSTM_CHUNK, MLSTM_CHUNK), dtype=bool))

    def step(carry, inp):
        C, n, m = carry
        qc, kc, vc, ic, fc = inp
        b = jnp.cumsum(fc, axis=-1)
        d_log = jnp.where(causal, b[..., :, None] - b[..., None, :] + ic[..., None, :], -jnp.inf)
        m_inter = b + m[..., None]
        m_t = jnp.maximum(m_inter, jnp.max(d_log, axis=-1))
        w_intra = jnp.exp(d_log - m_t[..., None])
        w_inter = jnp.exp(m_inter - m_t)
        s = jnp.einsum('bhld,bhsd->bhls', qc, kc) * w_intra
        num = w_inter[..., None] * jnp.einsum('bhld,bhde->bhle', qc, C) + jnp.einsum('bhls,bhse->bhle', s, vc)
        den = w_inter * jnp.einsum('bhld,bhd->bhl', qc, n) + jnp.sum(s, axis=-1)
        h = num / jnp.maximum(jnp.abs(den), jnp.exp(-m_t))[..., None]
        b_last = b[..., -1]
        log_w = b_last[..., None] - b + ic
        m_new = jnp.maximum(b_last + m, jnp.max(log_w, axis=-1))
        w_s = jnp.exp(log_w - m_new[..., None])
        decay = jnp.exp(b_last + m - m_new)
        C_new = decay[..., None, None] * C + jnp.einsum('bhs,bhsd,bhse->bhde', w_s, kc, vc)
        n_new = decay[..., None] * n + jnp.einsum('bhs,bhsd->bhd', w_s, kc)
        return (C_new, n_new, m_new), h

    state, hs = lax.scan(step, state, xs)
    return jnp.moveaxis(hs, 0, 2).reshape(B, H, T, Dh), state

def mlstm_output(h, p, g_norm):
    B, H, T, Dh = h.shape
    h = rmsnorm(h.transpose(0, 2, 1, 3), g_norm.reshape(H, Dh)).reshape(B, T, H * Dh)
    return h * jax.nn.sigmoid(p[..., OFF_MO:OFF_MG].astype(jnp.float32))

def mlstm_group(p_lat, p_ctx, conv_w, conv_b, b_gate, g_norm, need_ctx):
    ql, kl, vl, ifl, lfl, ibl, lbl = mlstm_project(p_lat, conv_w, conv_b, b_gate)
    qc, kc, vc, ifc, lfc, ibc, lbc = mlstm_project(p_ctx, conv_w, conv_b, b_gate)
    B = p_lat.shape[0]
    zero = (jnp.zeros((B, MLSTM_HEADS, MLSTM_HEAD_DIM, MLSTM_HEAD_DIM), jnp.float32),
            jnp.zeros((B, MLSTM_HEADS, MLSTM_HEAD_DIM), jnp.float32),
            jnp.zeros((B, MLSTM_HEADS), jnp.float32))

    def rev(*arrs):
        return tuple(jnp.flip(a, axis=2) for a in arrs)

    hc_f, st_f = mlstm_chunkwise(qc, kc, vc, ifc, lfc, zero)
    hl_f, _ = mlstm_chunkwise(ql, kl, vl, ifl, lfl, st_f)
    hc_b, st_b = mlstm_chunkwise(*rev(qc, kc, vc, ibc, lbc), zero)
    hl_b, _ = mlstm_chunkwise(*rev(ql, kl, vl, ibl, lbl), st_b)
    out_lat = mlstm_output(hl_f + jnp.flip(hl_b, axis=2), p_lat, g_norm)
    out_ctx = mlstm_output(hc_f + jnp.flip(hc_b, axis=2), p_ctx, g_norm) if need_ctx else None
    return out_lat, out_ctx

def diff_split(p):
    B, T, _ = p.shape
    q = p[..., OFF_DQ:OFF_DK].reshape(B, T, DIFF_HEADS, 2, DIFF_QK_DIM)
    k = p[..., OFF_DK:OFF_DV].reshape(B, T, DIFF_HEADS, 2, DIFF_QK_DIM)
    v = p[..., OFF_DV:IN_COLS].reshape(B, T, DIFF_HEADS, DIFF_V_DIM)
    return q, k, v

def diff_attend(q, k, v, lam):
    B, Tq = q.shape[:2]
    qb = jnp.moveaxis(q.astype(jnp.float32).reshape(B, Tq // Q_BLOCK, Q_BLOCK, *q.shape[2:]), 1, 0)
    k32 = k.astype(jnp.float32)
    v32 = v.astype(jnp.float32)
    scale = DIFF_QK_DIM ** -0.5

    def one_block(qblk):
        s = jnp.einsum('bqhcd,bkhcd->bhcqk', qblk, k32) * scale
        pr = jax.nn.softmax(s, axis=-1)
        pd = pr[:, :, 0] - lam * pr[:, :, 1]
        return jnp.einsum('bhqk,bkhe->bqhe', pd, v32)

    o = lax.map(one_block, qb)
    return jnp.moveaxis(o, 0, 1).reshape(B, Tq, DIFF_HEADS, DIFF_V_DIM)

def diff_output(o, g_norm, lam_init):
    B, T = o.shape[:2]
    return (rmsnorm(o, g_norm) * (1.0 - lam_init)).reshape(B, T, DIFF_WIDTH)

def diff_group(p_lat, p_ctx, cos, sin, lam, lam_init, g_norm, need_ctx):
    ql, kl, vl = diff_split(p_lat)
    qc, kc, vc = diff_split(p_ctx)
    ql = rope_2d(ql, cos, sin)
    kl = rope_2d(kl, cos, sin)
    k_all = jnp.concatenate([kc.astype(jnp.float32), kl.astype(jnp.float32)], axis=1)
    v_all = jnp.concatenate([vc, vl], axis=1)
    out_lat = diff_output(diff_attend(ql, k_all, v_all, lam), g_norm, lam_init)
    out_ctx = diff_output(diff_attend(qc, kc, vc, lam), g_norm, lam_init) if need_ctx else None
    return out_lat, out_ctx

def conv_ffn(h, w_up, conv_w, conv_b, w_down):
    u = dwconv3(h @ w_up, conv_w, conv_b)
    gate, val = jnp.split(u, 2, axis=-1)
    return (jax.nn.silu(gate) * val) @ w_down

def second_inputs(seed: int = 0) -> dict:
    key = jax.random.key(seed)
    ks = jax.random.split(key, 32)
    f32 = jnp.float32

    def nrm(k, shape, s):
        return jax.random.normal(k, shape, f32) * s

    x = nrm(ks[0], (BATCH, SEQ, D_MODEL), 1.0)
    c = nrm(ks[1], (BATCH, D_MODEL), 1.0)
    ctx = nrm(ks[2], (BATCH, CTX_LEN, D_MODEL), 1.0)
    c_ctx = nrm(ks[3], (D_MODEL,), 1.0)
    w_mod = nrm(ks[4], (DEPTH, D_MODEL, N_MOD * D_MODEL), 0.5 * D_MODEL ** -0.5)
    b_mod = nrm(ks[5], (DEPTH, N_MOD * D_MODEL), 0.02)
    g_pre_mix = 1.0 + nrm(ks[6], (DEPTH, D_MODEL), 0.05)
    g_post_mix = 1.0 + nrm(ks[7], (DEPTH, D_MODEL), 0.05)
    w_in = nrm(ks[8], (DEPTH, D_MODEL, IN_COLS), D_MODEL ** -0.5)
    i_bias = nrm(ks[9], (DEPTH, 2, MLSTM_HEADS), 0.1)
    f_bias = 3.0 + 3.0 * jax.random.uniform(ks[10], (DEPTH, 2, MLSTM_HEADS), f32)
    b_gate = jnp.stack([i_bias[:, 0], f_bias[:, 0], i_bias[:, 1], f_bias[:, 1]], axis=1)
    conv_qk_w = nrm(ks[11], (DEPTH, CONV_W, 2 * MLSTM_WIDTH), CONV_W ** -0.5)
    conv_qk_b = nrm(ks[12], (DEPTH, 2 * MLSTM_WIDTH), 0.02)
    g_mlstm = 1.0 + nrm(ks[13], (DEPTH, MLSTM_WIDTH), 0.05)
    lambda_q1 = nrm(ks[14], (DEPTH, DIFF_QK_DIM), 0.1)
    lambda_k1 = nrm(ks[15], (DEPTH, DIFF_QK_DIM), 0.1)
    lambda_q2 = nrm(ks[16], (DEPTH, DIFF_QK_DIM), 0.1)
    lambda_k2 = nrm(ks[17], (DEPTH, DIFF_QK_DIM), 0.1)
    g_diff = 1.0 + nrm(ks[18], (DEPTH, DIFF_V_DIM), 0.05)
    w_out = nrm(ks[19], (DEPTH, MIX_WIDTH, D_MODEL), MIX_WIDTH ** -0.5)
    g_pre_ffn = 1.0 + nrm(ks[20], (DEPTH, D_MODEL), 0.05)
    g_post_ffn = 1.0 + nrm(ks[21], (DEPTH, D_MODEL), 0.05)
    w_up = nrm(ks[22], (DEPTH, D_MODEL, 2 * D_FF_2), D_MODEL ** -0.5)
    conv_ffn_w = nrm(ks[23], (DEPTH, CONV_W, 2 * D_FF_2), CONV_W ** -0.5)
    conv_ffn_b = nrm(ks[24], (DEPTH, 2 * D_FF_2), 0.02)
    w_down = nrm(ks[25], (DEPTH, D_FF_2, D_MODEL), D_FF_2 ** -0.5)
    return {"x": x, "c": c, "ctx": ctx, "c_ctx": c_ctx, "w_mod": w_mod, "b_mod": b_mod,
            "g_pre_mix": g_pre_mix, "g_post_mix": g_post_mix, "w_in": w_in, "b_gate": b_gate,
            "conv_qk_w": conv_qk_w, "conv_qk_b": conv_qk_b, "g_mlstm": g_mlstm,
            "lambda_q1": lambda_q1, "lambda_k1": lambda_k1, "lambda_q2": lambda_q2, "lambda_k2": lambda_k2,
            "g_diff": g_diff, "w_out": w_out, "g_pre_ffn": g_pre_ffn, "g_post_ffn": g_post_ffn,
            "w_up": w_up, "conv_ffn_w": conv_ffn_w, "conv_ffn_b": conv_ffn_b, "w_down": w_down}

def second_block(x, c, ctx, c_ctx, w_mod, b_mod, g_pre_mix, g_post_mix, w_in, b_gate,
              conv_qk_w, conv_qk_b, g_mlstm, lambda_q1, lambda_k1, lambda_q2, lambda_k2,
              g_diff, w_out, g_pre_ffn, g_post_ffn, w_up, conv_ffn_w, conv_ffn_b, w_down):
    n_lat = x.shape[1]
    ROWS = n_lat // GRID_W
    cos, sin = axial_rope_tables(ROWS, n_lat)
    for l in range(DEPTH):
        need_ctx = l < DEPTH - 1
        mod = jax.nn.silu(c) @ w_mod[l] + b_mod[l]
        sh1, sc1, ga1, sh2, sc2, ga2 = jnp.split(mod[:, None, :], N_MOD, axis=-1)
        cmod = jax.nn.silu(c_ctx) @ w_mod[l] + b_mod[l]
        csh1, csc1, cga1, csh2, csc2, cga2 = jnp.split(cmod, N_MOD, axis=-1)

        p_lat = modulate(rmsnorm(x, g_pre_mix[l]), sh1, sc1) @ w_in[l]
        p_ctx = modulate(rmsnorm(ctx, g_pre_mix[l]), csh1, csc1) @ w_in[l]
        m_lat, m_ctx = mlstm_group(p_lat, p_ctx, conv_qk_w[l], conv_qk_b[l], b_gate[l], g_mlstm[l], need_ctx)
        lam_init = 0.8 - 0.6 * math.exp(-0.3 * l)
        lam = (jnp.exp(jnp.sum(lambda_q1[l].astype(jnp.float32) * lambda_k1[l].astype(jnp.float32)))
               - jnp.exp(jnp.sum(lambda_q2[l].astype(jnp.float32) * lambda_k2[l].astype(jnp.float32)))
               + lam_init)
        d_lat, d_ctx = diff_group(p_lat, p_ctx, cos, sin, lam, lam_init, g_diff[l], need_ctx)
        y_lat = jnp.concatenate([m_lat, d_lat], axis=-1).astype(x.dtype) @ w_out[l]
        x = x + ga1 * rmsnorm(y_lat, g_post_mix[l])

        h_lat = modulate(rmsnorm(x, g_pre_ffn[l]), sh2, sc2)
        x = x + ga2 * rmsnorm(conv_ffn(h_lat, w_up[l], conv_ffn_w[l], conv_ffn_b[l], w_down[l]), g_post_ffn[l])

        if need_ctx:
            y_ctx = jnp.concatenate([m_ctx, d_ctx], axis=-1).astype(ctx.dtype) @ w_out[l]
            ctx = ctx + cga1 * rmsnorm(y_ctx, g_post_mix[l])
            h_ctx = modulate(rmsnorm(ctx, g_pre_ffn[l]), csh2, csc2)
            ctx = ctx + cga2 * rmsnorm(conv_ffn(h_ctx, w_up[l], conv_ffn_w[l], conv_ffn_b[l], w_down[l]), g_post_ffn[l])
    return x


def setup_inputs(seed=0):
    out = dict(first_inputs(seed))
    for name, value in second_inputs(seed + 1).items():
        if name != "x":
            out[name + "_2"] = value
    return out


def reference(
    x, c, rel_bias, hgrn_lb_logits, w_ada, b_ada, mix_norm_pre, mix_norm_post, w_in, w_gate,
    b_gate, hgrn_norm_w, conv_w, conv_b, conv_ln_g, conv_ln_b, w_a_out, w_b_out, w_c_out, w_o,
    mlp_norm_pre, mlp_norm_post, w_up, w_down, c_2, ctx_2, c_ctx_2, w_mod_2, b_mod_2,
    g_pre_mix_2, g_post_mix_2, w_in_2, b_gate_2, conv_qk_w_2, conv_qk_b_2, g_mlstm_2,
    lambda_q1_2, lambda_k1_2, lambda_q2_2, lambda_k2_2, g_diff_2, w_out_2, g_pre_ffn_2,
    g_post_ffn_2, w_up_2, conv_ffn_w_2, conv_ffn_b_2, w_down_2,
):
    x = first_block(
        x, c, rel_bias, hgrn_lb_logits, w_ada, b_ada, mix_norm_pre, mix_norm_post, w_in, w_gate,
        b_gate, hgrn_norm_w, conv_w, conv_b, conv_ln_g, conv_ln_b, w_a_out, w_b_out, w_c_out,
        w_o, mlp_norm_pre, mlp_norm_post, w_up, w_down,
    )
    return second_block(
        x, c_2, ctx_2, c_ctx_2, w_mod_2, b_mod_2, g_pre_mix_2, g_post_mix_2, w_in_2, b_gate_2,
        conv_qk_w_2, conv_qk_b_2, g_mlstm_2, lambda_q1_2, lambda_k1_2, lambda_q2_2, lambda_k2_2,
        g_diff_2, w_out_2, g_pre_ffn_2, g_post_ffn_2, w_up_2, conv_ffn_w_2, conv_ffn_b_2,
        w_down_2,
    )


_drawn_inputs = setup_inputs


def setup_inputs(seed=0):
    import zlib

    import numpy as np

    out = dict(_drawn_inputs(seed))
    spreads = {}
    factors = {'rel_bias': 3.021,
     'mix_norm_pre': 4.448,
     'mix_norm_post': 5.625,
     'b_gate': 8.0,
     'hgrn_norm_w': 7.965,
     'conv_b': 8.0,
     'conv_ln_g': 7.338,
     'conv_ln_b': 43.084,
     'mlp_norm_pre': 5.333,
     'mlp_norm_post': 5.621,
     'g_pre_mix_2': 4.424,
     'g_post_mix_2': 4.104,
     'conv_qk_b_2': 64.0,
     'g_mlstm_2': 6.732,
     'lambda_q1_2': 64.0,
     'lambda_k1_2': 64.0,
     'lambda_q2_2': 8.0,
     'lambda_k2_2': 8.0,
     'g_diff_2': 12.138,
     'g_pre_ffn_2': 3.035,
     'g_post_ffn_2': 4.204,
     'conv_ffn_b_2': 8.0}
    for name, (base, spread) in spreads.items():
        noise = np.random.default_rng([zlib.crc32(name.encode()), seed]).standard_normal(out[name].shape)
        drawn = base * np.exp(spread * noise) if base else spread * noise
        out[name] = __import__('jax').numpy.asarray(drawn.astype(out[name].dtype))
    for name, factor in factors.items():
        out[name] = (out[name] * factor).astype(out[name].dtype)
    return out
```

```python
from contextlib import ExitStack

import concourse.bass as bass
from concourse import mybir

F32 = mybir.dt.float32
U8 = mybir.dt.uint8
ALU = mybir.AluOpType
ACT = mybir.ActivationFunctionType
AX_X = mybir.AxisListType.X

P = 128
S = 256
D = 2048
KT = D // P
COLS = 256
SLOTS = 4
EPS = 1e-6
TINY = 1e-30
MASK_VALUE = -1e30
A_HEADS, B_HEADS, B_SLOTS = 8, 12, 4
C_TILES, C_TAPS = 6, 31
FF1, FF2 = 8192 // P, 5632 // P
M_HEADS = 8
LAM_INIT = 0.2
BROW = 383
BPITCH = 384

STREAM = [
    ("ada1", 48), ("c_a", 3), ("c_g", 3), ("a_f", 4), ("a_q", 4), ("a_g", 4), ("b_q", 3), ("b_k", 3),
    ("a_i", 4), ("b_v", 3), ("merge", 32), ("w_o", 8), ("up1", 32), ("down1", 32),
    ("ada2", 48), ("m_q", 4), ("m_o", 4), ("m_k", 4), ("m_v", 4), ("d_q", 4), ("d_k", 4), ("d_v", 4),
    ("w_out", 8), ("up2", FF2), ("down2", 32),
]
DOWN2_KT = FF2 // 4


def block_bases():
    first, ready, n, e = {}, {}, 0, 0
    for name, blocks in STREAM:
        first[name], ready[name] = n, e
        n += blocks
        e += blocks // 4 if name.startswith("down") else blocks
    first["end"] = n
    return first, ready


FIRST, READY = block_bases()

VECTORS = [
    ("c1", 16), ("c2", 16), ("cctx", 16), ("b_ada", 96), ("mix_pre", 16), ("mix_post", 16), ("mlp_pre", 16),
    ("mlp_post", 16), ("b_gate", 48), ("lb", 8), ("hgrn_w", 1), ("conv_w", C_TILES * C_TAPS), ("conv_b", 6),
    ("ln_g", 6), ("ln_b", 6), ("b_mod", 96), ("g_pre_mix", 16), ("g_post_mix", 16), ("g_pre_ffn", 16),
    ("g_post_ffn", 16), ("qk_w", 48), ("qk_b", 16), ("g_mlstm", 8), ("g_diff", 1), ("ffn_w", 3 * 2 * FF2),
    ("ffn_b", 2 * FF2), ("mg_b", 1), ("lam", 4),
]


def vector_columns():
    at, n = {}, 0
    for name, width in VECTORS:
        at[name] = n
        n += width
    return at, n


VEC, NVEC = vector_columns()

CONSTS = [("perm", P), ("cos", S), ("sin", S), ("tri_f", 384), ("tri_b", 384), ("onehot", BPITCH), ("bmask", BPITCH)]


def const_columns():
    at, n = {}, 0
    for name, width in CONSTS:
        at[name] = n
        n += width
    return at, n


CONST, NCONST = const_columns()


class Chain:

    def __init__(self, engine, sem):
        self.engine, self.sem, self.n, self.offset = engine, sem, 0, 0

    def __call__(self, instruction):
        self.n += 1
        instruction.then_inc(self.sem, 1)
        self.engine.wait_ge(self.sem, self.n + self.offset)


def two_blocks_kernel(nc, stream, stream_down2, x_t, ctx_t, vec_d, const_d, lvl_mask_d, ident_d, mg_w, rel_bias, scratch, out_t):
    with ExitStack() as ctx:
        def sb(name, shape, dt=F32):
            return ctx.enter_context(nc.sbuf_tensor("sb_" + name, shape, dt))

        def sem(name):
            return ctx.enter_context(nc.semaphore(name))

        ring = sb("ring", [P, SLOTS, KT, COLS])
        ident = sb("ident", [P, P])
        ones = sb("ones", [P, P])
        vec = sb("vec", [P, NVEC])
        cstat = sb("cstat", [P, 2, KT, 32])
        sel = sb("sel", [P, 2])
        mod1 = sb("mod1", [P, 96])
        mod2 = sb("mod2", [P, 2, 96])
        lvl_mask = sb("lvl_mask", [P, 8, P], U8)
        rstd = sb("rstd", [P, 512])
        small = sb("small", [P, 256])
        ARENA = 33000
        arena = sb("arena", [P, ARENA])
        G = [ctx.enter_context(nc.psum_tensor(f"gemm{i}", [P, 512], F32)) for i in range(4)]
        M = [ctx.enter_context(nc.psum_tensor(f"mix{i}", [P, 512], F32)) for i in range(4)]

        def region(at, *dims):
            n = 1
            for d in dims:
                n *= d
            assert at + n <= ARENA, (at, dims)
            flat = arena[:, at:at + n]
            if len(dims) == 1:
                return flat
            names = "abc"[:len(dims)]
            return flat.rearrange(f"p ({' '.join(names)}) -> p {' '.join(names)}", **dict(zip(names, dims)))

        def v(name, i=0, n=1):
            return vec[:, VEC[name] + i:VEC[name] + i + n]

        xT = region(0, KT, S)
        h1 = region(4096, KT, S)
        hw = region(4096, KT, 512)
        y1 = region(8192, KT, S)
        R = 12288
        fP = region(R, 8, S)
        kk = region(R + 2048, 8, S)
        qq = region(R + 4096, 8, S)
        og = region(R + 6144, 8, S)
        ii = region(R + 8192, 2, 1024)
        bq = region(R + 10240, 6, S)
        bk = region(R + 11776, 6, S)
        bv = region(R + 13312, 2, 768)
        T0 = R + 14848
        ca = region(T0, 6, S)
        upad = region(T0 + 1536, 6, 30 + S)
        cy = region(T0 + 1536 + 6 * (30 + S), 6, S)
        suf = region(T0, 4, S)
        qs = region(T0 + 1024, 4, S)
        ks = region(T0 + 2048, 4, S)
        attn = region(T0 + 3072, 8, P)
        attx = region(T0 + 4096, 4, P)
        bias = region(R, 12, S)
        blog = [region(R + 3072 + 768 * i, 3, S) for i in range(2)]
        bpt = [region(R + 4608 + 768 * i, 6, P) for i in range(2)]
        bdg = [region(T0 + P * i, P) for i in range(2)]
        gates = region(R, 2, 3, 512)
        mtmp = region(R + 3072, 2, 512)
        merged = region(R + 4096, KT, S)
        proj1 = region(R + 8192, KT, S)
        sq0 = region(R, KT, S)
        sq1 = region(R + 12288, KT, S)
        up1 = region(8192, FF1, S)
        down1 = region(8192 + FF1 * S, KT, S)
        sq1b = region(8192 + FF1 * S + 4096, KT, S)
        modrow1 = region(R + 19636, SLOTS, COLS)
        onehot = region(R + 4096, BPITCH)
        bmask = region(R + 4480, BPITCH)
        brow = region(R + 4864, BPITCH)
        relb = region(R + 5248, 12)
        lvl_f = region(R + 6144, 8, P)
        y2 = region(12288, KT, S)
        R2 = 16384
        sqw = region(R2, KT, 512)
        mq = region(R2, 8, S)
        mk = region(R2 + 2048, 8, 512)
        mv = region(R2 + 6144, 4, 1024)
        mo = region(R2 + 10240, 8, S)
        T2 = R2 + 12288
        modrow2 = region(T2, SLOTS, COLS)
        mW = [region(T2 + 1024 * i, 4, S) for i in range(2)]
        gB = region(T2, 2, 512)
        gM = region(T2 + 1024, 2, 512)
        mfl = [region(T2 + 2048 + S * i, S) for i in range(2)]
        mden = region(T2 + 2560, S)
        aT = region(T2 + 2816, 2, 4, 8)
        tri = [region(T2 + 2880 + 384 * i, 384) for i in range(2)]
        gG = region(12288, 4, 512)
        grows = region(12288 + 2048, 2, 2, S)
        gtmp = region(12288 + 2048, 2, 512)
        gsb = region(12288 + 3072, 512)
        wg = region(12288 + 3584, KT, 32)
        dq = region(R2, 8, S)
        dk = region(R2 + 2048, 8, 512)
        dv = region(R2 + 6144, 4, 1024)
        D0 = R2 + 10240
        dE = [region(D0 + 1024 * i, 2, 512) for i in range(2)]
        dpd = [region(D0 + 2048 + 512 * i, 512) for i in range(2)]
        dPT = [region(D0 + 3072 + 512 * i, 4, P) for i in range(2)]
        rtab = region(D0 + 5120, 640)
        rtmp = region(D0 + 5760, 2, S)
        proj2 = region(R2, KT, S)
        sq2 = region(R2 + 4096, KT, S)
        up2 = region(R2, FF2, S)
        down2 = region(R2 + FF2 * S, KT, S)
        fv = region(R2 + FF2 * S + 4096, 2, 2, S)
        sq2b = region(12288, KT, S)

        def tile_of(t, i):
            return t[:, i, :]

        amul, gmul = small[:, 0:16], small[:, 16:32]
        lbc, lb1 = small[:, 32:40], small[:, 40:48]
        lamn = small[:, 48:49]
        cmul = small[:, 64:80]
        sm_e = small[:, 80:88]
        nm = [small[:, 96 + 2 * i:98 + 2 * i] for i in range(2)]
        zz = [small[:, 104 + 2 * i:106 + 2 * i] for i in range(2)]
        rz = [small[:, 112 + 2 * i:114 + 2 * i] for i in range(2)]
        lamp = small[:, 120:122]
        lame = small[:, 122:124]

        loaded = [sem(f"loaded{i}") for i in range(SLOTS)]
        retired = [sem(f"retired{i}") for i in range(SLOTS)]
        block_ready = sem("block_ready")
        boot = sem("boot")
        x_in = sem("x_in")
        fills = sem("fills")
        c_ready = sem("c_ready")
        ada_cols = sem("ada_cols")
        mod_ready = sem("mod_ready")
        sq_ready, ms_ready, inv_ready, rstd_ready = (sem(n) for n in ("sq_ready", "ms_ready", "inv_ready", "rstd_ready"))
        h_ready = sem("h_ready")
        x_ready = sem("x_ready")
        dve_step, act_step, pool_step = sem("dve_step"), sem("act_step"), sem("pool_step")
        brow_mm, brow_ready, brow_out, bias_in = sem("brow_mm"), sem("brow_ready"), sem("brow_out"), sem("bias_in")
        u_pad = sem("u_pad")
        conv_tap, conv_done = sem("conv_tap"), sem("conv_done")
        conv_y, mean_mm, conv_cent, yc_in = sem("conv_y"), sem("mean_mm"), sem("conv_cent"), sem("yc_in")
        lvl_prep, lvl_mm, lvl_read = sem("lvl_prep"), sem("lvl_mm"), sem("lvl_read")
        attn_ready, o_mm, o_copied = sem("attn_ready"), sem("o_mm"), sem("o_copied")
        hgrn_free, ya_ready = sem("hgrn_free"), sem("ya_ready")
        qk_mm, log_ready, exp_ready, dg_ready = sem("qk_mm"), sem("log_ready"), sem("exp_ready"), sem("dg_ready")
        pt_mm, pt_ready, pv_mm, yb_ready = sem("pt_mm"), sem("pt_ready"), sem("pv_mm"), sem("yb_ready")
        gates_ready, merged_ready = sem("gates_ready"), sem("merged_ready")
        up_ready = sem("up_ready")
        cx_in, tab_in, mg_mm, mg_sb, mg_rows = sem("cx_in"), sem("tab_in"), sem("mg_mm"), sem("mg_sb"), sem("mg_rows")
        log_abs, ln_ready, rows_ready, at_mm, at_ready = (sem(n) for n in ("log_abs", "ln_ready", "rows_ready", "at_mm", "at_ready"))
        conv3_in, conv3_done, silu_done = sem("conv3_in"), sem("conv3_done"), sem("silu_done")
        s_mm, bc_mm, w_arg, w_ready, ws_ready = (sem(n) for n in ("s_mm", "bc_mm", "w_arg", "w_ready", "ws_ready"))
        nd_mm, den_ready, fin_ready = sem("nd_mm"), sem("den_ready"), sem("fin_ready")
        ym_ready, rot_mm, rope_done = sem("ym_ready"), sem("rot_mm"), sem("rope_done")
        lam_in, lam_mm, lam_exp, lam_ready = sem("lam_in"), sem("lam_mm"), sem("lam_exp"), sem("lam_ready")
        dqk_mm, dmax, dexp, dpd_ready = sem("dqk_mm"), sem("dmax"), sem("dexp"), sem("dpd_ready")
        dpt_mm, dpt_ready, dpv_mm, dy_ready = sem("dpt_mm"), sem("dpt_ready"), sem("dpv_mm"), sem("dy_ready")
        yd_ready = sem("yd_ready")
        taps_in, ffn_done = sem("taps_in"), sem("ffn_done")
        stored = sem("stored")

        N_MAIN = FIRST["down2"]

        def use(n, step=0):
            return n % SLOTS, n // SLOTS + step

        def copied(eng, n, step=0):
            slot, uses = use(n, step)
            eng.wait_ge(retired[slot], uses + 1)

        block = ctx.enter_context(nc.Block())

        @block.sync
        def _(sp):
            def load(n, step, source, kt=KT):
                slot, uses = use(n, step)
                if n >= SLOTS:
                    sp.wait_ge(retired[slot], uses)
                sp.dma_start(ring[:, slot, 0:kt, :], source).then_inc(loaded[slot], 16)

            for n in range(SLOTS):
                load(n, 0, stream[n])
            rounds = N_MAIN // SLOTS
            with sp.Fori(1, rounds) as r:
                for j in range(SLOTS):
                    sp.wait_ge(retired[j], r)
                    sp.dma_start(ring[:, j, :, :], stream[r * SLOTS + j]).then_inc(loaded[j], 16)
            for n in range(rounds * SLOTS, N_MAIN):
                load(n, 0, stream[n])
            with sp.Fori(0, 8) as r:
                for j in range(SLOTS):
                    load(N_MAIN + j, r, stream_down2[r * SLOTS + j], DOWN2_KT)
            sp.wait_ge(x_ready, 4)
            sp.dma_start(out_t, xT).then_inc(stored, 16)
            sp.wait_ge(stored, 16)

        @block.gpsimd
        def _(pool):
            pool.memset(cstat[:, :, :, :], 0.0).then_inc(fills, 1)
            pool.memset(ones[:, :], 1.0).then_inc(fills, 1)
            pool.memset(upad[:, :, :], 0.0).then_inc(fills, 1)
            pool.wait_ge(brow_ready, 1)
            pool.dma_start(scratch[:, 0:P * BPITCH].rearrange("h (p c) -> h p c", c=BPITCH),
                           brow[0:12, :].unsqueeze(1).to_broadcast([12, P, BPITCH])).then_inc(brow_out, 16)
            pool.wait_ge(brow_out, 16)
            pool.wait_ge(ya_ready, 1)
            skew = scratch[:, 0:P * (BPITCH - 1)].rearrange("h (p c) -> p h c", c=BPITCH - 1)
            pool.dma_start(bias, skew[:, :, P - 1:P - 1 + S]).then_inc(bias_in, 16)
            pool.wait_ge(h_ready, 2)
            pool.wait_ge(x_ready, 2)
            pool.dma_start(hw[:, :, 0:S], ctx_t).then_inc(cx_in, 16)
            pool.dma_start(wg, mg_w).then_inc(cx_in, 16)
            pool.wait_ge(h_ready, 4)
            pool.dma_start(tri[0], const_d[:, CONST["tri_f"]:CONST["tri_f"] + 384]).then_inc(tab_in, 16)
            pool.dma_start(tri[1], const_d[:, CONST["tri_b"]:CONST["tri_b"] + 384]).then_inc(tab_in, 16)
            pool.wait_ge(mg_sb, 1)
            for g in range(4):
                pool.dma_start(gG[0:8, g, :], gsb[8 * g:8 * g + 8, :]).then_inc(mg_rows, 16)
            pool.wait_ge(ym_ready, 1)
            pool.dma_start(rtab, const_d[:, 0:640]).then_inc(tab_in, 16)

        @block.scalar
        def _(act):
            step = Chain(act, act_step)
            norms = [0]

            act.dma_start(vec[:, :], vec_d).then_inc(boot, 16)
            act.dma_start(ident[:, :], ident_d[:, 0:P]).then_inc(boot, 16)
            act.dma_start(sel[:, :], ident_d[:, P:P + 2]).then_inc(boot, 16)
            act.dma_start(lvl_f, lvl_mask_d).then_inc(boot, 16)
            act.dma_start(onehot, const_d[:, CONST["onehot"]:CONST["onehot"] + BPITCH]).then_inc(boot, 16)
            act.dma_start(bmask, const_d[:, CONST["bmask"]:CONST["bmask"] + BPITCH]).then_inc(boot, 16)
            act.dma_start(relb[0:32, :], rel_bias).then_inc(boot, 16)
            act.dma_start(xT, x_t).then_inc(x_in, 16)

            def square(dst, src):
                norms[0] += 1
                act.activation(dst, src, ACT.Square).then_inc(sq_ready, 1)

            def root(t):
                act.wait_ge(inv_ready, norms[0])
                act.activation(t, t, ACT.Sqrt).then_inc(rstd_ready, 1)

            def copy_out(part, i, dst, func=ACT.Copy, its=None, per=0, wide=None):
                n, r = FIRST[part] + i, READY[part] + i
                slot = n % SLOTS
                act.wait_ge(block_ready, r + 1 if its is None else r + 1 + its * per)
                if wide is not None:
                    act.activation(wide, M[slot][:, :], func)
                act.activation(dst, G[slot][:, :], func).then_inc(retired[slot], 1)

            act.wait_ge(boot, 112)
            act.wait_ge(fills, 1)
            act.activation(cstat[:, 0, :, 0], v("c1", 0, 16), ACT.Silu)
            act.activation(cstat[:, 1, :, 0], v("c2", 0, 16), ACT.Silu)
            act.activation(cstat[:, 1, :, 1], v("cctx", 0, 16), ACT.Silu).then_inc(c_ready, 1)

            act.wait_ge(x_in, 16)
            square(sq0, xT)
            root(rstd[:, 0:S])

            def ada(part, modrow):
                with act.Fori(0, 12) as it:
                    for j in range(SLOTS):
                        n = FIRST[part] + j
                        slot = n % SLOTS
                        act.wait_ge(block_ready, READY[part] + j + 1 + it * SLOTS)
                        act.activation(modrow[:, slot, :], G[slot][:, 0:COLS], ACT.Copy).then_inc(retired[slot], 1)

            ada("ada1", modrow1)
            def two(t, i):
                return t[:, 2 * i:2 * i + 2, :].rearrange("p a b -> p (a b)")

            for i in range(3):
                copy_out("c_a", i, two(ca, i))
            for i in range(3):
                copy_out("c_g", i, two(cy, i), ACT.Sigmoid)
            for i in range(4):
                n, r = FIRST["a_f"] + i, READY["a_f"] + i
                act.wait_ge(block_ready, r + 1)
                act.activation(two(fP, i), G[n % SLOTS][:, :], ACT.Sigmoid)
                act.activation(two(kk, i), G[n % SLOTS][:, :], ACT.Sigmoid, scale=-1.0).then_inc(retired[n % SLOTS], 1)
            act.wait_ge(brow_out, 16)
            for i in range(4):
                copy_out("a_q", i, two(qq, i), ACT.Silu)
            for i in range(4):
                copy_out("a_g", i, two(og, i), ACT.Silu)
            for i in range(3):
                copy_out("b_q", i, two(bq, i))
            for i in range(3):
                copy_out("b_k", i, two(bk, i))

            def copy_tokens(part, i, dst, wide=None):
                n, r = FIRST[part] + i, READY[part] + i
                act.wait_ge(block_ready, r + 1)
                c = slice(i * COLS, (i + 1) * COLS)
                if wide is not None:
                    act.activation(dst[:, 2:4, c], M[n % SLOTS][:, :].rearrange("p (a b) -> p a b", a=2), ACT.Copy)
                act.activation(dst[:, 0:2, c], G[n % SLOTS][:, :].rearrange("p (a b) -> p a b", a=2), ACT.Copy)\
                   .then_inc(retired[n % SLOTS], 1)

            for i in range(4):
                copy_tokens("a_i", i, ii)
            for i in range(3):
                copy_tokens("b_v", i, bv)
            act.wait_ge(conv_cent, 1)
            square(ca, cy)
            root(rstd[:, 0:S])
            act.wait_ge(yc_in, 1)
            for t in range(C_TILES):
                ins = act.activation(y1[:, 10 + t, :], cy[:, t, :], ACT.Silu, bias=v("ln_b", t), scale=v("ln_g", t))
            ins.then_inc(conv_done, 1)
            for half in range(2):
                act.wait_ge(o_mm, half + 1)
                for b in range(2):
                    ins = act.activation(two(qq, 2 * half + b), G[2 * half + b][:, :], ACT.Copy)
                ins.then_inc(o_copied, 1)
            act.wait_ge(o_copied, 2)
            square(fP, qq)
            root(kk)
            for u in range(9):
                if u < 8:
                    T, e = u // 4, u % 2
                    w = P * (T + 1)
                    act.wait_ge(log_ready, u + 1)
                    act.activation(blog[e][:, :, 0:w], blog[e][:, :, 0:w], ACT.Exp, bias=nm[e][:, 0:1],
                                   accum_out=zz[e][:, 0:1]).then_inc(exp_ready, 1)
                if u >= 1:
                    T, slot, e = (u - 1) // 4, (u - 1) % 4, (u - 1) % 2
                    po = 64 * (slot % 2)
                    act.wait_ge(pv_mm, u)
                    act.activation(y1[po:po + 64, 8 + slot // 2, P * T:P * T + P], G[e][po:po + 64, 0:P], ACT.Copy)\
                       .then_inc(yb_ready, 1)
            with act.Fori(0, 8) as it:
                for g in range(3):
                    n = FIRST["merge"] + g
                    act.wait_ge(block_ready, READY["merge"] + g + 1 + it * 4)
                    if g == 0:
                        act.wait_ge(merged_ready, it + 1)
                    for j in range(2):
                        ins = act.activation(gates[:, 0, g, j * S:(j + 1) * S], G[n % SLOTS][:, j * S:(j + 1) * S],
                                             ACT.Sigmoid, bias=vec[:, bass.ds(VEC["b_gate"] + 16 * g + j + it * 2, 1)])
                    ins.then_inc(retired[n % SLOTS], 1)
            with act.Fori(0, 2) as it:
                for j in range(4):
                    copy_out("w_o", j, proj1[:, bass.ds(2 * j + it * 8, 2), :].rearrange("p a b -> p (a b)"), its=it, per=4)
            copied(act, FIRST["w_o"] + 7)
            square(sq1, proj1)
            root(rstd[:, 0:S])
            act.wait_ge(x_ready, 1)
            square(sq1, xT)
            root(rstd[:, 0:S])
            with act.Fori(0, 8) as it:
                for j in range(4):
                    copy_out("up1", j, up1[:, bass.ds(2 * j + it * 8, 2), :].rearrange("p a b -> p (a b)"),
                             ACT.Relu, its=it, per=4)

            def copy_down(part, dst, its, parity):
                n, r = FIRST[part] + 4 * parity + 3, READY[part] + parity
                act.wait_ge(block_ready, r + 1 + its * 2)
                act.activation(dst[:, bass.ds(2 * parity + its * 4, 2), :].rearrange("p a b -> p (a b)"),
                               M[parity][:, :], ACT.Copy).then_inc(retired[n % SLOTS], 1)

            with act.Fori(0, 4) as it:
                for parity in range(2):
                    copy_down("down1", down1, it, parity)
            copied(act, FIRST["down1"] + 31)
            square(sq1b, down1)
            root(rstd[:, 0:S])
            act.wait_ge(x_ready, 2)
            act.wait_ge(cx_in, 32)
            square(sqw[:, :, 0:S], hw[:, :, 0:S])
            root(rstd[:, 0:S])
            square(sqw[:, :, S:512], xT)
            root(rstd[:, S:512])
            ada("ada2", modrow2)

            def conv3_block(part, i, dst, tile0, wide):
                n, r = FIRST[part] + i, READY[part] + i
                act.wait_ge(block_ready, r + 1)
                for j in range(2):
                    t = tile0 + 2 * i + j
                    bank = (M if wide and j else G)[n % SLOTS]
                    src = bank[:, :] if wide else bank[:, j * S:(j + 1) * S]
                    act.activation(dst[:, 2 * i + j, :], src, ACT.Identity, scale=v("qk_w", 16 + t), bias=v("qk_b", t))\
                       .then_inc(conv3_in, 1)

            for i in range(4):
                conv3_block("m_q", i, mq, 0, False)
            for i in range(4):
                copy_out("m_o", i, two(mo, i), ACT.Sigmoid)
            for i in range(4):
                conv3_block("m_k", i, mk, 8, True)
            for i in range(4):
                copy_tokens("m_v", i, mv, True)
            act.wait_ge(mg_mm, 1)
            act.activation(gsb[0:32, :], M[0][0:32, :], ACT.Identity, bias=v("mg_b")[0:32, :]).then_inc(mg_sb, 1)
            act.wait_ge(mg_rows, 64)
            fg = gG[0:8, 1:4:2, :]
            step(act.activation(gtmp[0:8, :, :], fg, ACT.Abs))
            step(act.activation(gtmp[0:8, :, :], gtmp[0:8, :, :], ACT.Exp, scale=-1.0))
            act.activation(gtmp[0:8, :, :], gtmp[0:8, :, :], ACT.Ln, bias=1.0).then_inc(ln_ready, 1)
            act.wait_ge(conv3_done, 16)
            act.activation(mq, mq, ACT.Silu)
            act.activation(mk, mk, ACT.Silu).then_inc(silu_done, 1)
            for u in range(17):
                if u < 16:
                    e = u % 2
                    act.wait_ge(w_arg, u + 1)
                    if u >= 2:
                        act.wait_ge(fin_ready, u - 1)
                    act.activation(mW[e], mW[e], ACT.Exp)
                    act.activation(mfl[e], M[e][:, S:512], ACT.Exp).then_inc(w_ready, 1)
                if u >= 1:
                    act.wait_ge(nd_mm, u)
                    if u >= 2:
                        act.wait_ge(fin_ready, u - 1)
                    act.activation(mden, M[2 + (u - 1) % 2][:, S:512], ACT.Abs).then_inc(den_ready, 1)
            act.wait_ge(fin_ready, 16)
            square(mq, y2[:, 0:8, :])
            root(mk[:, :, 0:S])
            act.wait_ge(ym_ready, 1)
            for i in range(4):
                copy_out("d_q", i, two(dq, i))
            for i in range(4):
                copy_out("d_k", i, dk[:, 2 * i, :], wide=dk[:, 2 * i + 1, :])
            for i in range(4):
                copy_tokens("d_v", i, dv, True)
            act.wait_ge(lam_mm, 1)
            act.activation(lame, M[3][:, 0:2], ACT.Exp).then_inc(lam_exp, 1)
            for u in range(17):
                if u < 16:
                    e = u % 2
                    act.wait_ge(dmax, u + 1)
                    if u >= 2:
                        act.wait_ge(dpd_ready, u - 1)
                    for c in range(2):
                        ins = act.activation(dE[e][:, c, :], M[c][:, :], ACT.Exp, bias=nm[e][:, c:c + 1], scale=0.125,
                                             accum_out=zz[e][:, c:c + 1])
                    ins.then_inc(dexp, 1)
                if u >= 1:
                    head, T = (u - 1) // 2, (u - 1) % 2
                    act.wait_ge(dpt_mm, u)
                    if u >= 3:
                        act.wait_ge(dpv_mm, u - 2)
                    act.activation(dPT[(u - 1) % 2].rearrange("p a b -> p (a b)"), M[2][:, :], ACT.Copy).then_inc(dpt_ready, 1)
                    act.wait_ge(dpv_mm, u)
                    act.activation(y2[:, 8 + head, P * T:P * T + P], M[3][:, 0:P], ACT.Copy).then_inc(dy_ready, 1)
            act.wait_ge(dy_ready, 16)
            square(dq, y2[:, 8:16, :])
            root(dk[:, :, 0:S])
            act.wait_ge(yd_ready, 1)
            with act.Fori(0, 2) as it:
                for j in range(4):
                    copy_out("w_out", j, proj2[:, bass.ds(2 * j + it * 8, 2), :].rearrange("p a b -> p (a b)"), its=it, per=4)
            copied(act, FIRST["w_out"] + 7)
            square(sq2, proj2)
            root(rstd[:, 0:S])
            act.wait_ge(x_ready, 3)
            square(sq2, xT)
            root(rstd[:, 0:S])
            with act.Fori(0, FF2 // 4) as it:
                for j in range(4):
                    n = FIRST["up2"] + j
                    act.wait_ge(block_ready, READY["up2"] + j + 1 + it * 4)
                    act.wait_ge(ffn_done, it * 4 + j + 1)
                    for c in range(2):
                        col = bass.ds(c * FF2 + j + it * 4 + VEC["ffn_w"] + 2 * FF2, 1)
                        bcol = bass.ds(c * FF2 + j + it * 4 + VEC["ffn_b"], 1)
                        ins = act.activation(fv[:, j % 2, c, :], G[n % SLOTS][:, c * S:(c + 1) * S], ACT.Identity,
                                             scale=vec[:, col], bias=vec[:, bcol])
                    ins.then_inc(taps_in, 1)
                    copied(act, n, it)
                    act.activation(fv[:, j % 2, 0, :], fv[:, j % 2, 0, :], ACT.Silu).then_inc(up_ready, 1)
            with act.Fori(0, 4) as it:
                for parity in range(2):
                    copy_down("down2", down2, it, parity)
            copied(act, FIRST["down2"] + 31)
            square(sq2b, down2)
            root(rstd[:, 0:S])

        @block.tensor
        def _(pe):
            norms = [0]

            def arrive(n, step=0):
                slot, uses = use(n, step)
                pe.wait_ge(loaded[slot], 16 * (uses + 1))
                return slot

            def gemm_T(n, moving, step=0, wide=False):
                slot = arrive(n, step)
                for j in range(2):
                    out = (M if j else G)[slot][:, :] if wide else G[slot][:, j * S:(j + 1) * S]
                    for k in range(KT):
                        ins = pe.matmul(out, ring[:, slot, k, j * P:(j + 1) * P], moving[:, k, :],
                                        start=(k == 0), stop=(k == KT - 1))
                ins.then_inc(block_ready, 1)

            def gemm_tokens(n, stationary, tiles):
                slot = arrive(n)
                for t in range(tiles):
                    out = (G if t < 2 else M)[slot][:, (t % 2) * S:(t % 2 + 1) * S]
                    for k in range(KT):
                        ins = pe.matmul(out, stationary[:, k, t * P:(t + 1) * P], ring[:, slot, k, :],
                                        start=(k == 0), stop=(k == KT - 1))
                ins.then_inc(block_ready, 1)

            def norm(src, n, cols=S):
                norms[0] += 1
                pe.wait_ge(sq_ready, norms[0])
                for k in range(n):
                    ins = pe.matmul(M[2][:, 0:cols], ones[:, :], src[:, k, :], start=(k == 0), stop=(k == n - 1))
                ins.then_inc(ms_ready, 1)

            def norm_heads(src):
                norms[0] += 1
                pe.wait_ge(sq_ready, norms[0])
                for h in range(8):
                    ins = pe.matmul(G[h // 2][:, (h % 2) * S:(h % 2 + 1) * S], ones[:, :], src[:, h, :], start=True, stop=True)
                ins.then_inc(ms_ready, 1)

            pe.wait_ge(fills, 2)
            pe.wait_ge(boot, 112)
            pe.matmul(M[3][0:12, 0:BPITCH], relb[0:32, :], onehot[0:32, :], start=True, stop=True).then_inc(brow_mm, 1)
            norm(sq0, KT)

            def ada(part, b, modrow):
                def turn(j, it):
                    n = FIRST[part] + j
                    slot, uses = use(n, it)
                    pe.wait_ge(retired[slot], uses + 1)
                    for i in range(2):
                        ins = pe.matmul(M[3][:, bass.ds(4 * j + 2 * i + it * 16, 2)], modrow[:, slot, i * P:(i + 1) * P],
                                        sel[:, :], start=True, stop=True)
                    ins.then_inc(ada_cols, 1)

                with pe.Fori(0, 12) as it:
                    for j in range(SLOTS):
                        slot = arrive(FIRST[part] + j, it)
                        for k in range(KT):
                            g = k % 4
                            ins = pe.matmul(G[slot][32 * g:32 * g + 32, 0:COLS], cstat[:, b, k, :], ring[:, slot, k, :],
                                            start=(k < 4), stop=(k >= KT - 4))
                        ins.then_inc(block_ready, 1)
                        if j:
                            turn(j - 1, it)
                    turn(SLOTS - 1, it)

            pe.wait_ge(c_ready, 1)
            pe.wait_ge(brow_ready, 1)
            ada("ada1", 0, modrow1)
            pe.wait_ge(h_ready, 1)
            with pe.Fori(0, 6) as it:
                for j in range(4):
                    gemm_T(FIRST["c_a"] + j, h1, it)
            for i in range(7):
                gemm_tokens(FIRST["a_i"] + i, h1, 2)
            pe.wait_ge(conv_y, 1)
            for t in range(C_TILES):
                ins = pe.matmul(M[2][:, S:512], ones[:, :], cy[:, t, :], start=(t == 0), stop=(t == C_TILES - 1))
            ins.then_inc(mean_mm, 1)
            norm(ca, C_TILES)
            for half in range(2):
                for L in range(9):
                    q_, k_ = (qq[:, 4 * half:4 * half + 4, :], kk[:, 4 * half:4 * half + 4, :]) if L == 0 else (qs, ks)
                    pe.wait_ge(lvl_prep, 9 * half + L + 1)
                    c = 9 * half + L
                    if c >= 2:
                        pe.wait_ge(lvl_read, c - 1)
                    for h in range(4):
                        if L < 8:
                            for t in range(2):
                                i = 2 * h + t
                                ins = pe.matmul(M[2 * (c % 2) + i // 4][:, (i % 4) * P:(i % 4 + 1) * P],
                                                k_[:, h, t * P:(t + 1) * P], q_[:, h, t * P:(t + 1) * P], start=True, stop=True)
                        else:
                            ins = pe.matmul(M[2 * (c % 2)][:, h * P:(h + 1) * P], k_[:, h, 0:P], q_[:, h, P:S],
                                            start=True, stop=True)
                    ins.then_inc(lvl_mm, 1)
                pe.wait_ge(attn_ready, half + 1)
                if half == 0:
                    copied(pe, FIRST["a_i"] + 3)
                    for i in range(3, 7):
                        copied(pe, FIRST["a_i"] + i)
                for h in range(4):
                    bank, o = G[2 * half + h // 2], (h % 2) * S
                    hd = slice((4 * half + h) * P, (4 * half + h + 1) * P)
                    pe.matmul(bank[:, o:o + P], ii[:, 0, hd], attn[:, 2 * h, :], start=True, stop=True)
                    pe.matmul(bank[:, o + P:o + S], ii[:, 0, hd], attx[:, h, :], start=True, stop=False)
                    ins = pe.matmul(bank[:, o + P:o + S], ii[:, 1, hd], attn[:, 2 * h + 1, :], start=False, stop=True)
                ins.then_inc(o_mm, 1)
            norm_heads(fP)
            pe.wait_ge(ya_ready, 1)
            for u in range(9):
                if u < 8:
                    T, slot = u // 4, u % 4
                    w = P * (T + 1)
                    if u >= 1:
                        pe.wait_ge(log_ready, u)
                    for g in range(3):
                        h = 4 * g + slot
                        po = 64 * (h % 2)
                        out = M[0][:, g * S:g * S + w] if g < 2 else M[1][:, 0:w]
                        ins = pe.matmul(out, bq[po:po + 64, h // 2, T * P:(T + 1) * P], bk[po:po + 64, h // 2, 0:w],
                                        start=True, stop=True)
                    ins.then_inc(qk_mm, 1)
                if u >= 1:
                    T, slot, e = (u - 1) // 4, (u - 1) % 4, (u - 1) % 2
                    pe.wait_ge(dg_ready, u)
                    if u >= 2:
                        pe.wait_ge(pt_ready, u - 1)
                    chunks = [(g, st) for g in range(3) for st in range(T + 1)]
                    for i, (g, st) in enumerate(chunks):
                        ins = pe.matmul(M[2 + i // 4][:, (i % 4) * P:(i % 4 + 1) * P], blog[e][:, g, st * P:(st + 1) * P],
                                        bdg[e], start=True, stop=True)
                    ins.then_inc(pt_mm, 1)
                    pe.wait_ge(pt_ready, u)
                    if u >= 3:
                        pe.wait_ge(yb_ready, u - 2)
                    po = 64 * (slot % 2)
                    for i, (g, st) in enumerate(chunks):
                        hc = (4 * g + slot) * 64
                        ins = pe.matmul(G[e][po:po + 64, 0:P], bv[:, st, hc:hc + 64], bpt[e][:, i, :],
                                        start=(i == 0), stop=(i == len(chunks) - 1))
                    ins.then_inc(pv_mm, 1)
            pe.wait_ge(conv_done, 1)
            pe.wait_ge(yb_ready, 8)
            with pe.Fori(0, 8) as it:
                for g in range(3):
                    gemm_T(FIRST["merge"] + g, h1, it)
                n = FIRST["merge"] + 3
                slot = arrive(n, it)
                pe.wait_ge(merged_ready, it + 1)
                for b, (k0, k1) in enumerate(((0, 8), (8, 10), (10, 16))):
                    for j in range(2):
                        for k in range(k0, k1):
                            ins = pe.matmul(M[b][:, j * S:(j + 1) * S], ring[:, slot, k, j * P:(j + 1) * P], y1[:, k, :],
                                            start=(k == k0), stop=(k == k1 - 1))
                ins.then_inc(block_ready, 1)
            pe.wait_ge(merged_ready, 9)
            with pe.Fori(0, 2) as it:
                for j in range(4):
                    gemm_T(FIRST["w_o"] + j, merged, it)
            norm(sq1, KT)
            norm(sq1, KT)
            pe.wait_ge(h_ready, 2)
            with pe.Fori(0, 8) as it:
                for j in range(4):
                    gemm_T(FIRST["up1"] + j, h1, it)

            def down(part, moving, kt):
                with pe.Fori(0, 4) as it:
                    for parity in range(2):
                        last = FIRST[part] + 4 * parity + 3
                        for q in range(4):
                            n = FIRST[part] + 4 * parity + q
                            slot = arrive(n, it * 2)
                            if q == 0:
                                pe.wait_ge(retired[last % SLOTS], use(last, it * 2)[1] - 1)
                            for j in range(2):
                                for k in range(kt):
                                    ins = pe.matmul(M[parity][:, j * S:(j + 1) * S],
                                                    ring[:, slot, k, j * P:(j + 1) * P], moving[:, q * kt + k, :],
                                                    start=(q == 0 and k == 0 and j == 0), stop=(q == 3 and k == kt - 1),
                                                    skip_group_check=True)
                            ins.then_inc(block_ready if q == 3 else retired[slot], 1)

            pe.wait_ge(up_ready, 32)
            down("down1", up1, KT)
            norm(sq1b, KT)
            norm(sqw[:, :, 0:S], KT)
            norm(sqw[:, :, S:512], KT)
            ada("ada2", 1, modrow2)
            pe.wait_ge(h_ready, 4)
            for i in range(8):
                gemm_T(FIRST["m_q"] + i, hw[:, :, S:512])
            for i in range(4):
                gemm_T(FIRST["m_k"] + i, hw, wide=True)
            for i in range(4):
                gemm_tokens(FIRST["m_v"] + i, hw, 4)
            for i in range(4):
                copied(pe, FIRST["m_v"] + i)
            for k in range(KT):
                ins = pe.matmul(M[0][0:32, :], wg[:, k, :], hw[:, k, :], start=(k == 0), stop=(k == KT - 1))
            ins.then_inc(mg_mm, 1)
            pe.wait_ge(rows_ready, 1)
            for d in range(2):
                for t in range(4):
                    ins = pe.matmul(M[1][:, d * 32 + t * 8:d * 32 + t * 8 + 8], gG[0:8, 2 * d, t * P:(t + 1) * P],
                                    ident[0:8, 0:8], start=True, stop=True)
            ins.then_inc(at_mm, 1)
            pe.wait_ge(silu_done, 1)
            pe.wait_ge(at_ready, 1)
            for u in range(17):
                if u < 16:
                    h, d = u // 2, u % 2
                    if d == 0:
                        if h >= 2:
                            pe.wait_ge(ws_ready, 2 * (h - 1))
                        for t in range(4):
                            ins = pe.matmul(G[2 * (h % 2) + t // 2][:, (t % 2) * S:(t % 2 + 1) * S],
                                            mk[:, h, t * P:(t + 1) * P], mq[:, h, :], start=True, stop=True)
                        ins.then_inc(s_mm, 1)
                    if u >= 2:
                        pe.wait_ge(w_ready, u - 1)
                    pe.matmul(M[d][:, :], ident[0:8, h:h + 1].to_broadcast([8, P]),
                              grows[0:8, d, :, :].rearrange("p a b -> p (a b)"), start=True, stop=True).then_inc(bc_mm, 1)
                if u >= 1:
                    h, d = (u - 1) // 2, (u - 1) % 2
                    pe.wait_ge(ws_ready, u)
                    if u >= 3:
                        pe.wait_ge(fin_ready, u - 2)
                    for t in range(4):
                        pe.matmul(M[2 + d][:, 0:S], mv[:, t, h * P:(h + 1) * P], mW[d][:, t, :], start=(t == 0), stop=(t == 3))
                    for t in range(4):
                        ins = pe.matmul(M[2 + d][:, S:512], ones[:, :], mW[d][:, t, :], start=(t == 0), stop=(t == 3))
                    ins.then_inc(nd_mm, 1)
            norm_heads(mq)
            pe.wait_ge(ym_ready, 1)
            for i in range(4):
                gemm_T(FIRST["d_q"] + i, hw[:, :, S:512])
            for i in range(4):
                gemm_T(FIRST["d_k"] + i, hw, wide=True)
            for i in range(4):
                gemm_tokens(FIRST["d_v"] + i, hw, 4)
            for i in range(4):
                copied(pe, FIRST["d_v"] + i)
            pe.wait_ge(tab_in, 48)
            for c in range(8):
                t = (dq if c < 4 else dk)
                if c >= 2:
                    pe.wait_ge(rope_done, c - 1)
                for j in range(2):
                    src = dq[:, 2 * c + j, :] if c < 4 else dk[:, 2 * (c - 4) + j, S:512]
                    ins = pe.matmul(G[c % 2][:, j * S:(j + 1) * S], rtab[:, 0:P], src, start=True, stop=True)
                ins.then_inc(rot_mm, 1)
            pe.wait_ge(lam_in, 1)
            pe.matmul(M[3][:, 0:2], ones[0:64, :], lamp[0:64, :], start=True, stop=True).then_inc(lam_mm, 1)
            pe.wait_ge(rope_done, 8)
            for u in range(17):
                if u < 16:
                    h, T = u // 2, u % 2
                    if u >= 1:
                        pe.wait_ge(dexp, u)
                    for c in range(2):
                        ins = pe.matmul(M[c][:, :], dq[64 * c:64 * c + 64, h, T * P:(T + 1) * P], dk[64 * c:64 * c + 64, h, :],
                                        start=True, stop=True)
                    ins.then_inc(dqk_mm, 1)
                if u >= 1:
                    h, T, e = (u - 1) // 2, (u - 1) % 2, (u - 1) % 2
                    pe.wait_ge(dpd_ready, u)
                    for t in range(4):
                        ins = pe.transpose(M[2][:, t * P:(t + 1) * P], dpd[e][:, t * P:(t + 1) * P], ident[:, :])
                    ins.then_inc(dpt_mm, 1)
                    pe.wait_ge(dpt_ready, u)
                    pe.wait_ge(lam_exp, 1)
                    if u >= 2:
                        pe.wait_ge(dy_ready, u - 1)
                    for t in range(4):
                        ins = pe.matmul(M[3][:, 0:P], dv[:, t, h * P:(h + 1) * P], dPT[e][:, t, :], start=(t == 0), stop=(t == 3))
                    ins.then_inc(dpv_mm, 1)
            norm_heads(dq)
            pe.wait_ge(yd_ready, 1)
            with pe.Fori(0, 2) as it:
                for j in range(4):
                    gemm_T(FIRST["w_out"] + j, y2, it)
            norm(sq2, KT)
            norm(sq2, KT)
            pe.wait_ge(h_ready, 5)
            with pe.Fori(0, FF2 // 4) as it:
                for j in range(4):
                    gemm_T(FIRST["up2"] + j, hw[:, :, S:512], it)
            pe.wait_ge(ffn_done, FF2 + 2)
            down("down2", up2, DOWN2_KT)
            norm(sq2b, KT)

        @block.vector
        def _(dve):
            step = Chain(dve, dve_step)
            norms = [0]

            def invert(t, scale):
                norms[0] += 1
                dve.wait_ge(ms_ready, norms[0])
                step(dve.tensor_scalar(t, M[2][:, 0:S], scale, EPS, ALU.mult, ALU.add))
                dve.reciprocal(t, t).then_inc(inv_ready, 1)
                dve.wait_ge(rstd_ready, norms[0])

            def invert_heads(t):
                norms[0] += 1
                dve.wait_ge(ms_ready, norms[0])
                for b in range(4):
                    last = dve.tensor_scalar(t[:, 2 * b:2 * b + 2, :], G[b][:, :].rearrange("p (a b) -> p a b", a=2),
                                             1.0 / P, EPS, ALU.mult, ALU.add)
                step(last)
                dve.reciprocal(t, t).then_inc(inv_ready, 1)
                dve.wait_ge(rstd_ready, norms[0])

            def over_tiles(t, n=KT):
                return t.unsqueeze(1).to_broadcast([P, n, t.shape[-1]])

            def modulate(dst, src, rs, mul, add):
                step(dve.tensor_tensor(dst, src, over_tiles(rs), ALU.mult))
                for k in range(KT):
                    last = dve.tensor_scalar(dst[:, k, :], dst[:, k, :], mul[:, k:k + 1], add[:, k:k + 1], ALU.mult, ALU.add)
                return last

            def residual(t, mul):
                step(dve.tensor_tensor(t, t, over_tiles(rstd[:, 0:S]), ALU.mult))
                for k in range(KT):
                    last = dve.scalar_tensor_tensor(xT[:, k, :], t[:, k, :], mul[:, k:k + 1], xT[:, k, :], ALU.mult, ALU.add)
                last.then_inc(x_ready, 1)

            dve.wait_ge(brow_mm, 1)
            dve.tensor_tensor(brow[0:12, :], M[3][0:12, 0:BPITCH], bmask[0:12, :], ALU.add).then_inc(brow_ready, 1)
            dve.wait_ge(x_in, 16)
            dve.wait_ge(boot, 112)
            step(dve.tensor_copy(lvl_mask[:, :, :], lvl_f))
            invert(rstd[:, 0:S], 1.0 / D)
            lg = v("lb", 0, 8)
            step(dve.tensor_tensor(sm_e, lg, lg, ALU.subtract))
            dve.wait_ge(ada_cols, 48)
            step(dve.tensor_tensor(mod1[:, :], M[3][:, 0:192:2], v("b_ada", 0, 96), ALU.add))
            step(dve.scalar_tensor_tensor(amul, mod1[:, 16:32], 1.0, v("mix_pre", 0, 16), ALU.add, ALU.mult))
            modulate(h1, xT, rstd[:, 0:S], amul, mod1[:, 0:16]).then_inc(h_ready, 1)

            for i in range(6):
                copied(dve, FIRST["c_a"] + i)
            dve.wait_ge(fills, 3)
            step(dve.tensor_tensor(upad[:, :, 30:30 + S], ca, cy, ALU.mult))
            with dve.Fori(0, C_TILES // 2) as it:
                for tap in range(C_TAPS):
                    for j in range(2):
                        t = it * 2 + j
                        w = vec[:, bass.ds(VEC["conv_w"] + tap + j * C_TAPS + it * 2 * C_TAPS, 1)]
                        src = upad[:, bass.ds(t, 1), tap:tap + S].rearrange("p a b -> p (a b)")
                        dst = cy[:, bass.ds(t, 1), :].rearrange("p a b -> p (a b)")
                        if tap == 0:
                            b = vec[:, bass.ds(VEC["conv_b"] + j + it * 2, 1)]
                            ins = dve.tensor_scalar(dst, src, w, b, ALU.mult, ALU.add)
                        else:
                            dve.wait_ge(conv_tap, it * 2 * C_TAPS + 2 * tap + j - 1)
                            ins = dve.scalar_tensor_tensor(dst, src, w, dst, ALU.mult, ALU.add)
                        ins.then_inc(conv_tap, 1)
            dve.wait_ge(conv_tap, C_TILES * C_TAPS)
            dve.sem_inc(conv_y, 1)
            for i in range(4):
                copied(dve, FIRST["a_f"] + i)
            step(dve.tensor_scalar(lbc, sm_e, 0.0, TINY, ALU.max, ALU.add))
            step(dve.tensor_scalar(lb1, sm_e, 0.0, None, ALU.max))
            step(dve.tensor_scalar(lb1, lb1, -1.0, 1.0, ALU.mult, ALU.add))
            for h in range(8):
                dve.tensor_scalar(fP[:, h, :], fP[:, h, :], lb1[:, h:h + 1], lbc[:, h:h + 1], ALU.mult, ALU.add)
                last = dve.tensor_scalar(kk[:, h, :], kk[:, h, :], lb1[:, h:h + 1], None, ALU.mult)
            step(last)
            dve.wait_ge(mean_mm, 1)
            step(dve.tensor_scalar(rstd[:, S:512], M[2][:, S:512], 1.0 / (C_TILES * P), None, ALU.mult))
            dve.tensor_tensor(cy, cy, over_tiles(rstd[:, S:512], C_TILES), ALU.subtract).then_inc(conv_cent, 1)
            invert(rstd[:, 0:S], 1.0 / (C_TILES * P))
            dve.tensor_tensor(cy, cy, over_tiles(rstd[:, 0:S], C_TILES), ALU.mult).then_inc(yc_in, 1)
            dve.wait_ge(conv_done, 1)
            for i in range(4):
                copied(dve, FIRST["a_q"] + i)
            for half in range(2):
                if half:
                    dve.wait_ge(o_mm, half)
                hs = slice(4 * half, 4 * half + 4)
                f_, q_, k_ = fP[:, hs, :], qq[:, hs, :], kk[:, hs, :]
                step(dve.memset(suf, 1.0))
                ins = dve.memset(attn, 0.0)
                ins.then_inc(lvl_prep, 1)
                dve.wait_ge(lvl_prep, 9 * half + 1)
                for L in range(9):
                    c = 9 * half + L
                    if L:
                        if L > 1:
                            dve.wait_ge(lvl_mm, c)
                        dve.tensor_tensor(qs, q_, f_, ALU.mult)
                        last = dve.tensor_tensor(ks, k_, suf, ALU.mult)
                        last.then_inc(lvl_prep, 1)
                        dve.wait_ge(lvl_prep, c + 1)
                        if L < 8:
                            w = 1 << (L - 1)
                            fv_ = f_.rearrange("p h (b two w) -> p (h b) two w", two=2, w=w)
                            sv_ = suf.rearrange("p h (b two w) -> p (h b) two w", two=2, w=w)
                            nb = 4 * S // (2 * w)
                            step(dve.tensor_tensor(sv_[:, :, 0, :], sv_[:, :, 0, :],
                                                   fv_[:, :, 1, w - 1:w].to_broadcast([P, nb, w]), ALU.mult))
                            step(dve.tensor_tensor(fv_[:, :, 1, :], fv_[:, :, 1, :],
                                                   fv_[:, :, 0, w - 1:w].to_broadcast([P, nb, w]), ALU.mult))
                    dve.wait_ge(lvl_mm, c + 1)
                    if L < 8:
                        for b in range(2):
                            last = dve.copy_predicated(attn[:, 4 * b:4 * b + 4, :],
                                                       lvl_mask[:, L:L + 1, :].to_broadcast([P, 4, P]),
                                                       M[2 * (c % 2) + b][:, :].rearrange("p (a b) -> p a b", a=4))
                        last.then_inc(lvl_read, 1)
                        dve.wait_ge(lvl_read, c + 1 - half)
                    else:
                        dve.tensor_copy(attx, M[2 * (c % 2)][:, :].rearrange("p (a b) -> p a b", a=4)).then_inc(attn_ready, 1)
            for i in range(4):
                copied(dve, FIRST["a_g"] + i)
            invert_heads(kk)
            step(dve.tensor_tensor(qq, qq, kk, ALU.mult))
            dve.scalar_tensor_tensor(y1[:, 0:8, :], qq, v("hgrn_w"), og, ALU.mult, ALU.mult).then_inc(ya_ready, 1)
            dve.wait_ge(bias_in, 16)
            for u in range(9):
                if u < 8:
                    T, slot, e = u // 4, u % 4, u % 2
                    w = P * (T + 1)
                    b0 = 0 if T else P
                    dve.wait_ge(qk_mm, u + 1)
                    if u >= 2:
                        dve.wait_ge(pt_mm, u - 1)
                    psum01 = M[0][:, :].rearrange("p (a b) -> p a b", a=2)
                    dve.scalar_tensor_tensor(blog[e][:, 0:2, 0:w], psum01[:, :, 0:w], 0.125,
                                             bias[:, slot:slot + 5:4, b0:b0 + w], ALU.mult, ALU.add)
                    step(dve.scalar_tensor_tensor(blog[e][:, 2, 0:w], M[1][:, 0:w], 0.125, bias[:, 8 + slot, b0:b0 + w],
                                                  ALU.mult, ALU.add))
                    step(dve.tensor_reduce(nm[e][:, 0:1], blog[e][:, :, 0:w], mybir.AxisListType.XY, ALU.max))
                    dve.tensor_scalar(nm[e][:, 0:1], nm[e][:, 0:1], -1.0, None, ALU.mult).then_inc(log_ready, 1)
                if u >= 1:
                    e, T = (u - 1) % 2, (u - 1) // 4
                    dve.wait_ge(exp_ready, u)
                    step(dve.reciprocal(rz[e][:, 0:1], zz[e][:, 0:1]))
                    dve.tensor_scalar(bdg[e], ident[:, :], rz[e][:, 0:1], None, ALU.mult).then_inc(dg_ready, 1)
                    nch = 3 * (T + 1)
                    dve.wait_ge(pt_mm, u)
                    if u >= 3:
                        dve.wait_ge(pv_mm, u - 2)
                    last = dve.tensor_copy(bpt[e][:, 0:min(nch, 4), :],
                                           M[2][:, 0:min(nch, 4) * P].rearrange("p (a b) -> p a b", b=P))
                    if nch > 4:
                        last = dve.tensor_copy(bpt[e][:, 4:nch, :], M[3][:, 0:(nch - 4) * P].rearrange("p (a b) -> p a b", b=P))
                    last.then_inc(pt_ready, 1)
            dve.sem_inc(merged_ready, 1)
            with dve.Fori(0, 8) as it:
                n = FIRST["merge"] + 3
                dve.wait_ge(block_ready, READY["merge"] + 4 + it * 4)
                for g in range(3):
                    copied(dve, FIRST["merge"] + g, it)
                g_ = gates[:, 0]
                out = merged[:, bass.ds(it * 2, 2), :].rearrange("p a b -> p (a b)")
                step.offset = it * 3
                dve.tensor_tensor(mtmp[:, 0, :], M[0][:, :], g_[:, 0, :], ALU.mult)
                step(dve.tensor_tensor(mtmp[:, 1, :], M[1][:, :], g_[:, 1, :], ALU.mult))
                step(dve.tensor_tensor(mtmp[:, 0, :], mtmp[:, 0, :], mtmp[:, 1, :], ALU.add))
                ins = dve.tensor_tensor(mtmp[:, 1, :], M[2][:, :], g_[:, 2, :], ALU.mult)
                step(ins)
                dve.sem_inc(retired[n % SLOTS], 1)
                dve.tensor_tensor(out, mtmp[:, 0, :], mtmp[:, 1, :], ALU.add).then_inc(merged_ready, 1)
                dve.wait_ge(merged_ready, it + 2)
            step.n += 3 * 7
            step.offset = 0
            invert(rstd[:, 0:S], 1.0 / D)
            step(dve.tensor_tensor(gmul, mod1[:, 32:48], v("mix_post", 0, 16), ALU.mult))
            residual(proj1, gmul)
            invert(rstd[:, 0:S], 1.0 / D)
            step(dve.scalar_tensor_tensor(amul, mod1[:, 64:80], 1.0, v("mlp_pre", 0, 16), ALU.add, ALU.mult))
            modulate(h1, xT, rstd[:, 0:S], amul, mod1[:, 48:64]).then_inc(h_ready, 1)
            with dve.Fori(0, 8) as it:
                for j in range(4):
                    copied(dve, FIRST["up1"] + j, it)
                    t = up1[:, bass.ds(2 * j + it * 8, 2), :].rearrange("p a b -> p (a b)")
                    dve.tensor_tensor(t, t, t, ALU.mult).then_inc(up_ready, 1)
            invert(rstd[:, 0:S], 1.0 / D)
            step(dve.tensor_tensor(gmul, mod1[:, 80:96], v("mlp_post", 0, 16), ALU.mult))
            residual(down1, gmul)
            invert(rstd[:, 0:S], 1.0 / D)
            invert(rstd[:, S:512], 1.0 / D)
            dve.wait_ge(ada_cols, 96)
            for r in range(2):
                last = dve.tensor_tensor(mod2[:, r, :], M[3][:, r:192:2], v("b_mod", 0, 96), ALU.add)
            step(last)
            dve.scalar_tensor_tensor(amul, mod2[:, 0, 16:32], 1.0, v("g_pre_mix", 0, 16), ALU.add, ALU.mult)
            step(dve.scalar_tensor_tensor(cmul, mod2[:, 1, 16:32], 1.0, v("g_pre_mix", 0, 16), ALU.add, ALU.mult))
            modulate(hw[:, :, S:512], xT, rstd[:, S:512], amul, mod2[:, 0, 0:16]).then_inc(h_ready, 1)
            modulate(hw[:, :, 0:S], hw[:, :, 0:S], rstd[:, 0:S], cmul, mod2[:, 1, 0:16]).then_inc(h_ready, 1)

            def outer_taps(part, i, dst, tile0, wide, seen):
                n = FIRST[part] + i
                for j in range(2):
                    t = tile0 + 2 * i + j
                    bank = (M if wide and j else G)[n % SLOTS]
                    src = bank[:, :] if wide else bank[:, j * S:(j + 1) * S]
                    y = dst[:, 2 * i + j, :]
                    if wide:
                        src, y = (a.rearrange("p (s t) -> p s t", s=2) for a in (src, y))
                    else:
                        src, y = src.unsqueeze(1), y.unsqueeze(1)
                    dve.wait_ge(conv3_in, seen + 2)
                    step(dve.scalar_tensor_tensor(y[:, :, 1:S], src[:, :, 0:S - 1], v("qk_w", t), y[:, :, 1:S], ALU.mult, ALU.add))
                    dve.scalar_tensor_tensor(y[:, :, 0:S - 1], src[:, :, 1:S], v("qk_w", 32 + t), y[:, :, 0:S - 1],
                                             ALU.mult, ALU.add).then_inc(conv3_done, 1)
                dve.wait_ge(conv3_done, seen + 2)
                dve.sem_inc(retired[n % SLOTS], 1)

            for i in range(4):
                outer_taps("m_q", i, mq, 0, False, 2 * i)
            for i in range(4):
                outer_taps("m_k", i, mk, 8, True, 8 + 2 * i)
            dve.wait_ge(ln_ready, 1)
            one = ones[0:8, 0:1].to_broadcast([8, 512])
            one_s = ones[0:8, 0:1].to_broadcast([8, S])
            g8 = gG[0:8]
            step(dve.scalar_tensor_tensor(g8[:, 1:4:2, :], g8[:, 1:4:2, :], 0.0, gtmp[0:8, :, :], ALU.min, ALU.subtract))
            B8, M8 = gB[0:8], gM[0:8]
            last_c = slice(0, 1)
            dve.tensor_tensor_scan(B8[:, 0, :], one, g8[:, 1, :], 0.0, ALU.mult, ALU.add)
            step(dve.tensor_tensor_scan(B8[:, 1, 0:S][:, ::-1], one_s, g8[:, 3, 0:S][:, ::-1], 0.0, ALU.mult, ALU.add))
            step(dve.tensor_tensor_scan(B8[:, 1, S:512][:, ::-1], one_s, g8[:, 3, S:512][:, ::-1], B8[:, 1, last_c],
                                        ALU.mult, ALU.add))
            step(dve.tensor_tensor(g8[:, 0:4:2, :], g8[:, 0:4:2, :], B8[:, :, :], ALU.subtract))
            dve.tensor_tensor_scan(M8[:, 0, :], one, g8[:, 0, :], 0.0, ALU.mult, ALU.max)
            step(dve.tensor_tensor_scan(M8[:, 1, 0:S][:, ::-1], one_s, g8[:, 2, 0:S][:, ::-1], 0.0, ALU.mult, ALU.max))
            step(dve.tensor_tensor_scan(M8[:, 1, S:512][:, ::-1], one_s, g8[:, 2, S:512][:, ::-1], M8[:, 1, last_c],
                                        ALU.mult, ALU.max))
            r8 = grows[0:8]
            dve.tensor_scalar(r8[:, :, 0, :], M8[:, :, S:512], -1.0, None, ALU.mult)
            dve.scalar_tensor_tensor(r8[:, :, 1, :], B8[:, :, S:512], -1.0, M8[:, :, S:512], ALU.mult, ALU.subtract)\
               .then_inc(rows_ready, 1)
            dve.wait_ge(at_mm, 1)
            step(dve.tensor_copy(aT.rearrange("p a b c -> p (a b c)"), M[1][:, 0:64]))
            dve.sem_inc(at_ready, 1)
            dve.wait_ge(tab_in, 32)
            scale = float(P) ** -0.5
            for u in range(18):
                if u < 16:
                    h, d = u // 2, u % 2
                    dve.wait_ge(bc_mm, u + 1)
                    if u >= 2:
                        dve.wait_ge(nd_mm, u - 1)
                    for t in range(4):
                        a = aT[:, d, t, h:h + 1]
                        if t < 2:
                            last = dve.tensor_scalar(mW[d][:, t, :], M[d][:, 0:S], a, 0.0, ALU.add, ALU.min)
                        else:
                            o = (P if t == 2 else 0)
                            mask = tri[d][:, o:o + S]
                            last = dve.scalar_tensor_tensor(mW[d][:, t, :], M[d][:, 0:S], a, mask, ALU.add, ALU.min)
                    last.then_inc(w_arg, 1)
                if 1 <= u <= 16:
                    h, d = (u - 1) // 2, (u - 1) % 2
                    dve.wait_ge(w_ready, u)
                    dve.wait_ge(s_mm, h + 1)
                    for b in range(2):
                        last = dve.scalar_tensor_tensor(mW[d][:, 2 * b:2 * b + 2, :],
                                                        G[2 * (h % 2) + b][:, :].rearrange("p (a b) -> p a b", a=2), scale,
                                                        mW[d][:, 2 * b:2 * b + 2, :], ALU.mult, ALU.mult)
                    last.then_inc(ws_ready, 1)
                if u >= 2:
                    h, d = (u - 2) // 2, (u - 2) % 2
                    dve.wait_ge(den_ready, u - 1)
                    step(dve.tensor_tensor(mfl[d], mfl[d], mden, ALU.max))
                    step(dve.reciprocal(mfl[d], mfl[d]))
                    num = M[2 + d][:, 0:S]
                    if d == 0:
                        dve.tensor_tensor(y2[:, h, :], num, mfl[d], ALU.mult).then_inc(fin_ready, 1)
                    else:
                        step(dve.tensor_tensor(mfl[d], num, mfl[d], ALU.mult))
                        dve.wait_ge(fin_ready, u - 2)
                        dve.tensor_tensor(y2[:, h, :], y2[:, h, :], mfl[d], ALU.add).then_inc(fin_ready, 1)
            for i in range(4):
                copied(dve, FIRST["m_o"] + i)
            rh = mk[:, :, 0:S]
            invert_heads(rh)
            step(dve.tensor_tensor(y2[:, 0:8, :], y2[:, 0:8, :], rh, ALU.mult))
            for h in range(8):
                last = dve.scalar_tensor_tensor(y2[:, h, :], y2[:, h, :], v("g_mlstm", h), mo[:, h, :], ALU.mult, ALU.mult)
            last.then_inc(ym_ready, 1)
            lv = v("lam", 0, 4)[0:64, :]
            dve.tensor_tensor(lamp[0:64, :], lv[:, 0:4:2], lv[:, 1:4:2], ALU.mult).then_inc(lam_in, 1)
            for i in range(12):
                copied(dve, FIRST["d_q"] + i)
            dve.wait_ge(tab_in, 48)
            cos = rtab[:, P:P + S].unsqueeze(1).to_broadcast([P, 2, S])
            sin = rtab[:, P + S:P + 2 * S].unsqueeze(1).to_broadcast([P, 2, S])
            for c in range(8):
                dve.wait_ge(rot_mm, c + 1)
                t = dq[:, 2 * c:2 * c + 2, :] if c < 4 else dk[:, 2 * (c - 4):2 * (c - 4) + 2, S:512]
                dve.tensor_tensor(rtmp, G[c % 2][:, :].rearrange("p (a b) -> p a b", a=2), sin, ALU.mult)
                step(dve.tensor_tensor(t, t, cos, ALU.mult))
                dve.tensor_tensor(t, t, rtmp, ALU.add).then_inc(rope_done, 1)
                dve.wait_ge(rope_done, c + 1)
            dve.wait_ge(lam_exp, 1)
            step(dve.tensor_tensor(lamn, lame[:, 1:2], lame[:, 0:1], ALU.subtract))
            step(dve.tensor_scalar(lamn, lamn, -LAM_INIT, None, ALU.add))
            for u in range(17):
                if u < 16:
                    e = u % 2
                    dve.wait_ge(dqk_mm, u + 1)
                    dve.tensor_reduce(nm[e][:, 0:1], M[0][:, :], AX_X, ALU.max)
                    step(dve.tensor_reduce(nm[e][:, 1:2], M[1][:, :], AX_X, ALU.max))
                    dve.tensor_scalar(nm[e], nm[e], -0.125, None, ALU.mult).then_inc(dmax, 1)
                if u >= 1:
                    e = (u - 1) % 2
                    dve.wait_ge(dexp, u)
                    step(dve.reciprocal(rz[e], zz[e]))
                    step(dve.tensor_tensor(rz[e][:, 1:2], rz[e][:, 1:2], lamn, ALU.mult))
                    if u >= 3:
                        dve.wait_ge(dpt_mm, u - 2)
                    step(dve.tensor_scalar(dpd[e], dE[e][:, 0, :], rz[e][:, 0:1], None, ALU.mult))
                    dve.scalar_tensor_tensor(dpd[e], dE[e][:, 1, :], rz[e][:, 1:2], dpd[e], ALU.mult, ALU.add)\
                       .then_inc(dpd_ready, 1)
            rh = dk[:, :, 0:S]
            invert_heads(rh)
            step(dve.tensor_tensor(y2[:, 8:16, :], y2[:, 8:16, :], rh, ALU.mult))
            dve.tensor_scalar(y2[:, 8:16, :], y2[:, 8:16, :], v("g_diff"), 1.0 - LAM_INIT, ALU.mult, ALU.mult).then_inc(yd_ready, 1)
            invert(rstd[:, 0:S], 1.0 / D)
            step(dve.tensor_tensor(gmul, mod2[:, 0, 32:48], v("g_post_mix", 0, 16), ALU.mult))
            residual(proj2, gmul)
            invert(rstd[:, 0:S], 1.0 / D)
            step(dve.scalar_tensor_tensor(amul, mod2[:, 0, 64:80], 1.0, v("g_pre_ffn", 0, 16), ALU.add, ALU.mult))
            modulate(hw[:, :, S:512], xT, rstd[:, 0:S], amul, mod2[:, 0, 48:64]).then_inc(h_ready, 1)
            dve.sem_inc(ffn_done, 2)
            with dve.Fori(0, FF2 // 4) as it:
                step.offset = it * 8
                for j in range(4):
                    n = FIRST["up2"] + j
                    dve.wait_ge(taps_in, it * 4 + j + 1)
                    for side in range(2):
                        for c in range(2):
                            w = vec[:, bass.ds(VEC["ffn_w"] + side * 4 * FF2 + c * FF2 + j + it * 4, 1)]
                            src, y = G[n % SLOTS][:, c * S:(c + 1) * S], fv[:, j % 2, c, :]
                            if side == 0:
                                last = dve.scalar_tensor_tensor(y[:, 1:S], src[:, 0:S - 1], w, y[:, 1:S], ALU.mult, ALU.add)
                            else:
                                last = dve.scalar_tensor_tensor(y[:, 0:S - 1], src[:, 1:S], w, y[:, 0:S - 1], ALU.mult, ALU.add)
                        step(last)
                    dve.sem_inc(retired[n % SLOTS], 1)
                    dve.wait_ge(up_ready, it * 4 + j + 33)
                    dve.tensor_tensor(up2[:, bass.ds(j + it * 4, 1), :].rearrange("p a b -> p (a b)"),
                                      fv[:, j % 2, 0, :], fv[:, j % 2, 1, :], ALU.mult).then_inc(ffn_done, 1)
            step.n += 8 * (FF2 // 4 - 1)
            step.offset = 0
            invert(rstd[:, 0:S], 1.0 / D)
            step(dve.tensor_tensor(gmul, mod2[:, 0, 80:96], v("g_post_ffn", 0, 16), ALU.mult))
            residual(down2, gmul)



def constant_arrays():
    import math
    import numpy as np

    f = np.float32
    consts = np.zeros((P, NCONST), f)
    freqs, grid_w, base = 16, 64, 10000.0
    inv = (f(base) ** (-np.arange(freqs, dtype=f) / f(freqs))).astype(f)
    tok = np.arange(S)
    axis = np.stack([(tok // grid_w).astype(f), (tok % grid_w).astype(f)])
    perm = np.zeros((P, P), f)
    for p in range(P):
        ax, half, fr = (p // 32) % 2, (p // 16) % 2, p % 16
        ang = (axis[ax] * inv[fr]).astype(f)
        consts[p, CONST["cos"]:CONST["cos"] + S] = np.cos(ang)
        consts[p, CONST["sin"]:CONST["sin"] + S] = np.sin(ang)
        perm[p + 16 if half == 0 else p - 16, p] = -1.0 if half == 0 else 1.0
    consts[:, 0:P] = perm
    p, j = np.arange(P)[:, None], np.arange(384)[None, :] - P
    consts[:, CONST["tri_f"]:CONST["tri_f"] + 384] = np.where(j >= p, 0.0, MASK_VALUE)
    consts[:, CONST["tri_b"]:CONST["tri_b"] + 384] = np.where(j <= p, 0.0, MASK_VALUE)
    exact, buckets, far = 16, 32, 2048
    for i in range(BROW):
        d = 255 - i
        if d >= 0:
            if d < exact:
                b = d
            else:
                large = exact + int(np.float32(np.log(f(d) / f(exact)) / f(math.log(far / exact))) * f(buckets - exact))
                b = min(max(large, exact), buckets - 1)
            consts[b, CONST["onehot"] + i] = 1.0
    for g, (window, dil) in enumerate(((128, 1), (512, 4), (2048, 16))):
        for i in range(BPITCH):
            d = 255 - i
            ok = 0 <= d <= window and d % dil == 0
            consts[4 * g:4 * g + 4, CONST["bmask"] + i] = 0.0 if ok else MASK_VALUE
    s, t = np.arange(P)[:, None], np.arange(P)[None, :]
    lvl = np.zeros((P, 8, P), f)
    lvl[:, 0] = s == t
    for n in range(1, 8):
        w = 1 << (n - 1)
        lvl[:, n] = (s // (2 * w) == t // (2 * w)) & ((s // w) % 2 == 0) & ((t // w) % 2 == 1)
    ident = np.zeros((P, P + 2), f)
    ident[:, 0:P] = np.eye(P, dtype=f)
    for r in range(2):
        ident[r::32, P + r] = 1.0
    return consts, lvl, ident


def kernel(**inputs):
    import numpy as _np
    import concourse.bacc as _bacc
    from concourse.bass_utils import run_bass_kernel_spmd as _run

    a = {k: _np.asarray(x) for k, x in inputs.items()}

    def columns(x):
        return _np.ascontiguousarray(x.reshape(-1, P).T)

    def blocks(w):
        k, n = w.shape
        return w.reshape(k // P, P, n // COLS, COLS).transpose(2, 1, 0, 3)

    def down_blocks(w, kt):
        k, n = w.shape
        return w.reshape(4, kt, P, n // COLS, COLS).transpose(3, 0, 2, 1, 4).reshape(4 * n // COLS, P, kt, COLS)

    w_in = blocks(a["w_in"][0])
    cuts = dict(a_q=(0, 4), a_f=(4, 8), a_i=(8, 12), a_g=(12, 16), b_q=(16, 19), b_k=(19, 22), b_v=(22, 25),
                c_a=(25, 28), c_g=(28, 31))
    parts = {k: w_in[i:j] for k, (i, j) in cuts.items()}
    gate = blocks(a["w_gate"][0]).reshape(3, 8, P, KT, COLS)
    branches = blocks(_np.concatenate([a["w_a_out"][0], a["w_b_out"][0], a["w_c_out"][0]]))
    parts["merge"] = _np.concatenate([gate, branches[None]]).transpose(1, 0, 2, 3, 4).reshape(32, P, KT, COLS)
    parts["ada1"], parts["w_o"], parts["up1"] = blocks(a["w_ada"][0]), blocks(a["w_o"][0]), blocks(a["w_up"][0])
    parts["down1"] = down_blocks(a["w_down"][0], KT)
    w2 = a["w_in_2"][0]
    mg = 4 * 1024
    parts["ada2"] = blocks(a["w_mod_2"][0])
    for name, at in (("m_q", 0), ("m_k", 1024), ("m_v", 2048), ("m_o", 3072), ("d_q", mg + 32), ("d_k", mg + 1056), ("d_v", mg + 2080)):
        parts[name] = blocks(w2[:, at:at + 1024])
    parts["w_out"] = blocks(a["w_out_2"][0])
    up2 = a["w_up_2"][0].reshape(KT, P, 2, FF2, P)
    parts["up2"] = up2.transpose(3, 1, 0, 2, 4).reshape(FF2, P, KT, COLS)
    stream = _np.concatenate([parts[name] for name, _ in STREAM if name != "down2"])

    vectors = dict(
        c1=a["c"][0], c2=a["c_2"][0], cctx=a["c_ctx_2"], b_ada=a["b_ada"][0], mix_pre=a["mix_norm_pre"][0],
        mix_post=a["mix_norm_post"][0], mlp_pre=a["mlp_norm_pre"][0], mlp_post=a["mlp_norm_post"][0],
        b_gate=a["b_gate"][0], lb=a["hgrn_lb_logits"][0], hgrn_w=a["hgrn_norm_w"][0],
        conv_w=a["conv_w"][0].reshape(C_TAPS, C_TILES, P).transpose(1, 0, 2), conv_b=a["conv_b"][0],
        ln_g=a["conv_ln_g"][0], ln_b=a["conv_ln_b"][0], b_mod=a["b_mod_2"][0], g_pre_mix=a["g_pre_mix_2"][0],
        g_post_mix=a["g_post_mix_2"][0], g_pre_ffn=a["g_pre_ffn_2"][0], g_post_ffn=a["g_post_ffn_2"][0],
        qk_w=a["conv_qk_w_2"][0], qk_b=a["conv_qk_b_2"][0], g_mlstm=a["g_mlstm_2"][0], g_diff=a["g_diff_2"][0],
        ffn_w=a["conv_ffn_w_2"][0], ffn_b=a["conv_ffn_b_2"][0])
    vec = _np.zeros((P, NVEC), _np.float32)
    for name, x in vectors.items():
        c = columns(x)
        vec[:, VEC[name]:VEC[name] + c.shape[1]] = c
    vec[0:32, VEC["mg_b"]] = a["b_gate_2"][0].reshape(-1)
    for i, name in enumerate(("lambda_q1_2", "lambda_k1_2", "lambda_q2_2", "lambda_k2_2")):
        vec[0:64, VEC["lam"] + i] = a[name][0]

    def tokens_last(x):
        return _np.ascontiguousarray(x.reshape(S, KT, P).transpose(2, 1, 0))

    consts, lvl, ident = constant_arrays()
    arrays = dict(
        stream=stream, stream_down2=_np.ascontiguousarray(down_blocks(a["w_down_2"][0], DOWN2_KT)),
        x_t=tokens_last(a["x"][0]), ctx_t=tokens_last(a["ctx_2"][0]), vec=vec, consts=consts, lvl_mask=lvl, ident=ident,
        mg_w=_np.ascontiguousarray(w2[:, mg:mg + 32].reshape(KT, P, 32).transpose(1, 0, 2)), rel_bias=a["rel_bias"])

    nc = _bacc.Bacc("TRN2", target_bir_lowering=False, num_devices=1)
    aps = [nc.dram_tensor(k, x.shape, mybir.dt.from_np(x.dtype), kind="ExternalInput").ap() for k, x in arrays.items()]
    scratch = nc.dram_tensor("bias_rows", (B_HEADS, P * BPITCH), F32, kind="Internal").ap()
    out = nc.dram_tensor("out_t", (P, KT, S), F32, kind="ExternalOutput").ap()
    two_blocks_kernel(nc, *aps, scratch, out)
    got = _run(nc, [arrays], core_ids=[0]).results[0]["out_t"]
    return _np.ascontiguousarray(got.transpose(2, 1, 0)).reshape(1, S, D)
```

```python
from contextlib import ExitStack

import concourse.bass as bass
from concourse import mybir

F32 = mybir.dt.float32
U8 = mybir.dt.uint8
ALU = mybir.AluOpType
ACT = mybir.ActivationFunctionType
AX_X = mybir.AxisListType.X

F32R = mybir.dt.float32r
P = 128
S = 256
D = 2048
KT = D // P
SLOTS = 4
EPS = 1e-6
TINY = 1e-30
MASK_VALUE = -1e30
A_HEADS, B_HEADS, B_SLOTS = 8, 12, 4
C_TILES, C_TAPS = 6, 31
FF1, FF2 = 8192 // P, 5632 // P
QUARTER = 4
UP2 = FF2 // QUARTER
LAM_INIT = 0.2
BROW = 383
BPITCH = 384

MIX = "GAGAGAAG"
SECTIONS = (
    [("ada1a", "A" * 4, 8), ("c_a", "G", 6), ("c_g", "G", 6), ("a_f", "G", 8), ("a_q", "G", 8), ("a_i", "G", 8), ("b_v", "G", 6),
     ("b_k", "G", 6), ("b_q", "G", 6), ("a_g", "G", 8), ("merge", MIX, 16), ("w_o", MIX, 4)]
    + [s for q in range(QUARTER) for s in ((f"up1_{q}", MIX, 4), (f"down1_{q}", "GGGG" if q else MIX, 4))]
    + [("m_q", "G", 8), ("m_k", "G", 8), ("m_g", "G", 1), ("m_v", "G", 8), ("m_o", "G", 8), ("d_q", "G", 8), ("d_k", "G", 8),
       ("d_v", "G", 8), ("w_out", "G", 16)]
    + [s for q in range(QUARTER) for s in ((f"up2_{q}", "G", 2 * UP2), (f"down2_{q}", "G", 16))]
)


def plan_stream():
    g, a, first = [], [], {}
    n = 0
    for name, pattern, times in SECTIONS:
        first[name] = (n, len(g), len(a))
        for kind in pattern * times:
            (g if kind == "G" else a).append(n)
            n += 1
    return g, a, first, n


G_AT, A_AT, FIRST, N_STREAM = plan_stream()


def gb(name, i=0):
    return FIRST[name][1] + i


VECTORS = [
    ("c1", 16), ("c2", 16), ("cctx", 16), ("b_ada", 96), ("mix_pre", 16), ("mix_post", 16), ("mlp_pre", 16),
    ("mlp_post", 16), ("b_gate", 48), ("lb", 8), ("hgrn_w", 1), ("conv_w", C_TILES * C_TAPS), ("conv_b", 6),
    ("ln_g", 6), ("ln_b", 6), ("b_mod", 96), ("g_pre_mix", 16), ("g_post_mix", 16), ("g_pre_ffn", 16),
    ("g_post_ffn", 16), ("qk_w", 48), ("qk_b", 16), ("g_mlstm", 8), ("g_diff", 1), ("ffn_w", 3 * 2 * FF2),
    ("ffn_b", 2 * FF2), ("mg_b", 1), ("lam", 4),
]


def vector_columns():
    at, n = {}, 0
    for name, width in VECTORS:
        at[name] = n
        n += width
    return at, n


VEC, NVEC = vector_columns()

CONSTS = [("perm", P), ("cos", S), ("sin", S), ("tri_f", P), ("tri_b", P), ("onehot", BPITCH), ("bmask", BPITCH)]


def const_columns():
    at, n = {}, 0
    for name, width in CONSTS:
        at[name] = n
        n += width
    return at, n


CONST, NCONST = const_columns()


class Chain:

    def __init__(self, engine, sem):
        self.engine, self.sem, self.n, self.offset = engine, sem, 0, 0

    def __call__(self, instruction):
        self.n += 1
        instruction.then_inc(self.sem, 1)
        self.engine.wait_ge(self.sem, self.n + self.offset)


def two_blocks_kernel(nc, stream, x_t, ctx_t, vec_d, const_d, lvl_mask_d, ident_d, rel_bias, scratch, x_keep, out_t):
    with ExitStack() as ctx:
        def sb(name, shape, dt=F32):
            return ctx.enter_context(nc.sbuf_tensor("sb_" + name, shape, dt))

        def sem(name):
            return ctx.enter_context(nc.semaphore(name))

        raw = sb("raw", [P, SLOTS, KT, P])
        parts = sb("parts", [P, 2, 2, KT, P], F32R)
        ident = sb("ident", [P, P])
        ones = sb("ones", [P, P])
        vec = sb("vec", [P, NVEC])
        cpad = sb("cpad", [P, KT, 64])
        sel = sb("sel", [P, 8])
        mod1 = sb("mod1", [P, 96])
        mod2 = sb("mod2", [P, 2, 96])
        lvl_mask = sb("lvl_mask", [P, 8, P], U8)
        rstd = sb("rstd", [P, 512])
        small = sb("small", [P, 128])
        ARENA = 33024

        def operand(name, at, *dims):
            with nc.sbuf_tensor("pad_" + name, [P, at], F32), nc.sbuf_tensor("op_" + name, [P, *dims], F32R) as t:
                return t

        opH = operand("h", 4096, 2, KT, S)
        opY1 = operand("y1", 20480, 2, KT, S)
        opG = operand("merged", 12288, 2, KT, S)
        opU1 = operand("up1", 12288, 2, KT, S)
        opW = operand("hw", 4096, 2, KT, 512)
        opY2 = operand("y2", 12288, 2, KT, S)
        opU2 = operand("up2", 12288, 2, UP2, S)
        arena = sb("arena", [P, ARENA])
        G = [ctx.enter_context(nc.psum_tensor(f"gemm{i}", [P, 512], F32)) for i in range(4)]
        M = [ctx.enter_context(nc.psum_tensor(f"mix{i}", [P, 512], F32)) for i in range(4)]

        def region(at, *dims):
            n = 1
            for d in dims:
                n *= d
            assert at + n <= ARENA, (at, dims)
            flat = arena[:, at:at + n]
            if len(dims) == 1:
                return flat
            names = "abc"[:len(dims)]
            return flat.rearrange(f"p ({' '.join(names)}) -> p {' '.join(names)}", **dict(zip(names, dims)))

        def v(name, i=0, n=1):
            return vec[:, VEC[name] + i:VEC[name] + i + n]

        xT = region(0, KT, S)
        sq0 = region(12288, KT, S)
        hf0 = region(16384, KT, S)
        onehot, bmask, brow = region(20480, BPITCH), region(20864, BPITCH), region(21248, BPITCH)
        relb = region(21632, 12)
        lvl_f = region(22528, 8, P)
        modrow1 = region(32640, P)
        fP = region(12288, 8, S)
        kk = region(14336, 8, S)
        qq = region(16384, 8, S)
        og = region(18432, 8, S)
        bq = region(20480, 6, S)
        bk = region(22016, 6, S)
        bv = region(23552, 2, 768)
        ii = region(25088, 2, 1024)
        ca = region(18432, 6, S)
        upad = region(19968, 6, 30 + S)
        cy = region(21684, 6, S)
        yc = region(28672, 6, S)
        yb = region(30208, 2, S)
        suf = region(30720, 2, S)
        qs = region(31232, 2, S)
        ks = region(31744, 2, S)
        attn = region(32256, 4, P)
        attx = region(32768, 2, P)
        bias = region(12288, 12, S)
        blog = [region(15360 + 768 * i, 3, S) for i in range(2)]
        bpt = [region(16896 + 768 * i, 6, P) for i in range(2)]
        bdg = [region(30720 + P * i, P) for i in range(2)]
        gates = region(28672, 2, 3, S)
        mtmp = region(30208, 2, S)
        mfp = region(30720, 2, S)
        proj1 = region(4096, KT, S)
        sq1 = region(8192, KT, S)
        hf1 = region(20480, KT, S)
        ut = region(20480, 2, 2, S)
        modrow2 = region(22528, P)
        down1 = region(24576, KT, S)
        sqd1 = region(28672, KT, S)
        hfc = region(20480, KT, S)
        sqc = region(24576, KT, S)
        hfx = region(28672, KT, S)
        mq = region(20480, 8, S)
        mk = region(22528, 8, 512)
        mv = region(26624, 4, 1024)
        ym = region(0, 8, S)
        gG = region(0, 4, 512)
        gsb = region(2048, 512)
        gB = region(30720, 2, 512)
        gM = region(31744, 2, 512)
        gtmp = region(31744, 2, 512)
        grows = region(2048, 2, 2, S)
        aT = region(3072, 2, 4, 8)
        tri = [region(3136 + P * i, P) for i in range(2)]
        mden = region(3392, S)
        mW = [region(30720 + 1024 * i, 4, S) for i in range(2)]
        mfl = [region(3648, S), region(32768, S)]
        mo = region(30720, 8, S)
        dq = region(20480, 8, S)
        dk = region(22528, 8, 512)
        dv = region(26624, 4, 1024)
        yd = region(2048, 8, S)
        dE = [region(4096 + 1024 * i, 2, 512) for i in range(2)]
        dpd = [region(6144 + 512 * i, 512) for i in range(2)]
        dPT = [region(7168 + 512 * i, 4, P) for i in range(2)]
        rtab = region(8192, 640)
        rtmp = region(8832, 2, S)
        nsq = region(4096, 8, S)
        nrs = region(6144, 8, S)
        proj2 = region(20480, KT, S)
        sq2 = region(24576, KT, S)
        hf2 = region(28672, KT, S)
        fv = region(18432, 2, 2, S)
        ftm = region(19456, 2, S)
        down2 = region(20480, KT, S)

        amul, gmul, cmul = small[:, 0:16], small[:, 16:32], small[:, 64:80]
        lbc, lb1, sm_e = small[:, 32:40], small[:, 40:48], small[:, 80:88]
        lamn = small[:, 48:49]
        nm = [small[:, 96 + 2 * i:98 + 2 * i] for i in range(2)]
        zz = [small[:, 104 + 2 * i:106 + 2 * i] for i in range(2)]
        rz = [small[:, 112 + 2 * i:114 + 2 * i] for i in range(2)]
        lamp, lame = small[:, 120:122], small[:, 122:124]

        loaded = [sem(f"loaded{i}") for i in range(SLOTS)]
        taken = [sem(f"taken{i}") for i in range(SLOTS)]
        hi_ready = sem("hi_ready")
        hi_used = sem("hi_used")
        block_done = sem("block_done")
        bank_read = [sem(f"bank_read{i}") for i in range(4)]
        boot, x_in, fills, c_ready = sem("boot"), sem("x_in"), sem("fills"), sem("c_ready")
        row_ready, ada_cols = sem("row_ready"), sem("ada_cols")
        sq_ready, ms_ready, inv_ready, rstd_ready = (sem(n) for n in ("sq_ready", "ms_ready", "inv_ready", "rstd_ready"))
        hf_ready, hh_ready, h_ready, x_ready = (sem(n) for n in ("hf_ready", "hh_ready", "h_ready", "x_ready"))
        dve_step, act_step = sem("dve_step"), sem("act_step")
        brow_mm, brow_ready, brow_out, bias_in = sem("brow_mm"), sem("brow_ready"), sem("brow_out"), sem("bias_in")
        conv_tap, conv_y, mean_mm, conv_cent, yc_in, conv_done = (
            sem(n) for n in ("conv_tap", "conv_y", "mean_mm", "conv_cent", "yc_in", "conv_done"))
        lvl_prep, lvl_mm, lvl_read, attn_ready, o_mm, o_copied, ya_ready = (
            sem(n) for n in ("lvl_prep", "lvl_mm", "lvl_read", "attn_ready", "o_mm", "o_copied", "ya_ready"))
        qk_mm, log_ready, exp_ready, dg_ready = sem("qk_mm"), sem("log_ready"), sem("exp_ready"), sem("dg_ready")
        pt_mm, pt_ready, pv_mm, yb_ready = sem("pt_mm"), sem("pt_ready"), sem("pv_mm"), sem("yb_ready")
        y_hi, y_ready = sem("y_hi"), sem("y_ready")
        gates_done, merged_part = sem("gates_done"), sem("merged_part")
        relu_ready, up_ready = sem("relu_ready"), sem("up_ready")
        x_kept, x_back, cx_in, tab_in, mg_sb, mg_rows = (sem(n) for n in ("x_kept", "x_back", "cx_in", "tab_in", "mg_sb", "mg_rows"))
        ln_ready, rows_ready, at_mm, at_ready = (sem(n) for n in ("ln_ready", "rows_ready", "at_mm", "at_ready"))
        conv3_in, conv3_done, silu_done = sem("conv3_in"), sem("conv3_done"), sem("silu_done")
        s_mm, bc_mm, w_arg, w_ready, ws_ready = (sem(n) for n in ("s_mm", "bc_mm", "w_arg", "w_ready", "ws_ready"))
        nd_mm, den_ready, fin_ready, ym_ready = sem("nd_mm"), sem("den_ready"), sem("fin_ready"), sem("ym_ready")
        rot_mm, rope_done = sem("rot_mm"), sem("rope_done")
        lam_in, lam_mm, lam_exp = sem("lam_in"), sem("lam_mm"), sem("lam_exp")
        dqk_mm, dmax, dexp, dpd_ready = sem("dqk_mm"), sem("dmax"), sem("dexp"), sem("dpd_ready")
        dpt_mm, dpt_ready, dpv_mm, dy_ready, yd_ready = (sem(n) for n in ("dpt_mm", "dpt_ready", "dpv_mm", "dy_ready", "yd_ready"))
        taps_in, gate_silu, ffn_done = sem("taps_in"), sem("gate_silu"), sem("ffn_done")
        stored = sem("stored")

        def use(n, it=0, dn=0):
            return n % SLOTS, n // SLOTS + it * (dn // SLOTS)

        def kt_of(b):
            return UP2 if any(gb(f"down2_{q}") <= b < gb(f"down2_{q}") + 16 for q in range(QUARTER)) else KT

        def buffer_of(b):
            q = max(q for q in range(QUARTER) if gb(f"up2_{q}") <= b)
            return (q * UP2 + (b - gb(f"up2_{q}")) // 2) % 2

        def tiles_of(direction):
            return (2, 3, slice(P, S)) if direction == 0 else (3, 2, slice(0, P))

        def bank(b):
            return G[b % 4]

        def done(eng, b, it=0):
            eng.wait_ge(block_done, b + 1 + it * 4)

        def was_read(eng, b, it=0):
            eng.wait_ge(bank_read[b % 4], b // 4 + 1 + it)

        def steps_of(section):
            pattern = {name: p for name, p, _ in SECTIONS}[section]
            return len(pattern) if len(pattern) > 1 else 4

        block = ctx.enter_context(nc.Block())

        @block.sync
        def _(sp):
            def load_run(n0, count, kt):
                def load(n, r):
                    slot, uses = use(n, r, SLOTS)
                    if n >= SLOTS:
                        sp.wait_ge(taken[slot], uses)
                    sp.dma_start(raw[:, slot, 0:kt, :], stream[r * SLOTS + n][:, 0:kt, :]).then_inc(loaded[slot], 16)

                if count >= 2 * SLOTS:
                    with sp.Fori(0, count // SLOTS) as r:
                        for j in range(SLOTS):
                            load(n0 + j, r)
                for n in range(n0 + (count // SLOTS * SLOTS if count >= 2 * SLOTS else 0), n0 + count):
                    load(n, 0)

            load_run(0, SLOTS, KT)
            at = SLOTS
            for q in range(QUARTER):
                d = FIRST[f"down2_{q}"][0]
                load_run(at, d - at, KT)
                load_run(d, 16, UP2)
                at = d + 16
            sp.wait_ge(x_ready, 4)
            sp.dma_start(out_t, xT).then_inc(stored, 16)
            sp.wait_ge(stored, 16)

        @block.gpsimd
        def _(pool):
            pool.memset(cpad[:, :, :], 0.0).then_inc(fills, 1)
            pool.memset(ones[:, :], 1.0).then_inc(fills, 1)
            pool.wait_ge(brow_ready, 1)
            pool.dma_start(scratch[:, 0:P * BPITCH].rearrange("h (p c) -> h p c", c=BPITCH),
                           brow[0:12, :].unsqueeze(1).to_broadcast([12, P, BPITCH])).then_inc(brow_out, 16)
            pool.wait_ge(brow_out, 16)
            pool.wait_ge(ya_ready, 1)
            skew = scratch[:, 0:P * (BPITCH - 1)].rearrange("h (p c) -> p h c", c=BPITCH - 1)
            pool.dma_start(bias, skew[:, :, P - 1:P - 1 + S]).then_inc(bias_in, 16)
            pool.wait_ge(x_ready, 2)
            pool.dma_start(hfc, ctx_t).then_inc(cx_in, 16)
            pool.wait_ge(hf_ready, 4)
            pool.dma_start(x_keep, xT).then_inc(x_kept, 16)
            pool.wait_ge(x_kept, 16)
            pool.dma_start(tri[0], const_d[:, CONST["tri_f"]:CONST["tri_f"] + P]).then_inc(tab_in, 16)
            pool.dma_start(tri[1], const_d[:, CONST["tri_b"]:CONST["tri_b"] + P]).then_inc(tab_in, 16)
            pool.wait_ge(mg_sb, 1)
            for g in range(4):
                pool.dma_start(gG[0:8, g, :], gsb[8 * g:8 * g + 8, :]).then_inc(mg_rows, 16)
            done(pool, gb("d_v", 7))
            pool.dma_start(rtab, const_d[:, 0:640]).then_inc(tab_in, 16)
            pool.wait_ge(h_ready, 5)
            pool.dma_start(xT, x_keep).then_inc(x_back, 16)

        @block.scalar
        def _(act):
            step = Chain(act, act_step)
            norms, rows, splits = [0], [0], [0]

            act.dma_start(vec[:, :], vec_d).then_inc(boot, 16)
            act.dma_start(ident[:, :], ident_d[:, 0:P]).then_inc(boot, 16)
            act.dma_start(sel[:, :], ident_d[:, P:P + 8]).then_inc(boot, 16)
            act.dma_start(lvl_f, lvl_mask_d).then_inc(boot, 16)
            act.dma_start(onehot, const_d[:, CONST["onehot"]:CONST["onehot"] + BPITCH]).then_inc(boot, 16)
            act.dma_start(bmask, const_d[:, CONST["bmask"]:CONST["bmask"] + BPITCH]).then_inc(boot, 16)
            act.dma_start(relb[0:32, :], rel_bias).then_inc(boot, 16)
            act.dma_start(xT, x_t).then_inc(x_in, 16)

            def square(dst, src):
                norms[0] += 1
                act.activation(dst, src, ACT.Square).then_inc(sq_ready, 1)

            def root(t):
                act.wait_ge(inv_ready, norms[0])
                act.activation(t, t, ACT.Sqrt).then_inc(rstd_ready, 1)

            def high(dst, src):
                splits[0] += 1
                act.wait_ge(hf_ready, splits[0])
                act.activation(dst, src, ACT.Copy).then_inc(hh_ready, 1)

            def split_high(b, it=0, dn=0):
                if b >= len(G_AT):
                    return
                slot, uses = use(G_AT[b], it, dn)
                kt = kt_of(b)
                act.wait_ge(loaded[slot], 16 * (uses + 1))
                if b >= 2:
                    act.wait_ge(hi_used, b - 1 + it * 4)
                act.activation(parts[:, b % 2, 0, 0:kt, :], raw[:, slot, 0:kt, :], ACT.Copy).then_inc(hi_ready, 1)

            def copy_rows(a_last, it, dn, modrow, group):
                slot, uses = use(A_AT[a_last], it, dn)
                act.wait_ge(taken[slot], uses + 1)
                act.wait_ge(ada_cols, group)
                act.activation(modrow, M[2][:, 0:P], ACT.Copy).then_inc(row_ready, 1)

            def copy_out(b, dst, func=ACT.Copy, it=0, cols=S):
                done(act, b, it)
                act.activation(dst, bank(b)[:, 0:cols], func).then_inc(bank_read[b % 4], 1)

            def rounds(section, body):
                n = {name: t * p.count("G") // 4 for name, p, t in SECTIONS}[section]
                with act.Fori(0, n - 1) as it:
                    body(it, 0)
                body(0, n - 1)

            def in_round(section, it, peeled):
                b0, dn = gb(section), steps_of(section)

                def ahead(j):
                    if peeled:
                        split_high(b0 + 4 * peeled + j + 2)
                    else:
                        split_high(b0 + j + 2, it, dn)
                return b0 + 4 * peeled, it, ahead

            act.wait_ge(x_in, 16)
            square(sq0, xT)
            root(rstd[:, 0:S])
            act.wait_ge(boot, 112)
            act.wait_ge(fills, 1)
            act.activation(cpad[:, :, 32], v("c1", 0, 16), ACT.Silu).then_inc(c_ready, 1)
            with act.Fori(0, 8) as it:
                slot, uses = use(3, it, 4)
                act.wait_ge(taken[slot], uses + 1)
                act.activation(modrow1, M[2][:, 0:P], ACT.Copy).then_inc(row_ready, 1)
            split_high(0)
            split_high(1)
            high(opH[:, 0], hf0)
            for i in range(6):
                b = gb("c_a", i)
                split_high(b + 2)
                copy_out(b, ca[:, i, :])
            for i in range(6):
                b = gb("c_g", i)
                split_high(b + 2)
                copy_out(b, cy[:, i, :], ACT.Sigmoid)
            act.wait_ge(brow_out, 16)
            for i in range(8):
                b = gb("a_f", i)
                split_high(b + 2)
                done(act, b)
                act.activation(fP[:, i, :], bank(b)[:, 0:S], ACT.Sigmoid)
                act.activation(kk[:, i, :], bank(b)[:, 0:S], ACT.Sigmoid, scale=-1.0).then_inc(bank_read[b % 4], 1)
            for i in range(8):
                b = gb("a_q", i)
                split_high(b + 2)
                copy_out(b, qq[:, i, :], ACT.Silu)

            def copy_tokens(part, i, dst, tiles):
                b = gb(part, i)
                done(act, b)
                act.activation(dst[:, 0:tiles, i * P:(i + 1) * P], bank(b)[:, 0:tiles * P].rearrange("p (a b) -> p a b", b=P),
                               ACT.Copy).then_inc(bank_read[b % 4], 1)

            def copy_o(quarter):
                act.wait_ge(o_mm, quarter + 1)
                act.activation(qq[:, 2 * quarter:2 * quarter + 2, :], M[3][:, :].rearrange("p (a b) -> p a b", a=2), ACT.Copy)\
                   .then_inc(o_copied, 1)

            late = [("a_i", i) for i in range(8)] + [("b_v", i) for i in range(6)] + [("b_k", i) for i in range(6)] \
                + [("b_q", i) for i in range(6)] + [("a_g", i) for i in range(8)]
            for s in range(36):
                if s < len(late):
                    part, i = late[s]
                    b = gb(part, i)
                    split_high(b + 2)
                    if part in ("a_i", "b_v"):
                        copy_tokens(part, i, ii if part == "a_i" else bv, 2)
                    elif part == "a_g":
                        copy_out(b, og[:, i, :], ACT.Silu)
                    else:
                        copy_out(b, (bk if part == "b_k" else bq)[:, i, :])
                if s % 9 == 0 and s:
                    copy_o(s // 9 - 1)
                if s == 3:
                    act.wait_ge(conv_cent, 1)
                    square(ca, cy)
                if s == 5:
                    root(rstd[:, 0:S])
                if s == 7:
                    act.wait_ge(yc_in, 1)
                    for t in range(C_TILES):
                        ins = act.activation(yc[:, t, :], cy[:, t, :], ACT.Silu, bias=v("ln_b", t), scale=v("ln_g", t))
                    ins.then_inc(conv_done, 1)
            copy_o(3)
            act.wait_ge(o_copied, 4)
            square(fP, qq)
            root(kk)
            for u in range(9):
                if u < 8:
                    T, e = u // 4, u % 2
                    w = P * (T + 1)
                    act.wait_ge(log_ready, u + 1)
                    act.activation(blog[e][:, :, 0:w], blog[e][:, :, 0:w], ACT.Exp, bias=nm[e][:, 0:1],
                                   accum_out=zz[e][:, 0:1]).then_inc(exp_ready, 1)
                if u >= 1:
                    T, slot, e = (u - 1) // 4, (u - 1) % 4, (u - 1) % 2
                    po = 64 * (slot % 2)
                    act.wait_ge(pv_mm, u)
                    act.activation(yb[po:po + 64, slot // 2, P * T:P * T + P], G[e][po:po + 64, 0:P], ACT.Copy)\
                       .then_inc(yb_ready, 1)
            act.wait_ge(yb_ready, 8)
            act.activation(opY1[:, 0, 0:8, :], og, ACT.Copy)
            act.activation(opY1[:, 0, 8:10, :], yb, ACT.Copy)
            act.activation(opY1[:, 0, 10:16, :], yc, ACT.Copy).then_inc(y_hi, 1)
            act.wait_ge(y_ready, 1)

            def merge_round(it, peeled):
                b0, it, ahead = in_round("merge", it, peeled)
                for j in range(4):
                    ahead(j)
                    if j < 3:
                        done(act, b0 + j, it)
                        if j == 0:
                            act.wait_ge(merged_part, it + peeled + 1)
                        act.activation(gates[:, 0, j, :], bank(b0 + j)[:, 0:S], ACT.Sigmoid,
                                       bias=vec[:, bass.ds(VEC["b_gate"] + 16 * j + it + peeled, 1)]).then_inc(bank_read[(b0 + j) % 4], 1)
                    if j == 2:
                        a = FIRST["merge"][2] + 3 + 4 * peeled
                        copy_rows(a, it, 8, modrow1, FIRST["merge"][2] // 4 + it + peeled)

            rounds("merge", merge_round)
            act.wait_ge(ada_cols, 24)
            act.activation(cpad[:, :, 32], v("c2", 0, 16), ACT.Silu)
            act.activation(cpad[:, :, 33], v("cctx", 0, 16), ACT.Silu).then_inc(c_ready, 1)

            def plain_round(section, dst, func=ACT.Copy, modrow=None):
                def body(it, peeled):
                    b0, it, ahead = in_round(section, it, peeled)
                    for j in range(4):
                        ahead(j)
                        copy_out(b0 + j, dst[:, bass.ds(j + it * 4 + 4 * peeled, 1), :].rearrange("p a b -> p (a b)"), func, it)
                        if modrow is not None and j == 2:
                            a = FIRST[section][2] + 3 + 4 * peeled
                            copy_rows(a, it, 8, modrow, FIRST[section][2] // 4 + it + peeled)
                return body

            rounds("w_o", plain_round("w_o", proj1, modrow=modrow2))
            was_read(act, gb("w_o", 15))
            square(sq1, proj1)
            root(rstd[:, 0:S])
            act.wait_ge(x_ready, 1)
            square(sq1, xT)
            root(rstd[:, 0:S])
            high(opH[:, 0], hf1)
            for q in range(QUARTER):
                def up_round(it, peeled, section=f"up1_{q}", q=q):
                    b0, it, ahead = in_round(section, it, peeled)
                    for j in range(4):
                        ahead(j)
                        done(act, b0 + j, it)
                        act.wait_ge(up_ready, 16 * q + 4 * peeled + j + 1 + it * 4)
                        act.activation(ut[:, j % 2, 0, :], bank(b0 + j)[:, 0:S], ACT.Relu).then_inc(bank_read[(b0 + j) % 4], 1)
                        if j == 2:
                            a = FIRST[section][2] + 3 + 4 * peeled
                            copy_rows(a, it, 8, modrow2, FIRST[section][2] // 4 + it + peeled)
                rounds(f"up1_{q}", up_round)

                if q == 0:
                    rounds("down1_0", plain_round("down1_0", down1, modrow=modrow2))
                else:
                    def down_round(it, peeled, section=f"down1_{q}"):
                        b0, it, ahead = in_round(section, it, peeled)
                        for j in range(4):
                            ahead(j)
                    rounds(f"down1_{q}", down_round)
            was_read(act, gb("down1_3", 15))
            square(sqd1, down1)
            root(rstd[:, 0:S])
            act.wait_ge(x_ready, 2)
            act.wait_ge(cx_in, 16)
            square(sqc, hfc)
            root(rstd[:, 0:S])
            high(opW[:, 0, :, 0:S], hfc)
            square(sqc, xT)
            root(rstd[:, S:512])
            high(opW[:, 0, :, S:512], hfx)

            def conv3_block(part, i, dst, tile0, cols):
                b = gb(part, i)
                split_high(b + 2)
                done(act, b)
                act.activation(dst[:, i, :], bank(b)[:, 0:cols], ACT.Identity, scale=v("qk_w", 16 + tile0 + i), bias=v("qk_b", tile0 + i))\
                   .then_inc(conv3_in, 1)

            for i in range(8):
                conv3_block("m_q", i, mq, 0, S)
            for i in range(8):
                conv3_block("m_k", i, mk, 8, 512)
            b = gb("m_g")
            split_high(b + 2)
            done(act, b)
            act.wait_ge(x_kept, 16)
            act.activation(gsb[0:32, :], bank(b)[0:32, :], ACT.Identity, bias=v("mg_b")[0:32, :]).then_inc(mg_sb, 1)
            act.wait_ge(mg_sb, 1)
            act.sem_inc(bank_read[b % 4], 1)
            for i in range(8):
                split_high(gb("m_v", i) + 2)
                copy_tokens("m_v", i, mv, 4)
            act.wait_ge(mg_rows, 64)
            fg = gG[0:8, 1:4:2, :]
            step(act.activation(gtmp[0:8, :, :], fg, ACT.Abs))
            step(act.activation(gtmp[0:8, :, :], gtmp[0:8, :, :], ACT.Exp, scale=-1.0))
            act.activation(gtmp[0:8, :, :], gtmp[0:8, :, :], ACT.Ln, bias=1.0).then_inc(ln_ready, 1)
            act.wait_ge(conv3_done, 16)
            act.activation(mq, mq, ACT.Silu)
            act.activation(mk, mk, ACT.Silu).then_inc(silu_done, 1)
            for u in range(17):
                if u < 16:
                    e = u % 2
                    act.wait_ge(w_arg, u + 1)
                    if u >= 2:
                        act.wait_ge(fin_ready, u - 1)
                    last, half, cut = tiles_of(e)
                    act.activation(mW[e][:, 0:2, :], mW[e][:, 0:2, :], ACT.Exp)
                    act.activation(mW[e][:, last, :], mW[e][:, last, :], ACT.Exp)
                    act.activation(mW[e][:, half, cut], mW[e][:, half, cut], ACT.Exp)
                    act.activation(mfl[e], M[e][:, S:512], ACT.Exp).then_inc(w_ready, 1)
                if u >= 1:
                    act.wait_ge(nd_mm, u)
                    if u >= 2:
                        act.wait_ge(fin_ready, u - 1)
                    act.activation(mden, M[2 + (u - 1) % 2][:, S:512], ACT.Abs).then_inc(den_ready, 1)
            act.wait_ge(fin_ready, 16)
            for i in range(8):
                b = gb("m_o", i)
                split_high(b + 2)
                copy_out(b, mo[:, i, :], ACT.Sigmoid)
            for i in range(8):
                b = gb("d_q", i)
                split_high(b + 2)
                copy_out(b, dq[:, i, :])
            for i in range(8):
                b = gb("d_k", i)
                split_high(b + 2)
                copy_out(b, dk[:, i, :], cols=512)
            for i in range(8):
                split_high(gb("d_v", i) + 2)
                copy_tokens("d_v", i, dv, 4)
            square(nsq, ym)
            root(nrs)
            act.wait_ge(lam_mm, 1)
            act.activation(lame, M[3][:, 0:2], ACT.Exp).then_inc(lam_exp, 1)
            for u in range(17):
                if u < 16:
                    e = u % 2
                    act.wait_ge(dmax, u + 1)
                    if u >= 2:
                        act.wait_ge(dpd_ready, u - 1)
                    for c in range(2):
                        ins = act.activation(dE[e][:, c, :], M[c][:, :], ACT.Exp, bias=nm[e][:, c:c + 1], scale=0.125,
                                             accum_out=zz[e][:, c:c + 1])
                    ins.then_inc(dexp, 1)
                if u >= 1:
                    head, T = (u - 1) // 2, (u - 1) % 2
                    act.wait_ge(dpt_mm, u)
                    if u >= 3:
                        act.wait_ge(dpv_mm, u - 2)
                    act.activation(dPT[(u - 1) % 2].rearrange("p a b -> p (a b)"), M[2][:, :], ACT.Copy).then_inc(dpt_ready, 1)
                    act.wait_ge(dpv_mm, u)
                    act.activation(yd[:, head, P * T:P * T + P], M[3][:, 0:P], ACT.Copy).then_inc(dy_ready, 1)
            act.wait_ge(dy_ready, 16)
            square(dq, yd)
            root(dk[:, :, 0:S])
            high(opY2[:, 0], region(0, KT, S))
            rounds("w_out", plain_round("w_out", proj2))
            was_read(act, gb("w_out", 15))
            square(sq2, proj2)
            root(rstd[:, 0:S])
            act.wait_ge(x_ready, 3)
            square(sq2, xT)
            root(rstd[:, 0:S])
            high(opH[:, 0], hf2)
            for q in range(QUARTER):
                def pair(b, pos, tile, it, ahead):
                    for c in range(2):
                        ahead(c)
                        done(act, b + c, it)
                        if c == 0:
                            act.wait_ge(ffn_done, pos + 1)
                        w = vec[:, bass.ds(tile + VEC["ffn_w"] + 2 * FF2 + c * FF2, 1)]
                        bb = vec[:, bass.ds(tile + VEC["ffn_b"] + c * FF2, 1)]
                        act.activation(fv[:, buffer_of(b), c, :], bank(b + c)[:, 0:S], ACT.Identity, scale=w, bias=bb)\
                           .then_inc(taps_in, 1)
                    was_read(act, b, it)
                    act.activation(fv[:, buffer_of(b), 0, :], fv[:, buffer_of(b), 0, :], ACT.Silu).then_inc(gate_silu, 1)

                b0, t0 = gb(f"up2_{q}"), q * UP2
                with act.Fori(0, 5) as it:
                    for j in range(2):
                        pair(b0 + 2 * j, t0 + j + it * 2, t0 + j + it * 2, it,
                             lambda c, j=j: split_high(b0 + 2 * j + c + 2, it, 4))
                pair(b0 + 20, t0 + 10, t0 + 10, 0, lambda c: split_high(b0 + 20 + c + 2))
                if q == 0:
                    rounds("down2_0", plain_round("down2_0", down2))
                else:
                    def down_round(it, peeled, section=f"down2_{q}"):
                        b0, it, ahead = in_round(section, it, peeled)
                        for j in range(4):
                            ahead(j)
                    rounds(f"down2_{q}", down_round)
            was_read(act, gb("down2_3", 15))
            square(sq2, down2)
            root(rstd[:, 0:S])

        @block.tensor
        def _(pe):
            norms = [0]

            def begin(b, it):
                pe.wait_ge(hi_ready, b + 1 + it * 4)
                if b >= 4:
                    pe.wait_ge(bank_read[b % 4], b // 4 + it)

            def product(b, pieces, it=0, dn=0):
                begin(b, it)
                hi, lo = parts[:, b % 2, 0], parts[:, b % 2, 1]
                for out, opens, terms in pieces:
                    for i, (w, xh, xl) in enumerate(terms):
                        for x in (xh, xl):
                            l, r = w(hi, x)
                            ins = pe.matmul(out, l, r, start=(opens and i == 0 and x is xh), stop=False, skip_group_check=True)
                slot, uses = use(G_AT[b], it, dn)
                pe.wait_ge(taken[slot], uses + 1)
                for n, (out, opens, terms) in enumerate(pieces):
                    for i, (w, xh, xl) in enumerate(terms):
                        l, r = w(lo, xh)
                        ins = pe.matmul(out, l, r, start=False, stop=(i == len(terms) - 1), skip_group_check=True)
                        if n == 0 and i == 0:
                            ins.then_inc(hi_used, 1)
                ins.then_inc(block_done, 1)

            def features(out, op, k0=0, k1=KT, cols=slice(0, S), kw=0):
                return (out, True, [(lambda w, x, k=k: (w[:, kw + k - k0, :], x), op[:, 0, k, cols], op[:, 1, k, cols])
                                    for k in range(k0, k1)])

            def gemm_T(b, op, it=0, dn=0, cols=slice(0, S), kt=KT):
                product(b, [features(bank(b)[:, 0:cols.stop - cols.start], op, 0, kt, cols)], it, dn)

            def gemm_tokens(b, op, tiles):
                product(b, [(bank(b)[:, t * P:(t + 1) * P], t == 0,
                             [(lambda w, x, k=k: (x, w[:, k, :]), op[:, 0, k, t * P:(t + 1) * P], op[:, 1, k, t * P:(t + 1) * P])
                              for k in range(KT)]) for t in range(tiles)])

            def norm(src, n, cols=S):
                norms[0] += 1
                pe.wait_ge(sq_ready, norms[0])
                for k in range(n):
                    ins = pe.matmul(M[2][:, 0:cols], ones[:, :], src[:, k, :], start=(k == 0), stop=(k == n - 1))
                ins.then_inc(ms_ready, 1)

            def norm_heads(src):
                norms[0] += 1
                pe.wait_ge(sq_ready, norms[0])
                for h in range(8):
                    ins = pe.matmul(M[h // 2][:, (h % 2) * S:(h % 2 + 1) * S], ones[:, :], src[:, h, :], start=True, stop=True)
                ins.then_inc(ms_ready, 1)

            def ada(a, j, it, dn):
                slot, uses = use(A_AT[a], it, dn)
                pe.wait_ge(loaded[slot], 16 * (uses + 1))
                for k in range(KT):
                    g = k % 4
                    ins = pe.matmul(M[2][32 * g:32 * g + 32, 0:P], cpad[:, k, 32 - 2 * j:64 - 2 * j], raw[:, slot, k, :],
                                    start=(j == 0 and k < 4), stop=(j == 3 and k >= KT - 4), skip_group_check=True)
                ins.then_inc(taken[slot], 1)

            def turn(group, modrow):
                pe.wait_ge(row_ready, group + 1)
                pe.matmul(M[3][:, bass.ds(group * 8, 8)], modrow, sel[:, :], start=True, stop=True).then_inc(ada_cols, 1)

            pe.wait_ge(fills, 2)
            pe.wait_ge(boot, 112)
            pe.matmul(M[3][0:12, 0:BPITCH], relb[0:32, :], onehot[0:32, :], start=True, stop=True).then_inc(brow_mm, 1)
            norm(sq0, KT)
            pe.wait_ge(inv_ready, 1)
            pe.wait_ge(c_ready, 1)
            pe.wait_ge(brow_ready, 1)
            with pe.Fori(0, 8) as it:
                for j in range(4):
                    ada(j, j, it, 4)
                turn(it, modrow1)
            pe.wait_ge(h_ready, 1)
            for j in range(4):
                gemm_T(gb("c_a") + j, opH)
            with pe.Fori(0, 6) as it:
                for j in range(4):
                    gemm_T(gb("c_a") + 4 + j, opH, it, 4)
            late = [("a_i", i) for i in range(8)] + [("b_v", i) for i in range(6)] + [("b_k", i) for i in range(6)] \
                + [("b_q", i) for i in range(6)] + [("a_g", i) for i in range(8)]

            def level(s):
                quarter, L = s // 9, s % 9
                hs = slice(2 * quarter, 2 * quarter + 2)
                q_, k_ = (qq[:, hs, :], kk[:, hs, :]) if L == 0 else (qs, ks)
                pe.wait_ge(lvl_prep, s + 1)
                if s >= 2:
                    pe.wait_ge(lvl_read, s - 1)
                for h in range(2):
                    if L < 8:
                        for t in range(2):
                            i = 2 * h + t
                            ins = pe.matmul(M[s % 2][:, i * P:(i + 1) * P], k_[:, h, t * P:(t + 1) * P],
                                            q_[:, h, t * P:(t + 1) * P], start=True, stop=True)
                    else:
                        ins = pe.matmul(M[s % 2][:, h * P:(h + 1) * P], k_[:, h, 0:P], q_[:, h, P:S], start=True, stop=True)
                ins.then_inc(lvl_mm, 1)

            def outputs(quarter):
                pe.wait_ge(lvl_read, 9 * quarter + 9)
                if quarter == 0:
                    was_read(pe, gb("a_i", 7))
                    for i in range(4, 7):
                        was_read(pe, gb("a_i", i))
                else:
                    pe.wait_ge(o_copied, quarter)
                for h in range(2):
                    o = h * S
                    hd = slice((2 * quarter + h) * P, (2 * quarter + h + 1) * P)
                    pe.matmul(M[3][:, o:o + P], ii[:, 0, hd], attn[:, 2 * h, :], start=True, stop=True)
                    pe.matmul(M[3][:, o + P:o + S], ii[:, 0, hd], attx[:, h, :], start=True, stop=False)
                    ins = pe.matmul(M[3][:, o + P:o + S], ii[:, 1, hd], attn[:, 2 * h + 1, :], start=False, stop=True)
                ins.then_inc(o_mm, 1)

            for s in range(36):
                if s < len(late):
                    part, i = late[s]
                    if part in ("a_i", "b_v"):
                        gemm_tokens(gb(part, i), opH, 2)
                    else:
                        gemm_T(gb(part, i), opH)
                if s and s % 9 == 0:
                    outputs(s // 9 - 1)
                if s == 1:
                    pe.wait_ge(conv_y, 1)
                    for t in range(C_TILES):
                        ins = pe.matmul(M[2][:, S:512], ones[:, :], cy[:, t, :], start=(t == 0), stop=(t == C_TILES - 1))
                    ins.then_inc(mean_mm, 1)
                if s == 4:
                    norm(ca, C_TILES)
                level(s)
            outputs(3)
            norm_heads(fP)
            pe.wait_ge(ya_ready, 1)
            for i in range(4):
                was_read(pe, gb("a_g", 4 + i))
            for u in range(9):
                if u < 8:
                    T, slot = u // 4, u % 4
                    w = P * (T + 1)
                    if u >= 1:
                        pe.wait_ge(log_ready, u)
                    for g in range(3):
                        h = 4 * g + slot
                        po = 64 * (h % 2)
                        out = M[0][:, g * S:g * S + w] if g < 2 else M[1][:, 0:w]
                        ins = pe.matmul(out, bq[po:po + 64, h // 2, T * P:(T + 1) * P], bk[po:po + 64, h // 2, 0:w],
                                        start=True, stop=True)
                    ins.then_inc(qk_mm, 1)
                if u >= 1:
                    T, slot, e = (u - 1) // 4, (u - 1) % 4, (u - 1) % 2
                    pe.wait_ge(dg_ready, u)
                    if u >= 2:
                        pe.wait_ge(pt_ready, u - 1)
                    chunks = [(g, st) for g in range(3) for st in range(T + 1)]
                    for i, (g, st) in enumerate(chunks):
                        ins = pe.matmul(M[2 + i // 4][:, (i % 4) * P:(i % 4 + 1) * P], blog[e][:, g, st * P:(st + 1) * P],
                                        bdg[e], start=True, stop=True)
                    ins.then_inc(pt_mm, 1)
                    pe.wait_ge(pt_ready, u)
                    if u >= 3:
                        pe.wait_ge(yb_ready, u - 2)
                    po = 64 * (slot % 2)
                    for i, (g, st) in enumerate(chunks):
                        hc = (4 * g + slot) * 64
                        ins = pe.matmul(G[e][po:po + 64, 0:P], bv[:, st, hc:hc + 64], bpt[e][:, i, :],
                                        start=(i == 0), stop=(i == len(chunks) - 1))
                    ins.then_inc(pv_mm, 1)
            pe.wait_ge(y_ready, 1)
            with pe.Fori(0, 16) as it:
                b0, a0 = gb("merge"), FIRST["merge"][2]
                for j in range(3):
                    gemm_T(b0 + j, opH, it, 8)
                    ada(a0 + j, j, it, 8)
                ada(a0 + 3, 3, it, 8)
                b = b0 + 3
                pe.wait_ge(merged_part, it + 1)
                product(b, [features(M[0][:, 0:S], opY1, 0, 8), features(M[1][:, 0:S], opY1, 8, 10, kw=8),
                            features(bank(b)[:, 0:S], opY1, 10, 16, kw=10)], it, 8)
                turn(it + a0 // 4, modrow1)
            pe.wait_ge(h_ready, 2)

            def mixed(section, op, modrow):
                b0, a0 = gb(section), FIRST[section][2]
                with pe.Fori(0, 4) as it:
                    for j in range(3):
                        gemm_T(b0 + j, op, it, 8)
                        ada(a0 + j, j, it, 8)
                    ada(a0 + 3, 3, it, 8)
                    gemm_T(b0 + 3, op, it, 8)
                    turn(it + a0 // 4, modrow)

            pe.wait_ge(c_ready, 2)
            mixed("w_o", opG, modrow2)
            norm(sq1, KT)
            norm(sq1, KT)
            pe.wait_ge(h_ready, 3)
            for q in range(QUARTER):
                mixed(f"up1_{q}", opH, modrow2)
                pe.wait_ge(up_ready, 16 * (q + 1) + 2)
                if q == 0:
                    mixed("down1_0", opU1, modrow2)
                else:
                    with pe.Fori(0, 4) as it:
                        for j in range(4):
                            gemm_T(gb(f"down1_{q}") + j, opU1, it, 4)
            norm(sqd1, KT)
            norm(sqc, KT)
            norm(sqc, KT)
            pe.wait_ge(h_ready, 4)
            with pe.Fori(0, 2) as it:
                for j in range(4):
                    gemm_T(gb("m_q") + j, opW, it, 4, slice(S, 512))
            with pe.Fori(0, 2) as it:
                for j in range(4):
                    gemm_T(gb("m_k") + j, opW, it, 4, slice(0, 512))
            gemm_T(gb("m_g"), opW, cols=slice(0, 512))
            for i in range(8):
                gemm_tokens(gb("m_v", i), opW, 4)
            pe.wait_ge(rows_ready, 1)
            for d in range(2):
                for t in range(4):
                    ins = pe.matmul(M[1][:, d * 32 + t * 8:d * 32 + t * 8 + 8], gG[0:8, 2 * d, t * P:(t + 1) * P],
                                    ident[0:8, 0:8], start=True, stop=True)
            ins.then_inc(at_mm, 1)
            pe.wait_ge(silu_done, 1)
            pe.wait_ge(at_ready, 1)
            for i in range(4):
                was_read(pe, gb("m_v", 4 + i))
            for u in range(17):
                if u < 16:
                    h, d = u // 2, u % 2
                    if d == 0:
                        if h >= 2:
                            pe.wait_ge(ws_ready, 2 * (h - 1))
                        for t in range(4):
                            ins = pe.matmul(G[2 * (h % 2) + t // 2][:, (t % 2) * S:(t % 2 + 1) * S],
                                            mk[:, h, t * P:(t + 1) * P], mq[:, h, :], start=True, stop=True)
                        ins.then_inc(s_mm, 1)
                    if u >= 2:
                        pe.wait_ge(w_ready, u - 1)
                    pe.matmul(M[d][:, :], ident[0:8, h:h + 1].to_broadcast([8, P]),
                              grows[0:8, d, :, :].rearrange("p a b -> p (a b)"), start=True, stop=True).then_inc(bc_mm, 1)
                if u >= 1:
                    h, d = (u - 1) // 2, (u - 1) % 2
                    pe.wait_ge(ws_ready, u)
                    if u >= 3:
                        pe.wait_ge(fin_ready, u - 2)
                    last, half, cut = tiles_of(d)
                    for o, lhs in ((0, None), (S, ones[:, :])):
                        for t in (0, 1, last, half):
                            c = slice(0, S) if t != half else cut
                            ins = pe.matmul(M[2 + d][:, o + c.start:o + c.stop], mv[:, t, h * P:(h + 1) * P] if lhs is None else lhs,
                                            mW[d][:, t, c], start=(t == 0), stop=(t == half), skip_group_check=True)
                    ins.then_inc(nd_mm, 1)
            pe.wait_ge(fin_ready, 16)
            with pe.Fori(0, 4) as it:
                for j in range(4):
                    gemm_T(gb("m_o") + j, opW, it, 4, slice(S, 512))
            with pe.Fori(0, 2) as it:
                for j in range(4):
                    gemm_T(gb("d_k") + j, opW, it, 4, slice(0, 512))
            for i in range(8):
                gemm_tokens(gb("d_v", i), opW, 4)
            norm_heads(nsq)
            pe.wait_ge(tab_in, 48)
            for i in range(4):
                was_read(pe, gb("d_v", 4 + i))
            for c in range(8):
                if c >= 2:
                    pe.wait_ge(rope_done, c - 1)
                for j in range(2):
                    src = dq[:, 2 * c + j, :] if c < 4 else dk[:, 2 * (c - 4) + j, S:512]
                    ins = pe.matmul(G[c % 2][:, j * S:(j + 1) * S], rtab[:, 0:P], src, start=True, stop=True)
                ins.then_inc(rot_mm, 1)
            pe.wait_ge(lam_in, 1)
            pe.matmul(M[3][:, 0:2], ones[0:64, :], lamp[0:64, :], start=True, stop=True).then_inc(lam_mm, 1)
            pe.wait_ge(rope_done, 8)
            for u in range(17):
                if u < 16:
                    h, T = u // 2, u % 2
                    if u >= 1:
                        pe.wait_ge(dexp, u)
                    for c in range(2):
                        ins = pe.matmul(M[c][:, :], dq[64 * c:64 * c + 64, h, T * P:(T + 1) * P], dk[64 * c:64 * c + 64, h, :],
                                        start=True, stop=True)
                    ins.then_inc(dqk_mm, 1)
                if u >= 1:
                    h, T, e = (u - 1) // 2, (u - 1) % 2, (u - 1) % 2
                    pe.wait_ge(dpd_ready, u)
                    for t in range(4):
                        ins = pe.transpose(M[2][:, t * P:(t + 1) * P], dpd[e][:, t * P:(t + 1) * P], ident[:, :])
                    ins.then_inc(dpt_mm, 1)
                    pe.wait_ge(dpt_ready, u)
                    pe.wait_ge(lam_exp, 1)
                    if u >= 2:
                        pe.wait_ge(dy_ready, u - 1)
                    for t in range(4):
                        ins = pe.matmul(M[3][:, 0:P], dv[:, t, h * P:(h + 1) * P], dPT[e][:, t, :], start=(t == 0), stop=(t == 3))
                    ins.then_inc(dpv_mm, 1)
            norm_heads(dq)
            pe.wait_ge(h_ready, 5)
            with pe.Fori(0, 4) as it:
                for j in range(4):
                    gemm_T(gb("w_out") + j, opY2, it, 4)
            norm(sq2, KT)
            norm(sq2, KT)
            pe.wait_ge(h_ready, 6)
            for q in range(QUARTER):
                b0 = gb(f"up2_{q}")
                with pe.Fori(0, 5) as it:
                    for j in range(4):
                        gemm_T(b0 + j, opH, it, 4)
                for j in range(20, 22):
                    gemm_T(b0 + j, opH)
                pe.wait_ge(ffn_done, UP2 * (q + 1) + 2)
                with pe.Fori(0, 4) as it:
                    for j in range(4):
                        gemm_T(gb(f"down2_{q}") + j, opU2, it, 4, kt=UP2)
            norm(sq2, KT)

        @block.vector
        def _(dve):
            step = Chain(dve, dve_step)
            norms, splits = [0], [0]

            def split_low(b, it=0, dn=0):
                if b >= len(G_AT):
                    return
                slot, _ = use(G_AT[b])
                kt = kt_of(b)
                dve.wait_ge(hi_ready, b + 1 + it * 4)
                if b >= 2:
                    done(dve, b - 2, it)
                dve.tensor_tensor(parts[:, b % 2, 1, 0:kt, :], raw[:, slot, 0:kt, :], parts[:, b % 2, 0, 0:kt, :].bitcast(F32),
                                  ALU.subtract).then_inc(taken[slot], 1)

            def rounds(section, body):
                n = {name: t * p.count("G") // 4 for name, p, t in SECTIONS}[section]
                with dve.Fori(0, n - 1) as it:
                    body(it, 0)
                return n - 1

            def in_round(section, it, peeled):
                b0, dn = gb(section), steps_of(section)

                def ahead(j):
                    if peeled:
                        split_low(b0 + 4 * peeled + j + 2)
                    else:
                        split_low(b0 + j + 2, it, dn)
                return b0 + 4 * peeled, it, ahead

            def only_split(section):
                def body(it, peeled):
                    b0, it, ahead = in_round(section, it, peeled)
                    for j in range(4):
                        ahead(j)
                body(0, rounds(section, body))

            def low(dst, src, hi):
                splits[0] += 1
                dve.wait_ge(hh_ready, splits[0])
                dve.tensor_tensor(dst, src, hi.bitcast(F32), ALU.subtract).then_inc(h_ready, 1)

            def invert(t, scale):
                norms[0] += 1
                dve.wait_ge(ms_ready, norms[0])
                step(dve.tensor_scalar(t, M[2][:, 0:S], scale, EPS, ALU.mult, ALU.add))
                dve.reciprocal(t, t).then_inc(inv_ready, 1)
                dve.wait_ge(rstd_ready, norms[0])

            def invert_heads(t):
                norms[0] += 1
                dve.wait_ge(ms_ready, norms[0])
                for b in range(4):
                    last = dve.tensor_scalar(t[:, 2 * b:2 * b + 2, :], M[b][:, :].rearrange("p (a b) -> p a b", a=2),
                                             1.0 / P, EPS, ALU.mult, ALU.add)
                step(last)
                dve.reciprocal(t, t).then_inc(inv_ready, 1)
                dve.wait_ge(rstd_ready, norms[0])

            def over_tiles(t, n=KT):
                return t.unsqueeze(1).to_broadcast([P, n, t.shape[-1]])

            def modulate(dst, src, rs, mul, add):
                step(dve.tensor_tensor(dst, src, over_tiles(rs), ALU.mult))
                for k in range(KT):
                    last = dve.tensor_scalar(dst[:, k, :], dst[:, k, :], mul[:, k:k + 1], add[:, k:k + 1], ALU.mult, ALU.add)
                last.then_inc(hf_ready, 1)

            def residual(t, mul):
                step(dve.tensor_tensor(t, t, over_tiles(rstd[:, 0:S]), ALU.mult))
                for k in range(KT):
                    last = dve.scalar_tensor_tensor(xT[:, k, :], t[:, k, :], mul[:, k:k + 1], xT[:, k, :], ALU.mult, ALU.add)
                last.then_inc(x_ready, 1)

            dve.wait_ge(brow_mm, 1)
            dve.wait_ge(boot, 112)
            dve.tensor_tensor(brow[0:12, :], M[3][0:12, 0:BPITCH], bmask[0:12, :], ALU.add).then_inc(brow_ready, 1)
            step(dve.tensor_copy(lvl_mask[:, :, :], lvl_f))
            dve.wait_ge(x_in, 16)
            invert(rstd[:, 0:S], 1.0 / D)
            step(dve.tensor_tensor(hf0, xT, over_tiles(rstd[:, 0:S]), ALU.mult))
            lg = v("lb", 0, 8)
            step(dve.tensor_tensor(sm_e, lg, lg, ALU.subtract))
            step(dve.tensor_scalar(lbc, sm_e, 0.0, TINY, ALU.max, ALU.add))
            step(dve.tensor_scalar(lb1, sm_e, 0.0, None, ALU.max))
            step(dve.tensor_scalar(lb1, lb1, -1.0, 1.0, ALU.mult, ALU.add))
            split_low(0)
            split_low(1)
            dve.wait_ge(ada_cols, 8)
            step(dve.tensor_tensor(mod1[:, 0:32], M[3][:, 0:64:2], v("b_ada", 0, 32), ALU.add))
            step(dve.scalar_tensor_tensor(amul, mod1[:, 16:32], 1.0, v("mix_pre", 0, 16), ALU.add, ALU.mult))
            for k in range(KT):
                last = dve.tensor_scalar(hf0[:, k, :], hf0[:, k, :], amul[:, k:k + 1], mod1[:, k:k + 1], ALU.mult, ALU.add)
            last.then_inc(hf_ready, 1)
            low(opH[:, 1], hf0, opH[:, 0])
            for b in range(gb("c_a"), gb("c_g", 6)):
                split_low(b + 2)
            for i in range(6):
                was_read(dve, gb("c_a", i))
                was_read(dve, gb("c_g", i))
            dve.wait_ge(brow_out, 16)
            step(dve.memset(upad[:, :, 0:30], 0.0))
            step(dve.tensor_tensor(upad[:, :, 30:30 + S], ca, cy, ALU.mult))
            taps = 0
            for i in range(16):
                split_low(gb("a_f") + i + 2)
                for _ in range(12 if i < 15 else 6):
                    t, tap = 2 * (taps // (2 * C_TAPS)) + taps % 2, taps % (2 * C_TAPS) // 2
                    w = vec[:, VEC["conv_w"] + t * C_TAPS + tap:VEC["conv_w"] + t * C_TAPS + tap + 1]
                    if tap == 0:
                        ins = dve.tensor_scalar(cy[:, t, :], upad[:, t, 0:S], w, v("conv_b", t), ALU.mult, ALU.add)
                    else:
                        dve.wait_ge(conv_tap, taps - 1)
                        ins = dve.scalar_tensor_tensor(cy[:, t, :], upad[:, t, tap:tap + S], w, cy[:, t, :], ALU.mult, ALU.add)
                    ins.then_inc(conv_tap, 1)
                    taps += 1
            assert taps == C_TILES * C_TAPS
            dve.wait_ge(conv_tap, taps)
            dve.sem_inc(conv_y, 1)
            for i in range(8):
                was_read(dve, gb("a_f", i))
                was_read(dve, gb("a_q", i))
            for h in range(8):
                dve.tensor_scalar(fP[:, h, :], fP[:, h, :], lb1[:, h:h + 1], lbc[:, h:h + 1], ALU.mult, ALU.add)
                last = dve.tensor_scalar(kk[:, h, :], kk[:, h, :], lb1[:, h:h + 1], None, ALU.mult)
            step(last)
            for s in range(36):
                quarter, L = s // 9, s % 9
                hs = slice(2 * quarter, 2 * quarter + 2)
                f_, q_, k_ = fP[:, hs, :], qq[:, hs, :], kk[:, hs, :]
                if L == 0:
                    dve.memset(suf, 1.0).then_inc(lvl_prep, 1)
                    dve.wait_ge(lvl_prep, s + 1)
                else:
                    dve.wait_ge(lvl_mm, s)
                    dve.tensor_tensor(qs, q_, f_, ALU.mult)
                    dve.tensor_tensor(ks, k_, suf, ALU.mult).then_inc(lvl_prep, 1)
                    dve.wait_ge(lvl_prep, s + 1)
                    if L < 8:
                        w = 1 << (L - 1)
                        fv_ = f_.rearrange("p h (b two w) -> p (h b) two w", two=2, w=w)
                        sv_ = suf.rearrange("p h (b two w) -> p (h b) two w", two=2, w=w)
                        nb = 2 * S // (2 * w)
                        step(dve.tensor_tensor(sv_[:, :, 0, :], sv_[:, :, 0, :],
                                               fv_[:, :, 1, w - 1:w].to_broadcast([P, nb, w]), ALU.mult))
                        step(dve.tensor_tensor(fv_[:, :, 1, :], fv_[:, :, 1, :],
                                               fv_[:, :, 0, w - 1:w].to_broadcast([P, nb, w]), ALU.mult))
                if s == 2:
                    dve.wait_ge(mean_mm, 1)
                    step(dve.tensor_scalar(rstd[:, S:512], M[2][:, S:512], 1.0 / (C_TILES * P), None, ALU.mult))
                    dve.tensor_tensor(cy, cy, over_tiles(rstd[:, S:512], C_TILES), ALU.subtract).then_inc(conv_cent, 1)
                if s == 5:
                    invert(rstd[:, 0:S], 1.0 / (C_TILES * P))
                    dve.wait_ge(conv_cent, 1)
                    dve.tensor_tensor(cy, cy, over_tiles(rstd[:, 0:S], C_TILES), ALU.mult).then_inc(yc_in, 1)
                if s < 34:
                    split_low(gb("a_i") + s + 2)
                dve.wait_ge(lvl_mm, s + 1)
                if s % 9 == 0 and s:
                    dve.wait_ge(o_mm, quarter)
                bank4 = M[s % 2][:, :].rearrange("p (a b) -> p a b", a=4)
                if L == 0:
                    last = dve.tensor_tensor(attn, bank4, over_tiles(ident[:, :], 4), ALU.mult)
                elif L < 8:
                    last = dve.copy_predicated(attn, lvl_mask[:, L:L + 1, :].to_broadcast([P, 4, P]), bank4)
                else:
                    last = dve.tensor_copy(attx, bank4[:, 0:2, :])
                last.then_inc(lvl_read, 1)
                dve.wait_ge(lvl_read, s + 1)
            for i in range(8):
                was_read(dve, gb("a_g", i))
            invert_heads(kk)
            step(dve.tensor_tensor(qq, qq, kk, ALU.mult))
            dve.scalar_tensor_tensor(og, qq, v("hgrn_w"), og, ALU.mult, ALU.mult).then_inc(ya_ready, 1)
            dve.wait_ge(bias_in, 16)
            for u in range(9):
                if u < 8:
                    T, slot, e = u // 4, u % 4, u % 2
                    w = P * (T + 1)
                    b0 = 0 if T else P
                    dve.wait_ge(qk_mm, u + 1)
                    if u >= 2:
                        dve.wait_ge(pt_mm, u - 1)
                    psum01 = M[0][:, :].rearrange("p (a b) -> p a b", a=2)
                    dve.scalar_tensor_tensor(blog[e][:, 0:2, 0:w], psum01[:, :, 0:w], 0.125,
                                             bias[:, slot:slot + 5:4, b0:b0 + w], ALU.mult, ALU.add)
                    step(dve.scalar_tensor_tensor(blog[e][:, 2, 0:w], M[1][:, 0:w], 0.125, bias[:, 8 + slot, b0:b0 + w],
                                                  ALU.mult, ALU.add))
                    step(dve.tensor_reduce(nm[e][:, 0:1], blog[e][:, :, 0:w], mybir.AxisListType.XY, ALU.max))
                    dve.tensor_scalar(nm[e][:, 0:1], nm[e][:, 0:1], -1.0, None, ALU.mult).then_inc(log_ready, 1)
                if u >= 1:
                    e, T = (u - 1) % 2, (u - 1) // 4
                    dve.wait_ge(exp_ready, u)
                    step(dve.reciprocal(rz[e][:, 0:1], zz[e][:, 0:1]))
                    dve.tensor_scalar(bdg[e], ident[:, :], rz[e][:, 0:1], None, ALU.mult).then_inc(dg_ready, 1)
                    nch = 3 * (T + 1)
                    dve.wait_ge(pt_mm, u)
                    if u >= 3:
                        dve.wait_ge(pv_mm, u - 2)
                    last = dve.tensor_copy(bpt[e][:, 0:min(nch, 4), :],
                                           M[2][:, 0:min(nch, 4) * P].rearrange("p (a b) -> p a b", b=P))
                    if nch > 4:
                        last = dve.tensor_copy(bpt[e][:, 4:nch, :], M[3][:, 0:(nch - 4) * P].rearrange("p (a b) -> p a b", b=P))
                    last.then_inc(pt_ready, 1)
            dve.wait_ge(y_hi, 1)
            for k0, k1, t in ((0, 8, og), (8, 10, yb), (10, 16, yc)):
                last = dve.tensor_tensor(opY1[:, 1, k0:k1, :], t, opY1[:, 0, k0:k1, :].bitcast(F32), ALU.subtract)
            last.then_inc(y_ready, 1)

            dve.wait_ge(y_ready, 1)
            dve.sem_inc(merged_part, 1)

            def merge_round(it, peeled):
                b0, it, ahead = in_round("merge", it, peeled)
                for j in range(3):
                    ahead(j)
                for g in range(3):
                    was_read(dve, b0 + g, it)
                done(dve, b0 + 3, it)
                g_ = gates[:, 0]
                t = bass.ds(it + peeled, 1)
                dve.tensor_tensor(mtmp[:, 0, :], M[0][:, 0:S], g_[:, 0, :], ALU.mult)
                step(dve.tensor_tensor(mtmp[:, 1, :], M[1][:, 0:S], g_[:, 1, :], ALU.mult))
                step(dve.tensor_tensor(mtmp[:, 0, :], mtmp[:, 0, :], mtmp[:, 1, :], ALU.add))
                step(dve.tensor_tensor(mtmp[:, 1, :], bank(b0 + 3)[:, 0:S], g_[:, 2, :], ALU.mult))
                dve.sem_inc(bank_read[(b0 + 3) % 4], 1)
                dve.sem_inc(merged_part, 1)
                step(dve.tensor_tensor(mfp[:, 0, :], mtmp[:, 0, :], mtmp[:, 1, :], ALU.add))
                gh, gl = (opG[:, p, t, :].rearrange("p a b -> p (a b)") for p in range(2))
                step(dve.tensor_copy(gh, mfp[:, 0, :]))
                step(dve.tensor_tensor(gl, mfp[:, 0, :], gh.bitcast(F32), ALU.subtract))
                ahead(3)

            def counted(section, body, per):
                n = {name: t * p.count("G") // 4 for name, p, t in SECTIONS}[section]
                with dve.Fori(0, n - 1) as it:
                    step.offset = it * per
                    body(it, 0)
                step.n += per * (n - 2)
                step.offset = 0
                body(0, n - 1)

            counted("merge", merge_round, 6)
            dve.wait_ge(ada_cols, 24)
            step(dve.tensor_tensor(mod1[:, 32:96], M[3][:, 64:192:2], v("b_ada", 32, 64), ALU.add))
            dve.sem_inc(h_ready, 1)
            only_split("w_o")
            invert(rstd[:, 0:S], 1.0 / D)
            step(dve.tensor_tensor(gmul, mod1[:, 32:48], v("mix_post", 0, 16), ALU.mult))
            residual(proj1, gmul)
            invert(rstd[:, 0:S], 1.0 / D)
            step(dve.scalar_tensor_tensor(amul, mod1[:, 64:80], 1.0, v("mlp_pre", 0, 16), ALU.add, ALU.mult))
            modulate(hf1, xT, rstd[:, 0:S], amul, mod1[:, 48:64])
            low(opH[:, 1], hf1, opH[:, 0])
            dve.wait_ge(h_ready, 3)
            dve.sem_inc(up_ready, 2)

            def add_round(section, acc):
                def body(it, peeled):
                    b0, it, ahead = in_round(section, it, peeled)
                    for j in range(4):
                        done(dve, b0 + j, it)
                        t = acc[:, bass.ds(j + it * 4 + 4 * peeled, 1), :].rearrange("p a b -> p (a b)")
                        dve.tensor_tensor(t, bank(b0 + j)[:, 0:S], t, ALU.add).then_inc(bank_read[(b0 + j) % 4], 1)
                        ahead(j)
                body(0, rounds(section, body))

            for q in range(QUARTER):
                def up_round(it, peeled, section=f"up1_{q}"):
                    b0, it, ahead = in_round(section, it, peeled)
                    for j in range(4):
                        was_read(dve, b0 + j, it)
                        t = bass.ds(j + it * 4 + 4 * peeled, 1)
                        uh, ul = (opU1[:, p, t, :].rearrange("p a b -> p (a b)") for p in range(2))
                        r, r2 = ut[:, j % 2, 0, :], ut[:, j % 2, 1, :]
                        dve.tensor_tensor(r2, r, r, ALU.mult)
                        step(dve.tensor_tensor(uh, r, r, ALU.mult))
                        dve.tensor_tensor(ul, r2, uh.bitcast(F32), ALU.subtract).then_inc(up_ready, 1)
                        ahead(j)
                counted(f"up1_{q}", up_round, 4)
                if q == 0:
                    only_split("down1_0")
                else:
                    add_round(f"down1_{q}", down1)
            invert(rstd[:, 0:S], 1.0 / D)
            step(dve.tensor_tensor(gmul, mod1[:, 80:96], v("mlp_post", 0, 16), ALU.mult))
            residual(down1, gmul)
            dve.wait_ge(ada_cols, 48)
            for r in range(2):
                last = dve.tensor_tensor(mod2[:, r, :], M[3][:, 192 + r:384:2], v("b_mod", 0, 96), ALU.add)
            step(last)
            dve.scalar_tensor_tensor(amul, mod2[:, 0, 16:32], 1.0, v("g_pre_mix", 0, 16), ALU.add, ALU.mult)
            step(dve.scalar_tensor_tensor(cmul, mod2[:, 1, 16:32], 1.0, v("g_pre_mix", 0, 16), ALU.add, ALU.mult))
            invert(rstd[:, 0:S], 1.0 / D)
            modulate(hfc, hfc, rstd[:, 0:S], cmul, mod2[:, 1, 0:16])
            splits[0] += 1
            dve.wait_ge(hh_ready, splits[0])
            step(dve.tensor_tensor(opW[:, 1, :, 0:S], hfc, opW[:, 0, :, 0:S].bitcast(F32), ALU.subtract))
            invert(rstd[:, S:512], 1.0 / D)
            modulate(hfx, xT, rstd[:, S:512], amul, mod2[:, 0, 0:16])
            low(opW[:, 1, :, S:512], hfx, opW[:, 0, :, S:512])

            def outer_taps(part, i, dst, tile0, wide, seen):
                b = gb(part, i)
                t = tile0 + i
                src, y = bank(b)[:, 0:512 if wide else S], dst[:, i, :]
                if wide:
                    src, y = (a.rearrange("p (s t) -> p s t", s=2) for a in (src, y))
                else:
                    src, y = src.unsqueeze(1), y.unsqueeze(1)
                dve.wait_ge(conv3_in, seen + 1)
                step(dve.scalar_tensor_tensor(y[:, :, 1:S], src[:, :, 0:S - 1], v("qk_w", t), y[:, :, 1:S], ALU.mult, ALU.add))
                dve.scalar_tensor_tensor(y[:, :, 0:S - 1], src[:, :, 1:S], v("qk_w", 32 + t), y[:, :, 0:S - 1],
                                         ALU.mult, ALU.add).then_inc(conv3_done, 1)
                dve.wait_ge(conv3_done, seen + 1)
                dve.sem_inc(bank_read[b % 4], 1)
                split_low(b + 2)

            for i in range(8):
                outer_taps("m_q", i, mq, 0, False, i)
            for i in range(8):
                outer_taps("m_k", i, mk, 8, True, 8 + i)
            for i in range(9):
                split_low(gb("m_g") + i + 2)
            dve.wait_ge(ln_ready, 1)
            one = ones[0:8, 0:1].to_broadcast([8, 512])
            one_s = ones[0:8, 0:1].to_broadcast([8, S])
            g8 = gG[0:8]
            step(dve.scalar_tensor_tensor(g8[:, 1:4:2, :], g8[:, 1:4:2, :], 0.0, gtmp[0:8, :, :], ALU.min, ALU.subtract))
            B8, M8 = gB[0:8], gM[0:8]
            last_c = slice(0, 1)
            dve.tensor_tensor_scan(B8[:, 0, :], one, g8[:, 1, :], 0.0, ALU.mult, ALU.add)
            step(dve.tensor_tensor_scan(B8[:, 1, 0:S][:, ::-1], one_s, g8[:, 3, 0:S][:, ::-1], 0.0, ALU.mult, ALU.add))
            step(dve.tensor_tensor_scan(B8[:, 1, S:512][:, ::-1], one_s, g8[:, 3, S:512][:, ::-1], B8[:, 1, last_c],
                                        ALU.mult, ALU.add))
            step(dve.tensor_tensor(g8[:, 0:4:2, :], g8[:, 0:4:2, :], B8[:, :, :], ALU.subtract))
            dve.tensor_tensor_scan(M8[:, 0, :], one, g8[:, 0, :], 0.0, ALU.mult, ALU.max)
            step(dve.tensor_tensor_scan(M8[:, 1, 0:S][:, ::-1], one_s, g8[:, 2, 0:S][:, ::-1], 0.0, ALU.mult, ALU.max))
            step(dve.tensor_tensor_scan(M8[:, 1, S:512][:, ::-1], one_s, g8[:, 2, S:512][:, ::-1], M8[:, 1, last_c],
                                        ALU.mult, ALU.max))
            r8 = grows[0:8]
            dve.tensor_scalar(r8[:, :, 0, :], M8[:, :, S:512], -1.0, None, ALU.mult)
            dve.scalar_tensor_tensor(r8[:, :, 1, :], B8[:, :, S:512], -1.0, M8[:, :, S:512], ALU.mult, ALU.subtract)\
               .then_inc(rows_ready, 1)
            dve.wait_ge(at_mm, 1)
            step(dve.tensor_copy(aT.rearrange("p a b c -> p (a b c)"), M[1][:, 0:64]))
            dve.sem_inc(at_ready, 1)
            dve.wait_ge(tab_in, 32)
            scale = float(P) ** -0.5
            for u in range(18):
                if u < 16:
                    h, d = u // 2, u % 2
                    dve.wait_ge(bc_mm, u + 1)
                    if u >= 2:
                        dve.wait_ge(nd_mm, u - 1)
                    half = tiles_of(d)[1]
                    for t in range(2):
                        dve.tensor_scalar(mW[d][:, t, :], M[d][:, 0:S], aT[:, d, t, h:h + 1], 0.0, ALU.add, ALU.min)
                    for t in (2, 3):
                        a = aT[:, d, t, h:h + 1]
                        c = slice((t - 2) * P, (t - 1) * P)
                        last = dve.scalar_tensor_tensor(mW[d][:, t, c], M[d][:, c], a, tri[d], ALU.add, ALU.min)
                        if t != half:
                            c = slice(P, S) if d == 0 else slice(0, P)
                            last = dve.tensor_scalar(mW[d][:, t, c], M[d][:, c], a, 0.0, ALU.add, ALU.min)
                    last.then_inc(w_arg, 1)
                if 1 <= u <= 16:
                    h, d = (u - 1) // 2, (u - 1) % 2
                    dve.wait_ge(w_ready, u)
                    dve.wait_ge(s_mm, h + 1)
                    whole, half, cut = tiles_of(d)
                    for t0, t1, c in ((0, 2, slice(0, S)), (whole, whole + 1, slice(0, S)), (half, half + 1, cut)):
                        sc = G[2 * (h % 2) + t0 // 2][:, :].rearrange("p (a b) -> p a b", a=2)[:, t0 % 2:t0 % 2 + t1 - t0, c]
                        last = dve.scalar_tensor_tensor(mW[d][:, t0:t1, c], sc, scale, mW[d][:, t0:t1, c], ALU.mult, ALU.mult)
                    last.then_inc(ws_ready, 1)
                if u >= 2:
                    h, d = (u - 2) // 2, (u - 2) % 2
                    dve.wait_ge(den_ready, u - 1)
                    step(dve.tensor_tensor(mfl[d], mfl[d], mden, ALU.max))
                    step(dve.reciprocal(mfl[d], mfl[d]))
                    num = M[2 + d][:, 0:S]
                    if d == 0:
                        dve.tensor_tensor(ym[:, h, :], num, mfl[d], ALU.mult).then_inc(fin_ready, 1)
                    else:
                        step(dve.tensor_tensor(mfl[d], num, mfl[d], ALU.mult))
                        dve.wait_ge(fin_ready, u - 2)
                        dve.tensor_tensor(ym[:, h, :], ym[:, h, :], mfl[d], ALU.add).then_inc(fin_ready, 1)
            for b in range(gb("m_o"), gb("d_v", 8)):
                split_low(b + 2)
            for i in range(8):
                was_read(dve, gb("m_o", i))
            invert_heads(nrs)
            step(dve.tensor_tensor(ym, ym, nrs, ALU.mult))
            for h in range(8):
                last = dve.scalar_tensor_tensor(ym[:, h, :], ym[:, h, :], v("g_mlstm", h), mo[:, h, :], ALU.mult, ALU.mult)
            last.then_inc(ym_ready, 1)
            dve.wait_ge(ym_ready, 1)
            lv = v("lam", 0, 4)[0:64, :]
            dve.tensor_tensor(lamp[0:64, :], lv[:, 0:4:2], lv[:, 1:4:2], ALU.mult).then_inc(lam_in, 1)
            for i in range(8):
                was_read(dve, gb("d_q", i))
                was_read(dve, gb("d_k", i))
            dve.wait_ge(tab_in, 48)
            cos = rtab[:, P:P + S].unsqueeze(1).to_broadcast([P, 2, S])
            sin = rtab[:, P + S:P + 2 * S].unsqueeze(1).to_broadcast([P, 2, S])
            for c in range(8):
                dve.wait_ge(rot_mm, c + 1)
                t = dq[:, 2 * c:2 * c + 2, :] if c < 4 else dk[:, 2 * (c - 4):2 * (c - 4) + 2, S:512]
                dve.tensor_tensor(rtmp, G[c % 2][:, :].rearrange("p (a b) -> p a b", a=2), sin, ALU.mult)
                step(dve.tensor_tensor(t, t, cos, ALU.mult))
                dve.tensor_tensor(t, t, rtmp, ALU.add).then_inc(rope_done, 1)
                dve.wait_ge(rope_done, c + 1)
            dve.wait_ge(lam_exp, 1)
            step(dve.tensor_tensor(lamn, lame[:, 1:2], lame[:, 0:1], ALU.subtract))
            step(dve.tensor_scalar(lamn, lamn, -LAM_INIT, None, ALU.add))
            for u in range(17):
                if u < 16:
                    e = u % 2
                    dve.wait_ge(dqk_mm, u + 1)
                    dve.tensor_reduce(nm[e][:, 0:1], M[0][:, :], AX_X, ALU.max)
                    step(dve.tensor_reduce(nm[e][:, 1:2], M[1][:, :], AX_X, ALU.max))
                    dve.tensor_scalar(nm[e], nm[e], -0.125, None, ALU.mult).then_inc(dmax, 1)
                if u >= 1:
                    e = (u - 1) % 2
                    dve.wait_ge(dexp, u)
                    step(dve.reciprocal(rz[e], zz[e]))
                    step(dve.tensor_tensor(rz[e][:, 1:2], rz[e][:, 1:2], lamn, ALU.mult))
                    if u >= 3:
                        dve.wait_ge(dpt_mm, u - 2)
                    step(dve.tensor_scalar(dpd[e], dE[e][:, 0, :], rz[e][:, 0:1], None, ALU.mult))
                    dve.scalar_tensor_tensor(dpd[e], dE[e][:, 1, :], rz[e][:, 1:2], dpd[e], ALU.mult, ALU.add)\
                       .then_inc(dpd_ready, 1)
            rh = dk[:, :, 0:S]
            invert_heads(rh)
            step(dve.tensor_tensor(yd, yd, rh, ALU.mult))
            dve.tensor_scalar(yd, yd, v("g_diff"), 1.0 - LAM_INIT, ALU.mult, ALU.mult).then_inc(hf_ready, 1)
            low(opY2[:, 1], region(0, KT, S), opY2[:, 0])
            only_split("w_out")
            invert(rstd[:, 0:S], 1.0 / D)
            step(dve.tensor_tensor(gmul, mod2[:, 0, 32:48], v("g_post_mix", 0, 16), ALU.mult))
            dve.wait_ge(x_back, 16)
            residual(proj2, gmul)
            invert(rstd[:, 0:S], 1.0 / D)
            step(dve.scalar_tensor_tensor(amul, mod2[:, 0, 64:80], 1.0, v("g_pre_ffn", 0, 16), ALU.add, ALU.mult))
            modulate(hf2, xT, rstd[:, 0:S], amul, mod2[:, 0, 48:64])
            low(opH[:, 1], hf2, opH[:, 0])
            dve.wait_ge(h_ready, 6)
            dve.sem_inc(ffn_done, 2)
            for q in range(QUARTER):
                def pair(b, pos, tile, local, it, ahead):
                    for c in range(2):
                        dve.wait_ge(taps_in, pos * 2 + c + 1)
                        src, y = bank(b + c)[:, 0:S], fv[:, buffer_of(b), c, :]
                        w0, w2 = (vec[:, bass.ds(tile + VEC["ffn_w"] + side * 4 * FF2 + c * FF2, 1)] for side in range(2))
                        step(dve.scalar_tensor_tensor(y[:, 1:S], src[:, 0:S - 1], w0, y[:, 1:S], ALU.mult, ALU.add))
                        step(dve.scalar_tensor_tensor(y[:, 0:S - 1], src[:, 1:S], w2, y[:, 0:S - 1], ALU.mult, ALU.add))
                        dve.sem_inc(bank_read[(b + c) % 4], 1)
                        ahead(c)
                    dve.wait_ge(gate_silu, pos + 1)
                    e = buffer_of(b)
                    step(dve.tensor_tensor(ftm[:, e, :], fv[:, e, 0, :], fv[:, e, 1, :], ALU.mult))
                    uh, ul = (opU2[:, p, bass.ds(local, 1), :].rearrange("p a b -> p (a b)") for p in range(2))
                    step(dve.tensor_copy(uh, ftm[:, e, :]))
                    dve.tensor_tensor(ul, ftm[:, e, :], uh.bitcast(F32), ALU.subtract).then_inc(ffn_done, 1)

                b0, t0 = gb(f"up2_{q}"), q * UP2
                with dve.Fori(0, 5) as it:
                    step.offset = it * 12
                    for j in range(2):
                        pair(b0 + 2 * j, t0 + j + it * 2, t0 + j + it * 2, j + it * 2, it,
                             lambda c, j=j: split_low(b0 + 2 * j + c + 2, it, 4))
                step.n += 12 * 4
                step.offset = 0
                pair(b0 + 20, t0 + 10, t0 + 10, 10, 0, lambda c: split_low(b0 + 20 + c + 2))
                if q == 0:
                    only_split("down2_0")
                else:
                    add_round(f"down2_{q}", down2)
            invert(rstd[:, 0:S], 1.0 / D)
            step(dve.tensor_tensor(gmul, mod2[:, 0, 80:96], v("g_post_ffn", 0, 16), ALU.mult))
            residual(down2, gmul)


def constant_arrays():
    import math
    import numpy as np

    f = np.float32
    consts = np.zeros((P, NCONST), f)
    freqs, grid_w, base = 16, 64, 10000.0
    inv = (f(base) ** (-np.arange(freqs, dtype=f) / f(freqs))).astype(f)
    tok = np.arange(S)
    axis = np.stack([(tok // grid_w).astype(f), (tok % grid_w).astype(f)])
    perm = np.zeros((P, P), f)
    for p in range(P):
        ax, half, fr = (p // 32) % 2, (p // 16) % 2, p % 16
        ang = (axis[ax] * inv[fr]).astype(f)
        consts[p, CONST["cos"]:CONST["cos"] + S] = np.cos(ang)
        consts[p, CONST["sin"]:CONST["sin"] + S] = np.sin(ang)
        perm[p + 16 if half == 0 else p - 16, p] = -1.0 if half == 0 else 1.0
    consts[:, 0:P] = perm
    p, j = np.arange(P)[:, None], np.arange(P)[None, :]
    consts[:, CONST["tri_f"]:CONST["tri_f"] + P] = np.where(j >= p, 0.0, MASK_VALUE)
    consts[:, CONST["tri_b"]:CONST["tri_b"] + P] = np.where(j <= p, 0.0, MASK_VALUE)
    exact, buckets, far = 16, 32, 2048
    for i in range(BROW):
        d = 255 - i
        if d >= 0:
            if d < exact:
                b = d
            else:
                large = exact + int(np.float32(np.log(f(d) / f(exact)) / f(math.log(far / exact))) * f(buckets - exact))
                b = min(max(large, exact), buckets - 1)
            consts[b, CONST["onehot"] + i] = 1.0
    for g, (window, dil) in enumerate(((128, 1), (512, 4), (2048, 16))):
        for i in range(BPITCH):
            d = 255 - i
            ok = 0 <= d <= window and d % dil == 0
            consts[4 * g:4 * g + 4, CONST["bmask"] + i] = 0.0 if ok else MASK_VALUE
    s, t = np.arange(P)[:, None], np.arange(P)[None, :]
    lvl = np.zeros((P, 8, P), f)
    lvl[:, 0] = s == t
    for n in range(1, 8):
        w = 1 << (n - 1)
        lvl[:, n] = (s // (2 * w) == t // (2 * w)) & ((s // w) % 2 == 0) & ((t // w) % 2 == 1)
    ident = np.zeros((P, P + 8), f)
    ident[:, 0:P] = np.eye(P, dtype=f)
    for r in range(8):
        ident[r::32, P + r] = 1.0
    return consts, lvl, ident


def kernel(**inputs):
    import numpy as _np
    import concourse.bacc as _bacc
    from concourse.bass_utils import run_bass_kernel_spmd as _run

    a = {k: _np.asarray(x) for k, x in inputs.items()}

    def columns(x):
        return _np.ascontiguousarray(x.reshape(-1, P).T)

    def blocks(w):
        k, n = w.shape
        return w.reshape(k // P, P, n // P, P).transpose(2, 1, 0, 3)

    w_in, w_in_2 = blocks(a["w_in"][0]), a["w_in_2"][0]
    cuts = dict(a_q=(0, 8), a_f=(8, 16), a_i=(16, 24), a_g=(24, 32), b_q=(32, 38), b_k=(38, 44), b_v=(44, 50),
                c_a=(50, 56), c_g=(56, 62))
    parts = {k: w_in[i:j] for k, (i, j) in cuts.items()}
    gate = blocks(a["w_gate"][0]).reshape(3, KT, P, KT, P)
    branches = blocks(_np.concatenate([a["w_a_out"][0], a["w_b_out"][0], a["w_c_out"][0]]))
    parts["merge"] = [x for j in range(KT) for x in (gate[0, j], gate[1, j], gate[2, j], branches[j])]
    parts["w_o"], parts["w_out"] = blocks(a["w_o"][0]), blocks(a["w_out_2"][0])
    mg = 4 * 1024
    for name, at in (("m_q", 0), ("m_k", 1024), ("m_v", 2048), ("m_o", 3072), ("d_q", mg + 32), ("d_k", mg + 1056), ("d_v", mg + 2080)):
        parts[name] = blocks(w_in_2[:, at:at + 1024])
    parts["m_g"] = blocks(_np.pad(w_in_2[:, mg:mg + 32], ((0, 0), (0, P - 32))))
    up1, up2 = blocks(a["w_up"][0]), blocks(a["w_up_2"][0])
    for q in range(QUARTER):
        n1, n2 = FF1 // QUARTER, UP2
        parts[f"up1_{q}"] = up1[q * n1:(q + 1) * n1]
        parts[f"down1_{q}"] = blocks(a["w_down"][0][q * n1 * P:(q + 1) * n1 * P])
        parts[f"up2_{q}"] = [x for j in range(q * n2, (q + 1) * n2) for x in (up2[j], up2[FF2 + j])]
        parts[f"down2_{q}"] = blocks(a["w_down_2"][0][q * n2 * P:(q + 1) * n2 * P])
    stream = _np.zeros((N_STREAM, P, KT, P), _np.float32)
    g_blocks = [x for name, pattern, _ in SECTIONS if "G" in pattern for x in parts[name]]
    a_blocks = [x for w in (a["w_ada"][0], a["w_mod_2"][0]) for x in blocks(w)]
    for at, some in ((G_AT, g_blocks), (A_AT, a_blocks)):
        assert len(at) == len(some)
        for n, x in zip(at, some):
            stream[n, :, 0:x.shape[1], :] = x

    vectors = dict(
        c1=a["c"][0], c2=a["c_2"][0], cctx=a["c_ctx_2"], b_ada=a["b_ada"][0], mix_pre=a["mix_norm_pre"][0],
        mix_post=a["mix_norm_post"][0], mlp_pre=a["mlp_norm_pre"][0], mlp_post=a["mlp_norm_post"][0],
        b_gate=a["b_gate"][0], lb=a["hgrn_lb_logits"][0], hgrn_w=a["hgrn_norm_w"][0],
        conv_w=a["conv_w"][0].reshape(C_TAPS, C_TILES, P).transpose(1, 0, 2), conv_b=a["conv_b"][0],
        ln_g=a["conv_ln_g"][0], ln_b=a["conv_ln_b"][0], b_mod=a["b_mod_2"][0], g_pre_mix=a["g_pre_mix_2"][0],
        g_post_mix=a["g_post_mix_2"][0], g_pre_ffn=a["g_pre_ffn_2"][0], g_post_ffn=a["g_post_ffn_2"][0],
        qk_w=a["conv_qk_w_2"][0], qk_b=a["conv_qk_b_2"][0], g_mlstm=a["g_mlstm_2"][0], g_diff=a["g_diff_2"][0],
        ffn_w=a["conv_ffn_w_2"][0], ffn_b=a["conv_ffn_b_2"][0])
    vec = _np.zeros((P, NVEC), _np.float32)
    for name, x in vectors.items():
        c = columns(x)
        vec[:, VEC[name]:VEC[name] + c.shape[1]] = c
    vec[0:32, VEC["mg_b"]] = a["b_gate_2"][0].reshape(-1)
    for i, name in enumerate(("lambda_q1_2", "lambda_k1_2", "lambda_q2_2", "lambda_k2_2")):
        vec[0:64, VEC["lam"] + i] = a[name][0]

    def tokens_last(x):
        return _np.ascontiguousarray(x.reshape(S, KT, P).transpose(2, 1, 0))

    consts, lvl, ident = constant_arrays()
    arrays = dict(
        stream=stream, x_t=tokens_last(a["x"][0]), ctx_t=tokens_last(a["ctx_2"][0]), vec=vec, consts=consts, lvl_mask=lvl, ident=ident,
        rel_bias=a["rel_bias"])

    nc = _bacc.Bacc("TRN2", target_bir_lowering=False, num_devices=1)
    aps = [nc.dram_tensor(k, x.shape, mybir.dt.from_np(x.dtype), kind="ExternalInput").ap() for k, x in arrays.items()]
    scratch = nc.dram_tensor("bias_rows", (B_HEADS, P * BPITCH), F32, kind="Internal").ap()
    x_keep = nc.dram_tensor("x_keep", (P, KT, S), F32, kind="Internal").ap()
    out = nc.dram_tensor("out_t", (P, KT, S), F32, kind="ExternalOutput").ap()
    two_blocks_kernel(nc, *aps, scratch, x_keep, out)
    got = _run(nc, [arrays], core_ids=[0]).results[0]["out_t"]
    return _np.ascontiguousarray(got.transpose(2, 1, 0)).reshape(1, S, D)
```

```python
from contextlib import ExitStack

import concourse.bass as bass
from concourse import mybir

F32 = mybir.dt.float32
U8 = mybir.dt.uint8
ALU = mybir.AluOpType
ACT = mybir.ActivationFunctionType
AX_X = mybir.AxisListType.X

F32R = mybir.dt.float32r
P = 128
S = 256
D = 2048
KT = D // P
SLOTS = 4
EPS = 1e-6
TINY = 1e-30
MASK_VALUE = -1e30
A_HEADS, B_HEADS, B_SLOTS = 8, 12, 4
C_TILES, C_TAPS = 6, 31
EARLY = 2
CONV_DVE = 3
CONV_SIDE = (C_TILES - CONV_DVE) * C_TAPS + C_TAPS - 1
FF1, FF2 = 8192 // P, 5632 // P
QUARTER = 4
UP2 = FF2 // QUARTER
LAM_INIT = 0.2
BROW = 383
BPITCH = 384

MIX = "GAGAGAAG"
MIXED = ("w_o", "up1_0", "up1_1", "up1_2")
SECTIONS = (
    [("ada_a", "A" * 32), ("c_a", "G" * 6), ("c_g", "G" * 6), ("a_f", "G" * 8), ("a_q", "G" * 8), ("a_i", "G" * 8), ("b_v", "G" * 6),
     ("b_k", "G" * 6), ("b_q", "G" * 6), ("a_g", "G" * 8), ("merge", "GG"), ("ada_b", "A" * 32), ("merge", "G" * 62),
     ("w_o", MIX * 4)]
    + [s for q in range(QUARTER) for s in ((f"up1_{q}", (MIX if f"up1_{q}" in MIXED else "GGGG") * 4), (f"down1_{q}", "G" * 16))]
    + [("m_q", "G" * 8), ("m_k", "G" * 8), ("m_g", "G"), ("m_v", "G" * 8), ("m_o", "GG"), ("ada_m", "A" * 32), ("m_o", "G" * 6),
       ("d_q", "G" * 8), ("d_k", "G" * 8), ("d_v", "G" * 8), ("w_out", "GG"), ("ada_d", "A" * 32), ("w_out", "G" * 14)]
    + [s for q in range(QUARTER) for s in ((f"up2_{q}", "GG" * UP2), (f"down2_{q}", "G" * 16))]
)


def plan_stream():
    g, a, first, blocks = [], [], {}, {}
    n = 0
    for name, kinds in SECTIONS:
        first.setdefault(name, (n, len(g), len(a)))
        blocks[name] = blocks.get(name, 0) + kinds.count("G")
        for kind in kinds:
            (g if kind == "G" else a).append(n)
            n += 1
    return g, a, first, blocks, n


G_AT, A_AT, FIRST, BLOCKS, N_STREAM = plan_stream()


def gb(name, i=0):
    return FIRST[name][1] + i


VECTORS = [
    ("c1", 16), ("c2", 16), ("cctx", 16), ("b_ada", 96), ("mix_pre", 16), ("mix_post", 16), ("mlp_pre", 16),
    ("mlp_post", 16), ("b_gate", 48), ("lb", 8), ("hgrn_w", 1), ("conv_w", C_TILES * C_TAPS), ("conv_b", 6),
    ("ln_g", 6), ("ln_b", 6), ("b_mod", 96), ("g_pre_mix", 16), ("g_post_mix", 16), ("g_pre_ffn", 16),
    ("g_post_ffn", 16), ("qk_w", 48), ("qk_b", 16), ("g_mlstm", 8), ("g_diff", 1), ("ffn_w", 3 * 2 * FF2),
    ("ffn_b", 2 * FF2), ("mg_b", 1), ("lam", 4),
]


def vector_columns():
    at, n = {}, 0
    for name, width in VECTORS:
        at[name] = n
        n += width
    return at, n


VEC, NVEC = vector_columns()

CONSTS = [("perm", P), ("cos", S), ("sin", S), ("tri_f", P), ("tri_b", P), ("onehot", BPITCH), ("bmask", BPITCH)]


def const_columns():
    at, n = {}, 0
    for name, width in CONSTS:
        at[name] = n
        n += width
    return at, n


CONST, NCONST = const_columns()


class Chain:

    def __init__(self, engine, sem):
        self.engine, self.sem, self.n, self.offset = engine, sem, 0, 0

    def __call__(self, instruction):
        self.n += 1
        instruction.then_inc(self.sem, 1)
        self.engine.wait_ge(self.sem, self.n + self.offset)


def two_blocks_kernel(nc, stream, x_t, ctx_t, vec_d, const_d, lvl_mask_d, ident_d, rel_bias, scratch, x_keep, out_t):
    with ExitStack() as ctx:
        def sb(name, shape, dt=F32):
            return ctx.enter_context(nc.sbuf_tensor("sb_" + name, shape, dt))

        def sem(name):
            return ctx.enter_context(nc.semaphore(name))

        raw = sb("raw", [P, SLOTS, KT, P])
        parts = sb("parts", [P, 2, 2, KT, P], F32R)
        ident = sb("ident", [P, P])
        ones = sb("ones", [P, P])
        vec = sb("vec", [P, NVEC])
        cpad = sb("cpad", [P, KT, 64])
        sel = sb("sel", [P, 8])
        head_sum = sb("head_sum", [P, 16])
        mod1 = sb("mod1", [P, 96])
        mod2 = sb("mod2", [P, 2, 96])
        lvl_mask = sb("lvl_mask", [P, 8, P], U8)
        rstd = sb("rstd", [P, 512])
        small = sb("small", [P, 128])
        ARENA = 33024

        def operand(name, at, *dims):
            with nc.sbuf_tensor("pad_" + name, [P, at], F32), nc.sbuf_tensor("op_" + name, [P, *dims], F32R) as t:
                return t

        opH = operand("h", 4096, 2, KT, S)
        opY1 = operand("y1", 20480, 2, KT, S)
        opG = operand("merged", 12288, 2, KT, S)
        opU1 = operand("up1", 12288, 2, KT, S)
        opW = operand("hw", 4096, 2, KT, 512)
        opY2 = operand("y2", 12288, 2, KT, S)
        opU2 = operand("up2", 12288, 2, UP2, S)
        arena = sb("arena", [P, ARENA])
        G = [ctx.enter_context(nc.psum_tensor(f"gemm{i}", [P, 512], F32)) for i in range(4)]
        M = [ctx.enter_context(nc.psum_tensor(f"mix{i}", [P, 512], F32)) for i in range(4)]

        def region(at, *dims):
            n = 1
            for d in dims:
                n *= d
            assert at + n <= ARENA, (at, dims)
            flat = arena[:, at:at + n]
            if len(dims) == 1:
                return flat
            names = "abc"[:len(dims)]
            return flat.rearrange(f"p ({' '.join(names)}) -> p {' '.join(names)}", **dict(zip(names, dims)))

        def v(name, i=0, n=1):
            return vec[:, VEC[name] + i:VEC[name] + i + n]

        xT = region(0, KT, S)
        sq0 = region(12288, KT, S)
        hf0 = region(16384, KT, S)
        onehot, bmask, brow = region(20480, BPITCH), region(20864, BPITCH), region(21248, BPITCH)
        relb = region(21632, 12)
        lvl_f = region(22528, 8, P)
        modrow1 = region(32640, P)
        modrow_b = rstd[:, 0:P]
        fP = region(12288, 8, S)
        kk = region(14336, 8, S)
        qq = region(16384, 8, S)
        og = region(18432, 8, S)
        bq = region(20480, 6, S)
        bk = region(22016, 6, S)
        bv = region(23552, 2, 768)
        ii = region(25088, 2, 1024)
        ca = region(18432, 6, S)
        upad = region(19968, 6, 30 + S)
        ctap = region(18432, 3, S)
        cg = region(22016, 6, S)
        cy = yc = region(28672, 6, S)
        yb = region(30208, 2, S)
        suf = region(30720, 2, S)
        qs = region(31232, 2, S)
        ks = region(31744, 2, S)
        attn = region(32256, 4, P)
        attx = region(32768, 2, P)
        bias = region(12288, 12, S)
        blog = [region(15360 + 768 * i, 3, S) for i in range(2)]
        bpt = [region(16896 + 768 * i, 6, P) for i in range(2)]
        bdg = [region(30720 + P * i, P) for i in range(2)]
        gates = region(28672, 2, 3, S)
        mtmp = region(30208, 2, S)
        mfp = region(30720, 2, S)
        proj1 = region(4096, KT, S)
        sq1 = region(8192, KT, S)
        hf1 = region(20480, KT, S)
        ut = region(20480, 2, 2, S)
        modrow2 = region(22528, P)
        down1 = region(24576, KT, S)
        sqd1 = region(4096, KT, S)
        hfc = region(28672, KT, S)
        sqc = region(8192, KT, S)
        hfx = region(20480, KT, S)
        sqx = region(24576, KT, S)
        mq = region(20480, 8, S)
        mk = region(22528, 8, 512)
        mv = region(26624, 4, 1024)
        ym = region(0, 8, S)
        gG = region(0, 4, 512)
        gsb = region(2048, 512)
        gB = region(30720, 2, 512)
        gM = region(31744, 2, 512)
        gtmp = region(31744, 2, 512)
        grows = region(2048, 2, 2, S)
        aT = region(3072, 2, 4, 8)
        tri = [region(3136 + P * i, P) for i in range(2)]
        mden = region(3392, S)
        mW = [region(30720 + 1024 * i, 4, S) for i in range(2)]
        mfl = [region(3648, S), region(32768, S)]
        mo = region(30720, 8, S)
        dq = region(20480, 8, S)
        dk = region(22528, 8, 512)
        dv = region(26624, 4, 1024)
        yd = region(2048, 8, S)
        dE = [region(4096 + 1024 * i, 2, 512) for i in range(2)]
        dpd = [region(6144 + 512 * i, 512) for i in range(2)]
        dPT = [region(7168 + 512 * i, 4, P) for i in range(2)]
        rtab = region(2048, 640)
        rtmp = region(2688, 2, S)
        modrow_d = region(9344, P)
        modrow_m = region(3904, P)
        nsq = nrs = region(2048, 8, S)
        proj2 = region(20480, KT, S)
        sq2 = region(24576, KT, S)
        hf2 = region(28672, KT, S)
        fv = region(18432, 2, 2, S)
        ftm = region(19456, 2, S)
        down2 = region(20480, KT, S)

        amul, gmul, cmul = small[:, 0:16], small[:, 16:32], small[:, 64:80]
        lbc, lb1, sm_e = small[:, 32:40], small[:, 40:48], small[:, 80:88]
        lamn = small[:, 48:49]
        nm = [small[:, 96 + 2 * i:98 + 2 * i] for i in range(2)]
        zz = [small[:, 104 + 2 * i:106 + 2 * i] for i in range(2)]
        rz = [small[:, 112 + 2 * i:114 + 2 * i] for i in range(2)]
        lamp, lame = small[:, 120:122], small[:, 122:124]

        loaded = [sem(f"loaded{i}") for i in range(SLOTS)]
        taken = [sem(f"taken{i}") for i in range(SLOTS)]
        hi_ready = sem("hi_ready")
        hi_used = sem("hi_used")
        block_done = sem("block_done")
        bank_read = [sem(f"bank_read{i}") for i in range(4)]
        boot, x_in, fills, c_ready = sem("boot"), sem("x_in"), sem("fills"), sem("c_ready")
        row_ready, ada_cols, mod_read = sem("row_ready"), sem("ada_cols"), sem("mod_read")
        sq_ready, ms_ready, inv_ready, rstd_ready, heads_mm = (
            sem(n) for n in ("sq_ready", "ms_ready", "inv_ready", "rstd_ready", "heads_mm"))
        hf_ready, hh_ready, h_ready = sem("hf_ready"), sem("hh_ready"), sem("h_ready")
        sq_part, x_ready, hf_part, hh_part, h_part = (sem(n) for n in ("sq_part", "x_ready", "hf_part", "hh_part", "h_part"))
        dve_step, act_step = sem("dve_step"), sem("act_step")
        brow_mm, brow_ready, brow_out, bias_in = sem("brow_mm"), sem("brow_ready"), sem("brow_out"), sem("bias_in")
        conv_u, conv_tap, conv_side, mean_mm, conv_cent, yc_in, conv_done = (
            sem(n) for n in ("conv_u", "conv_tap", "conv_side", "mean_mm", "conv_cent", "yc_in", "conv_done"))
        lvl_prep, lvl_mm, lvl_read, o_mm, o_copied, ya_ready = (
            sem(n) for n in ("lvl_prep", "lvl_mm", "lvl_read", "o_mm", "o_copied", "ya_ready"))
        qk_mm, log_ready, exp_ready, dg_ready = sem("qk_mm"), sem("log_ready"), sem("exp_ready"), sem("dg_ready")
        pt_mm, pt_ready, pv_mm, yb_ready = sem("pt_mm"), sem("pt_ready"), sem("pv_mm"), sem("yb_ready")
        y_hi, y_ready = sem("y_hi"), sem("y_ready")
        merged_part, up_ready = sem("merged_part"), sem("up_ready")
        x_kept, x_back, cx_in, tab_in, mg_sb, mg_rows = (sem(n) for n in ("x_kept", "x_back", "cx_in", "tab_in", "mg_sb", "mg_rows"))
        ln_ready, rows_ready, at_mm, at_ready = (sem(n) for n in ("ln_ready", "rows_ready", "at_mm", "at_ready"))
        conv3_in, conv3_done, silu_done = sem("conv3_in"), sem("conv3_done"), sem("silu_done")
        s_mm, bc_mm, w_arg, w_ready, floor_ready, ws_ready = (
            sem(n) for n in ("s_mm", "bc_mm", "w_arg", "w_ready", "floor_ready", "ws_ready"))
        nd_mm, den_ready, fin_ready, ym_ready = sem("nd_mm"), sem("den_ready"), sem("fin_ready"), sem("ym_ready")
        rot_mm, rope_done = sem("rot_mm"), sem("rope_done")
        lam_in, lam_mm, lam_exp = sem("lam_in"), sem("lam_mm"), sem("lam_exp")
        dqk_mm, dmax, dexp, dpd_ready = sem("dqk_mm"), sem("dmax"), sem("dexp"), sem("dpd_ready")
        dpt_mm, dpt_ready, dpv_mm, dy_ready = (sem(n) for n in ("dpt_mm", "dpt_ready", "dpv_mm", "dy_ready"))
        taps_in, gate_silu, ffn_done = sem("taps_in"), sem("gate_silu"), sem("ffn_done")
        stored = sem("stored")

        def use(n, it=0, dn=0):
            return n % SLOTS, n // SLOTS + it * (dn // SLOTS)

        def kt_of(b):
            return UP2 if any(gb(f"down2_{q}") <= b < gb(f"down2_{q}") + 16 for q in range(QUARTER)) else KT

        def quarter_of(t, c):
            return t[:, bass.ds(c * 4, 4), :] if not isinstance(c, int) else t[:, 4 * c:4 * c + 4, :]

        def scores_bank(unit, c):
            return (M if unit % 2 == 0 else G)[c]

        def scores_of(head, half):
            return G[(2 * head + half) % 3]

        def conv_tap_of(t, tap):
            return v("conv_w", t * C_TAPS + tap)

        def buffer_of(b):
            q = max(q for q in range(QUARTER) if gb(f"up2_{q}") <= b)
            return (q * UP2 + (b - gb(f"up2_{q}")) // 2) % 2

        def tiles_of(direction):
            return (2, 3, slice(P, S)) if direction == 0 else (3, 2, slice(0, P))

        def bank(b):
            return G[b % 4]

        def done(eng, b, it=0):
            eng.wait_ge(block_done, b + 1 + it * 4)

        def was_read(eng, b, it=0):
            eng.wait_ge(bank_read[b % 4], b // 4 + 1 + it)

        def steps_of(section):
            return 2 * 4 if section in MIXED else 4

        def rounds_of(section):
            return BLOCKS[section] // 4

        block = ctx.enter_context(nc.Block())

        @block.sync
        def _(sp):
            def load_run(n0, count, kt):
                def load(n, r):
                    slot, uses = use(n, r, SLOTS)
                    if n >= SLOTS:
                        sp.wait_ge(taken[slot], uses)
                    sp.dma_start(raw[:, slot, 0:kt, :], stream[r * SLOTS + n][:, 0:kt, :]).then_inc(loaded[slot], 16)

                if count >= 2 * SLOTS:
                    with sp.Fori(0, count // SLOTS) as r:
                        for j in range(SLOTS):
                            load(n0 + j, r)
                for n in range(n0 + (count // SLOTS * SLOTS if count >= 2 * SLOTS else 0), n0 + count):
                    load(n, 0)

            load_run(0, SLOTS, KT)
            at = SLOTS
            for q in range(QUARTER):
                d = FIRST[f"down2_{q}"][0]
                load_run(at, d - at, KT)
                load_run(d, 16, UP2)
                at = d + 16
            for c in range(4):
                sp.wait_ge(x_ready, 12 + c + 1)
                sp.dma_start(quarter_of(out_t, c), quarter_of(xT, c)).then_inc(stored, 16)
            sp.wait_ge(stored, 64)

        @block.gpsimd
        def _(pool):
            pool.memset(cpad[:, :, :], 0.0).then_inc(fills, 1)
            pool.memset(ones[:, :], 1.0).then_inc(fills, 1)
            pool.memset(head_sum[:, :], 0.0).then_inc(fills, 1)
            pool.wait_ge(fills, 3)
            pool.memset(head_sum[:, 7:8], 1.0).then_inc(fills, 1)
            pool.wait_ge(brow_ready, 1)
            pool.dma_start(scratch[:, 0:P * BPITCH].rearrange("h (p c) -> h p c", c=BPITCH),
                           brow[0:12, :].unsqueeze(1).to_broadcast([12, P, BPITCH])).then_inc(brow_out, 16)
            pool.wait_ge(brow_out, 16)
            for i in range(6):
                was_read(pool, gb("c_a", i))
                was_read(pool, gb("c_g", i))
            pool.memset(upad[:, :, 0:30], 0.0).then_inc(conv_u, 1)
            pool.tensor_tensor(upad[:, :, 30:30 + S], ca, cg, ALU.mult).then_inc(conv_u, 1)
            pool.wait_ge(conv_u, 2)
            n = 0
            for tap in range(C_TAPS):
                if tap:
                    pool.wait_ge(conv_side, n)
                for t in range(CONV_DVE, C_TILES):
                    dst = ctap[:, t - CONV_DVE, :] if tap else cy[:, t, :]
                    pool.tensor_scalar(dst, upad[:, t, tap:tap + S], conv_tap_of(t, tap), None if tap else v("conv_b", t),
                                       ALU.mult, *(() if tap else (ALU.add,))).then_inc(conv_side, 1)
                    n += 1
                if tap:
                    pool.wait_ge(conv_side, n)
                    pool.tensor_tensor(cy[:, CONV_DVE:, :], cy[:, CONV_DVE:, :], ctap, ALU.add).then_inc(conv_side, 1)
                    n += 1
            assert n == CONV_SIDE
            pool.wait_ge(ya_ready, 1)
            skew = scratch[:, 0:P * (BPITCH - 1)].rearrange("h (p c) -> p h c", c=BPITCH - 1)
            pool.dma_start(bias, skew[:, :, P - 1:P - 1 + S]).then_inc(bias_in, 16)
            pool.wait_ge(x_ready, 4)
            pool.dma_start(hfc, ctx_t).then_inc(cx_in, 16)
            pool.wait_ge(hf_part, 12)
            pool.dma_start(x_keep, xT).then_inc(x_kept, 16)
            pool.wait_ge(x_kept, 16)
            pool.dma_start(tri[0], const_d[:, CONST["tri_f"]:CONST["tri_f"] + P]).then_inc(tab_in, 16)
            pool.dma_start(tri[1], const_d[:, CONST["tri_b"]:CONST["tri_b"] + P]).then_inc(tab_in, 16)
            pool.wait_ge(mg_sb, 1)
            for g in range(4):
                pool.dma_start(gG[0:8, g, :], gsb[8 * g:8 * g + 8, :]).then_inc(mg_rows, 16)
            pool.wait_ge(ym_ready, 1)
            pool.dma_start(rtab, const_d[:, 0:640]).then_inc(tab_in, 16)
            pool.wait_ge(h_ready, 2)
            pool.dma_start(xT, x_keep).then_inc(x_back, 16)

        @block.scalar
        def _(act):
            step = Chain(act, act_step)
            norms, splits = [0], [0]

            act.dma_start(vec[:, :], vec_d).then_inc(boot, 16)
            act.dma_start(ident[:, :], ident_d[:, 0:P]).then_inc(boot, 16)
            act.dma_start(sel[:, :], ident_d[:, P:P + 8]).then_inc(boot, 16)
            act.dma_start(lvl_f, lvl_mask_d).then_inc(boot, 16)
            act.dma_start(onehot, const_d[:, CONST["onehot"]:CONST["onehot"] + BPITCH]).then_inc(boot, 16)
            act.dma_start(bmask, const_d[:, CONST["bmask"]:CONST["bmask"] + BPITCH]).then_inc(boot, 16)
            act.dma_start(relb[0:32, :], rel_bias).then_inc(boot, 16)
            act.dma_start(xT, x_t).then_inc(x_in, 16)

            def square(dst, src):
                norms[0] += 1
                act.activation(dst, src, ACT.Square).then_inc(sq_ready, 1)

            def root(t, of_parts=False):
                norms[0] += of_parts
                act.wait_ge(inv_ready, norms[0])
                act.activation(t, t, ACT.Sqrt).then_inc(rstd_ready, 1)

            def square_part(sq, src, c):
                act.activation(quarter_of(sq, c), quarter_of(src, c), ACT.Square).then_inc(sq_part, 1)

            def square_x(sq, n):
                for c in range(4):
                    act.wait_ge(x_ready, 4 * n + c + 1)
                    square_part(sq, xT, c)

            def high_parts(dst, src, n):
                for c in range(4):
                    act.wait_ge(hf_part, 4 * n + c + 1)
                    act.activation(quarter_of(dst, c), quarter_of(src, c), ACT.Copy).then_inc(hh_part, 1)

            def high(dst, src):
                splits[0] += 1
                act.wait_ge(hf_ready, splits[0])
                act.activation(dst, src, ACT.Copy).then_inc(hh_ready, 1)

            def split_high(b, it=0, dn=0):
                if b >= len(G_AT):
                    return
                slot, uses = use(G_AT[b], it, dn)
                kt = kt_of(b)
                act.wait_ge(loaded[slot], 16 * (uses + 1))
                if b >= 2:
                    act.wait_ge(hi_used, b - 1 + it * 4)
                act.activation(parts[:, b % 2, 0, 0:kt, :], raw[:, slot, 0:kt, :], ACT.Copy).then_inc(hi_ready, 1)

            def copy_rows(a_last, it, dn, modrow, group, rows=M[2]):
                slot, uses = use(A_AT[a_last], it, dn)
                act.wait_ge(taken[slot], uses + 1)
                act.wait_ge(ada_cols, group)
                act.activation(modrow, rows[:, 0:P], ACT.Copy).then_inc(row_ready, 1)

            def rows_beside(part, blocks, modrow, rows):
                for n in blocks:
                    if n % 4 == 3:
                        a = FIRST[part][2] + n
                        copy_rows(a, 0, 0, modrow, a // 4, rows)

            def copy_out(b, dst, func=ACT.Copy, it=0, cols=S):
                done(act, b, it)
                act.activation(dst, bank(b)[:, 0:cols], func).then_inc(bank_read[b % 4], 1)

            def rounds(section, body, first=0, between=lambda: None):
                for r in range(first):
                    body(0, r)
                with act.Fori(0, rounds_of(section) - 1 - first) as it:
                    body(it, first)
                between()
                body(0, rounds_of(section) - 1)

            def in_round(section, it, r):
                b = gb(section) + 4 * r
                return b, lambda j: split_high(b + j + 2, it, steps_of(section))

            act.wait_ge(boot, 112)
            act.wait_ge(fills, 1)
            act.activation(cpad[:, :, 32], v("c1", 0, 16), ACT.Silu).then_inc(c_ready, 1)
            act.wait_ge(x_in, 16)
            square(sq0, xT)
            root(rstd[:, 0:S])
            with act.Fori(0, 8) as it:
                slot, uses = use(3, it, 4)
                act.wait_ge(taken[slot], uses + 1)
                act.activation(modrow1, M[2][:, 0:P], ACT.Copy).then_inc(row_ready, 1)
            split_high(0)
            split_high(1)
            high_parts(opH[:, 0], hf0, 0)
            for i in range(6):
                b = gb("c_a", i)
                split_high(b + 2)
                copy_out(b, ca[:, i, :])
            for i in range(6):
                b = gb("c_g", i)
                split_high(b + 2)
                copy_out(b, cg[:, i, :], ACT.Sigmoid)
            for i in range(8):
                b = gb("a_f", i)
                split_high(b + 2)
                done(act, b)
                act.activation(fP[:, i, :], bank(b)[:, 0:S], ACT.Sigmoid)
                act.activation(kk[:, i, :], bank(b)[:, 0:S], ACT.Sigmoid, scale=-1.0).then_inc(bank_read[b % 4], 1)
            for i in range(8):
                b = gb("a_q", i)
                split_high(b + 2)
                copy_out(b, qq[:, i, :], ACT.Silu)

            def copy_tokens(part, i, dst, tiles):
                b = gb(part, i)
                for n in range(2):
                    done(act, b + n)
                    if 2 * n < tiles:
                        act.activation(dst[:, 2 * n:2 * n + 2, i * P:(i + 2) * P], bank(b + n)[:, :].rearrange("p (a b) -> p a b", a=2),
                                       ACT.Copy).then_inc(bank_read[(b + n) % 4], 1)
                    else:
                        act.sem_inc(bank_read[(b + n) % 4], 1)

            def copy_o(quarter):
                act.wait_ge(o_mm, quarter + 1)
                act.activation(qq[:, 2 * quarter:2 * quarter + 2, :], M[3][:, :].rearrange("p (a b) -> p a b", a=2), ACT.Copy)\
                   .then_inc(o_copied, 1)

            late = [("a_i", i) for i in range(8)] + [("b_v", i) for i in range(6)] + [("b_k", i) for i in range(6)] \
                + [("b_q", i) for i in range(6)] + [("a_g", i) for i in range(8)]
            for s in range(36):
                if s < len(late):
                    part, i = late[s]
                    b = gb(part, i)
                    split_high(b + 2)
                    if part in ("a_i", "b_v"):
                        if i % 2 == 1:
                            copy_tokens(part, i - 1, ii if part == "a_i" else bv, 2)
                    elif part == "a_g":
                        copy_out(b, og[:, i, :], ACT.Silu)
                    else:
                        copy_out(b, (bk if part == "b_k" else bq)[:, i, :])
                if s % 9 == 0 and s:
                    copy_o(s // 9 - 1)
                if s == 16:
                    act.wait_ge(conv_cent, 1)
                    square(ca, cy)
                if s == 18:
                    root(rstd[:, 0:S])
                if s == 20:
                    act.wait_ge(yc_in, 1)
                    for t in range(C_TILES):
                        ins = act.activation(yc[:, t, :], cy[:, t, :], ACT.Silu, bias=v("ln_b", t), scale=v("ln_g", t))
                    ins.then_inc(conv_done, 1)
            rows_beside("ada_b", (3,), modrow_b, G[2])
            copy_o(3)
            act.wait_ge(o_copied, 4)
            square(fP, qq)
            root(kk[0:8, 0, :])
            for g in range(1, EARLY):
                rows_beside("ada_b", (4 * g + 3,), modrow_b, G[2])
            for u in range(9):
                n = 4 * EARLY + 3 * u
                if u < 8:
                    T, e = u // 4, u % 2
                    w = P * (T + 1)
                    act.wait_ge(log_ready, u + 1)
                    act.activation(blog[e][:, :, 0:w], blog[e][:, :, 0:w], ACT.Exp, bias=nm[e][:, 0:1],
                                   accum_out=zz[e][:, 0:1]).then_inc(exp_ready, 1)
                    rows_beside("ada_b", (n, n + 1), modrow_b, G[2])
                if u >= 1:
                    T, slot, e = (u - 1) // 4, (u - 1) % 4, (u - 1) % 2
                    po = 64 * (slot % 2)
                    act.wait_ge(pv_mm, u)
                    act.activation(yb[po:po + 64, slot // 2, P * T:P * T + P], G[e][po:po + 64, 0:P], ACT.Copy)\
                       .then_inc(yb_ready, 1)
                if u < 8:
                    rows_beside("ada_b", (n + 2,), modrow_b, G[2])
            act.wait_ge(yb_ready, 8)
            act.activation(opY1[:, 0, 0:8, :], og, ACT.Copy)
            act.activation(opY1[:, 0, 8:10, :], yb, ACT.Copy)
            act.activation(opY1[:, 0, 10:16, :], yc, ACT.Copy).then_inc(y_hi, 1)
            act.wait_ge(y_ready, 1)

            def merge_round(it, r):
                b0, ahead = in_round("merge", it, r)
                for j in range(4):
                    ahead(j)
                    if j < 3:
                        done(act, b0 + j, it)
                        if j == 0:
                            act.wait_ge(merged_part, it + r + 1)
                        act.activation(gates[:, 0, j, :], bank(b0 + j)[:, 0:S], ACT.Sigmoid,
                                       bias=vec[:, bass.ds(VEC["b_gate"] + 16 * j + it + r, 1)]).then_inc(bank_read[(b0 + j) % 4], 1)

            rounds("merge", merge_round, 1)

            def plain_round(section, dst, modrow=None, squares=None):
                def body(it, r):
                    b0, ahead = in_round(section, it, r)
                    for j in range(4):
                        ahead(j)
                        copy_out(b0 + j, dst[:, bass.ds(j + it * 4 + 4 * r, 1), :].rearrange("p a b -> p (a b)"), it=it)
                        if modrow is not None and j == 2:
                            a = FIRST[section][2] + 3 + 4 * r
                            copy_rows(a, it, 8, modrow, FIRST[section][2] // 4 + it + r)
                    if squares is not None:
                        was_read(act, b0 + 3, it)
                        square_part(squares, dst, it + r)
                return body

            rounds("w_o", plain_round("w_o", proj1, modrow2, sq1))
            root(rstd[:, 0:S], True)
            square_x(sq1, 0)
            root(rstd[:, 0:S], True)
            high_parts(opH[:, 0], hf1, 1)

            def down_round(section, acc=None, squares=None):
                def body(it, r):
                    b0, ahead = in_round(section, it, r)
                    for j in range(4):
                        ahead(j)
                    if squares is not None:
                        was_read(act, b0 + 3, it)
                        square_part(squares, acc, it + r)
                return body

            for q in range(QUARTER):
                def up_round(it, r, section=f"up1_{q}", q=q):
                    b0, ahead = in_round(section, it, r)
                    for j in range(4):
                        ahead(j)
                        done(act, b0 + j, it)
                        act.wait_ge(up_ready, 16 * q + 4 * r + j + 1 + it * 4)
                        act.activation(ut[:, j % 2, 0, :], bank(b0 + j)[:, 0:S], ACT.Relu).then_inc(bank_read[(b0 + j) % 4], 1)
                        if j == 2 and section in MIXED:
                            a = FIRST[section][2] + 3 + 4 * r
                            copy_rows(a, it, 8, modrow2, FIRST[section][2] // 4 + it + r)
                rounds(f"up1_{q}", up_round)
                if q == 0:
                    act.wait_ge(ada_cols, 24)
                    act.activation(cpad[:, :, 32], v("c2", 0, 16), ACT.Silu)
                    act.activation(cpad[:, :, 33], v("cctx", 0, 16), ACT.Silu).then_inc(c_ready, 1)
                    rounds("down1_0", plain_round("down1_0", down1))
                elif q < 3:
                    rounds(f"down1_{q}", down_round(f"down1_{q}"))
                else:
                    act.wait_ge(cx_in, 16)
                    square(sqc, hfc)
                    rounds("down1_3", down_round("down1_3", down1, sqd1), between=lambda: root(rstd[:, 0:S]))
            root(rstd[:, 0:S], True)
            high(opW[:, 0, :, 0:S], hfc)
            square_x(sqx, 1)
            root(rstd[:, S:512], True)
            high_parts(opW[:, 0, :, S:512], hfx, 2)

            def conv3_block(part, i, dst, tile0, cols):
                b = gb(part, i)
                split_high(b + 2)
                done(act, b)
                act.activation(dst[:, i, :], bank(b)[:, 0:cols], ACT.Identity, scale=v("qk_w", 16 + tile0 + i), bias=v("qk_b", tile0 + i))\
                   .then_inc(conv3_in, 1)

            for i in range(8):
                conv3_block("m_q", i, mq, 0, S)
            for i in range(8):
                conv3_block("m_k", i, mk, 8, 512)
            b = gb("m_g")
            split_high(b + 2)
            done(act, b)
            act.wait_ge(x_kept, 16)
            act.activation(gsb[0:32, :], bank(b)[0:32, :], ACT.Identity, bias=v("mg_b")[0:32, :]).then_inc(mg_sb, 1)
            act.wait_ge(mg_sb, 1)
            act.sem_inc(bank_read[b % 4], 1)
            for i in range(0, 8, 2):
                split_high(gb("m_v", i) + 2)
                split_high(gb("m_v", i) + 3)
                copy_tokens("m_v", i, mv, 4)
                if i == 0:
                    act.wait_ge(mg_rows, 64)
                    step(act.activation(gtmp[0:8, :, :], gG[0:8, 1:4:2, :], ACT.Abs))
                    step(act.activation(gtmp[0:8, :, :], gtmp[0:8, :, :], ACT.Exp, scale=-1.0))
                    act.activation(gtmp[0:8, :, :], gtmp[0:8, :, :], ACT.Ln, bias=1.0).then_inc(ln_ready, 1)
                if i == 2:
                    act.wait_ge(conv3_done, 16)
                    act.activation(mq, mq, ACT.Silu)
                if i == 4:
                    act.activation(mk, mk, ACT.Silu).then_inc(silu_done, 1)
            for u in range(17):
                if u < 16:
                    e = u % 2
                    act.wait_ge(w_arg, u + 1)
                    last, half, cut = tiles_of(e)
                    act.activation(mW[e][:, 0:2, :], mW[e][:, 0:2, :], ACT.Exp)
                    act.activation(mW[e][:, last, :], mW[e][:, last, :], ACT.Exp)
                    act.activation(mW[e][:, half, cut], mW[e][:, half, cut], ACT.Exp).then_inc(w_ready, 1)
                    if u >= 2:
                        act.wait_ge(fin_ready, u - 1)
                    act.activation(mfl[e], M[e][:, S:512], ACT.Exp).then_inc(floor_ready, 1)
                if u >= 1:
                    act.wait_ge(nd_mm, u)
                    if u >= 2:
                        act.wait_ge(fin_ready, u - 1)
                    act.activation(mden, M[2 + (u - 1) % 2][:, S:512], ACT.Abs).then_inc(den_ready, 1)
                if u < 16:
                    rows_beside("ada_m", (2 * u + 1,), modrow_m, G[3])
            act.wait_ge(fin_ready, 16)
            square(nsq, ym)
            for i in range(8):
                b = gb("m_o", i)
                split_high(b + 2)
                copy_out(b, mo[:, i, :], ACT.Sigmoid)
            for i in range(8):
                b = gb("d_q", i)
                split_high(b + 2)
                copy_out(b, dq[:, i, :])
            for i in range(8):
                b = gb("d_k", i)
                if i == 0:
                    root(nrs[0:8, 0, :])
                split_high(b + 2)
                copy_out(b, dk[:, i, :], cols=512)
            act.wait_ge(lam_mm, 1)
            act.activation(lame, M[3][:, 0:2], ACT.Exp).then_inc(lam_exp, 1)
            for i in range(0, 8, 2):
                split_high(gb("d_v", i) + 2)
                split_high(gb("d_v", i) + 3)
                copy_tokens("d_v", i, dv, 4)
            for u in range(18):
                if u < 16:
                    e = u % 2
                    act.wait_ge(dmax, u + 1)
                    if u >= 2:
                        act.wait_ge(dpd_ready, u - 1)
                    for c in range(2):
                        ins = act.activation(dE[e][:, c, :], scores_bank(u, c)[:, :], ACT.Exp, bias=nm[e][:, c:c + 1], scale=0.125,
                                             accum_out=zz[e][:, c:c + 1])
                    ins.then_inc(dexp, 1)
                if u >= 2:
                    head, T = (u - 2) // 2, u % 2
                    act.wait_ge(dpt_mm, u - 1)
                    if u >= 4:
                        act.wait_ge(dpv_mm, u - 3)
                    act.activation(dPT[u % 2].rearrange("p a b -> p (a b)"), M[2][:, :], ACT.Copy).then_inc(dpt_ready, 1)
                if u < 16:
                    rows_beside("ada_d", (2 * u + 1,), modrow_d, G[2])
                if u >= 2:
                    act.wait_ge(dpv_mm, u - 1)
                    act.activation(yd[:, head, P * T:P * T + P], M[3][:, 0:P], ACT.Copy).then_inc(dy_ready, 1)
            act.wait_ge(dy_ready, 16)
            square(dq, yd)
            root(dk[0:8, 0, 0:S])
            high(opY2[:, 0], region(0, KT, S))
            rounds("w_out", plain_round("w_out", proj2, squares=sq2), 1)
            root(rstd[:, 0:S], True)
            square_x(sq2, 2)
            root(rstd[:, 0:S], True)
            high_parts(opH[:, 0], hf2, 3)
            for q in range(QUARTER):
                def pair(b, pos, tile, it, ahead):
                    for c in range(2):
                        ahead(c)
                        done(act, b + c, it)
                        if c == 0:
                            act.wait_ge(ffn_done, pos + 1)
                        w = vec[:, bass.ds(tile + VEC["ffn_w"] + 2 * FF2 + c * FF2, 1)]
                        bb = vec[:, bass.ds(tile + VEC["ffn_b"] + c * FF2, 1)]
                        act.activation(fv[:, buffer_of(b), c, :], bank(b + c)[:, 0:S], ACT.Identity, scale=w, bias=bb)\
                           .then_inc(taps_in, 1)
                    was_read(act, b, it)
                    act.activation(fv[:, buffer_of(b), 0, :], fv[:, buffer_of(b), 0, :], ACT.Silu).then_inc(gate_silu, 1)

                b0, t0 = gb(f"up2_{q}"), q * UP2
                with act.Fori(0, 5) as it:
                    for j in range(2):
                        pair(b0 + 2 * j, t0 + j + it * 2, t0 + j + it * 2, it,
                             lambda c, j=j: split_high(b0 + 2 * j + c + 2, it, 4))
                pair(b0 + 20, t0 + 10, t0 + 10, 0, lambda c: split_high(b0 + 20 + c + 2))
                if q == 0:
                    rounds("down2_0", plain_round("down2_0", down2))
                elif q < 3:
                    rounds(f"down2_{q}", down_round(f"down2_{q}"))
                else:
                    rounds("down2_3", down_round("down2_3", down2, sq2))
            root(rstd[:, 0:S], True)

        @block.tensor
        def _(pe):
            norms, wholes, sq_parts = [0], [0], [0]

            def product(b, pieces, it=0, dn=0, pair=False, later=False, waits={}):
                both = range(b, b + 2) if pair else range(b, b + 1)
                for n in both:
                    pe.wait_ge(hi_ready, n + 1 + it * 4)
                    if n >= 4:
                        pe.wait_ge(bank_read[n % 4], n // 4 + it)
                hi, lo = (parts[:, :, 0], parts[:, :, 1]) if pair else (parts[:, b % 2, 0], parts[:, b % 2, 1])
                for out, opens, terms in pieces:
                    for i, (w, xh, xl) in enumerate(terms):
                        if i in waits:
                            pe.wait_ge(*waits[i])
                        for x in (xh, xl):
                            l, r = w(hi, x)
                            ins = pe.matmul(out, l, r, start=(opens and i == 0 and x is xh), stop=False, skip_group_check=True)

                def with_low():
                    for n in both:
                        slot, uses = use(G_AT[n], it, dn)
                        pe.wait_ge(taken[slot], uses + 1)
                    for n, (out, opens, terms) in enumerate(pieces):
                        for i, (w, xh, xl) in enumerate(terms):
                            l, r = w(lo, xh)
                            ins = pe.matmul(out, l, r, start=False, stop=(i == len(terms) - 1), skip_group_check=True)
                            if n == 0 and i == 0:
                                ins.then_inc(hi_used, len(both))
                    ins.then_inc(block_done, len(both))

                if later:
                    return with_low
                with_low()

            def features(out, op, k0=0, k1=KT, cols=slice(0, S), kw=0):
                return (out, True, [(lambda w, x, k=k: (w[:, kw + k - k0, :], x), op[:, 0, k, cols], op[:, 1, k, cols])
                                    for k in range(k0, k1)])

            def gemm_T(b, op, it=0, dn=0, cols=slice(0, S), kt=KT, waits={}):
                product(b, [features(bank(b)[:, 0:cols.stop - cols.start], op, 0, kt, cols)], it, dn, waits=waits)

            def quarters(n):
                return {4 * c: (h_part, 4 * n + c + 1) for c in range(4)}

            def gemm_tokens(b, op, tiles, later=False):
                def tile(t):
                    out = bank(b + t // 2)[:, (t % 2) * S:(t % 2 + 1) * S].rearrange("p (a b) -> p a b", a=2)
                    tok = slice(t * P, (t + 1) * P)
                    return (out, t % 2 == 0, [(lambda w, x, k=k: (x, w[:, :, k, :]), op[:, 0, k, tok], op[:, 1, k, tok])
                                              for k in range(KT)])

                return product(b, [tile(t) for t in range(tiles)], pair=True, later=later)

            def norm(src, n, sums=M[2]):
                norms[0] += 1
                wholes[0] += 1
                pe.wait_ge(sq_ready, wholes[0])
                for k in range(n):
                    ins = pe.matmul(sums[:, 0:S], ones[:, :], src[:, k, :], start=(k == 0), stop=(k == n - 1))
                ins.then_inc(ms_ready, 1)

            def norm_parts(src, quarters):
                for c in quarters:
                    sq_parts[0] += 1
                    pe.wait_ge(sq_part, sq_parts[0])
                    for k in range(4 * c, 4 * c + 4):
                        ins = pe.matmul(M[1][:, 0:S], ones[:, :], src[:, k, :], start=(k == 0), stop=(k == KT - 1))
                if 3 in quarters:
                    norms[0] += 1
                    ins.then_inc(ms_ready, 1)

            def norm_heads(src):
                norms[0] += 1
                wholes[0] += 1
                pe.wait_ge(sq_ready, wholes[0])
                for h in range(8):
                    ins = pe.matmul(M[0][0:8, 0:S], head_sum[:, 7 - h:15 - h], src[:, h, :], start=(h == 0), stop=(h == 7))
                ins.then_inc(ms_ready, 1)

            def spread_heads(rows):
                pe.wait_ge(rstd_ready, norms[0])
                for h in range(8):
                    ins = pe.matmul(M[h // 2][:, (h % 2) * S:(h % 2 + 1) * S], ident[0:8, h:h + 1].to_broadcast([8, P]), rows,
                                    start=True, stop=True)
                ins.then_inc(heads_mm, 1)

            def ada(a, j, it=0, dn=0, rows=M[2]):
                slot, uses = use(A_AT[a], it, dn)
                pe.wait_ge(loaded[slot], 16 * (uses + 1))
                for k in range(KT):
                    g = k % 4
                    ins = pe.matmul(rows[32 * g:32 * g + 32, 0:P], cpad[:, k, 32 - 2 * j:64 - 2 * j], raw[:, slot, k, :],
                                    start=(j == 0 and k < 4), stop=(j == 3 and k >= KT - 4), skip_group_check=True)
                ins.then_inc(taken[slot], 1)

            def turn(group, modrow, cols=M[3]):
                pe.wait_ge(row_ready, group + 1)
                pe.matmul(cols[:, bass.ds(group * 8, 8)], modrow, sel[:, :], start=True, stop=True).then_inc(ada_cols, 1)

            pe.wait_ge(fills, 4)
            pe.wait_ge(boot, 112)
            pe.matmul(M[3][0:12, 0:BPITCH], relb[0:32, :], onehot[0:32, :], start=True, stop=True).then_inc(brow_mm, 1)
            pe.wait_ge(c_ready, 1)
            for j in range(4):
                ada(j, j)
            norm(sq0, KT, M[1])
            pe.wait_ge(brow_ready, 1)
            turn(0, modrow1)
            with pe.Fori(0, 7) as it:
                for j in range(4):
                    ada(4 + j, j, it, 4)
                turn(it + 1, modrow1)
            for j in range(4):
                gemm_T(gb("c_a") + j, opH, waits=quarters(0) if j == 0 else {})
            with pe.Fori(0, 6) as it:
                for j in range(4):
                    gemm_T(gb("c_a") + 4 + j, opH, it, 4)
            late = [("a_i", i) for i in range(8)] + [("b_v", i) for i in range(6)] + [("b_k", i) for i in range(6)] \
                + [("b_q", i) for i in range(6)] + [("a_g", i) for i in range(8)]

            def level(s):
                quarter, L = s // 9, s % 9
                hs = slice(2 * quarter, 2 * quarter + 2)
                q_, k_ = (qq[:, hs, :], kk[:, hs, :]) if L == 0 else (qs, ks)
                pe.wait_ge(lvl_prep, s + 1)
                if s >= 2:
                    pe.wait_ge(lvl_read, s - 1)
                for h in range(2):
                    if L < 8:
                        for t in range(2):
                            i = 2 * h + t
                            ins = pe.matmul(M[s % 2][:, i * P:(i + 1) * P], k_[:, h, t * P:(t + 1) * P],
                                            q_[:, h, t * P:(t + 1) * P], start=True, stop=True)
                    else:
                        ins = pe.matmul(M[s % 2][:, h * P:(h + 1) * P], k_[:, h, 0:P], q_[:, h, P:S], start=True, stop=True)
                ins.then_inc(lvl_mm, 1)

            def outputs(quarter):
                pe.wait_ge(lvl_read, 9 * quarter + 9)
                if quarter == 0:
                    was_read(pe, gb("a_i", 7))
                    for i in range(4, 7):
                        was_read(pe, gb("a_i", i))
                else:
                    pe.wait_ge(o_copied, quarter)
                for h in range(2):
                    o = h * S
                    hd = slice((2 * quarter + h) * P, (2 * quarter + h + 1) * P)
                    pe.matmul(M[3][:, o:o + P], ii[:, 0, hd], attn[:, 2 * h, :], start=True, stop=True)
                    pe.matmul(M[3][:, o + P:o + S], ii[:, 0, hd], attx[:, h, :], start=True, stop=False)
                    ins = pe.matmul(M[3][:, o + P:o + S], ii[:, 1, hd], attn[:, 2 * h + 1, :], start=False, stop=True)
                ins.then_inc(o_mm, 1)

            def beside(part, blocks, modrow, rows, cols):
                a0 = FIRST[part][2]
                for n in blocks:
                    if n % 4 == 0 and n:
                        turn((a0 + n) // 4 - 1, modrow, cols)
                    ada(a0 + n, n % 4, rows=rows)

            for s in range(36):
                if s < len(late):
                    part, i = late[s]
                    if part in ("a_i", "b_v"):
                        if i % 2 == 0:
                            rest = gemm_tokens(gb(part, i), opH, 2, later=True)
                        else:
                            rest()
                    else:
                        gemm_T(gb(part, i), opH)
                if s and s % 9 == 0:
                    outputs(s // 9 - 1)
                if s == 14:
                    pe.wait_ge(conv_tap, CONV_DVE * C_TAPS)
                    pe.wait_ge(conv_side, CONV_SIDE)
                    for t in range(C_TILES):
                        ins = pe.matmul(M[2][:, S:512], ones[:, :], cy[:, t, :], start=(t == 0), stop=(t == C_TILES - 1))
                    ins.then_inc(mean_mm, 1)
                if s == 17:
                    norm(ca, C_TILES)
                if s == 34:
                    for i in range(4):
                        was_read(pe, gb("a_g", 4 + i))
                if s >= 34:
                    beside("ada_b", (2 * s - 68, 2 * s - 67), modrow_b, G[2], G[3])
                level(s)
            outputs(3)
            norm_heads(fP)
            beside("ada_b", range(4, 6), modrow_b, G[2], G[3])
            spread_heads(kk[0:8, 0, :])
            beside("ada_b", range(6, 4 * EARLY), modrow_b, G[2], G[3])
            pe.wait_ge(ya_ready, 1)
            for u in range(9):
                if u < 8:
                    T, slot = u // 4, u % 4
                    w = P * (T + 1)
                    if u >= 1:
                        pe.wait_ge(log_ready, u)
                    for g in range(3):
                        h = 4 * g + slot
                        po = 64 * (h % 2)
                        out = M[0][:, g * S:g * S + w] if g < 2 else M[1][:, 0:w]
                        ins = pe.matmul(out, bq[po:po + 64, h // 2, T * P:(T + 1) * P], bk[po:po + 64, h // 2, 0:w],
                                        start=True, stop=True)
                    ins.then_inc(qk_mm, 1)
                n = 4 * EARLY + 3 * u
                if u < 8:
                    beside("ada_b", (n, n + 1), modrow_b, G[2], G[3])
                if u >= 1:
                    T, slot, e = (u - 1) // 4, (u - 1) % 4, (u - 1) % 2
                    pe.wait_ge(dg_ready, u)
                    if u >= 2:
                        pe.wait_ge(pt_ready, u - 1)
                    chunks = [(g, st) for g in range(3) for st in range(T + 1)]
                    for i, (g, st) in enumerate(chunks):
                        ins = pe.matmul(M[2 + i // 4][:, (i % 4) * P:(i % 4 + 1) * P], blog[e][:, g, st * P:(st + 1) * P],
                                        bdg[e], start=True, stop=True)
                    ins.then_inc(pt_mm, 1)
                    pe.wait_ge(pt_ready, u)
                    if u >= 3:
                        pe.wait_ge(yb_ready, u - 2)
                    po = 64 * (slot % 2)
                    for i, (g, st) in enumerate(chunks):
                        hc = (4 * g + slot) * 64
                        ins = pe.matmul(G[e][po:po + 64, 0:P], bv[:, st, hc:hc + 64], bpt[e][:, i, :],
                                        start=(i == 0), stop=(i == len(chunks) - 1))
                    ins.then_inc(pv_mm, 1)
                if u < 8:
                    beside("ada_b", (n + 2,), modrow_b, G[2], G[3])
            turn(FIRST["ada_b"][2] // 4 + 7, modrow_b, G[3])
            pe.wait_ge(yb_ready, 8)
            pe.wait_ge(mod_read, 1)

            def merge_round(it, r):
                b = gb("merge") + 4 * r
                for j in range(3):
                    gemm_T(b + j, opH, it, 4)
                if r == 0:
                    pe.wait_ge(y_ready, 1)
                pe.wait_ge(merged_part, it + r + 1)
                product(b + 3, [features(M[0][:, 0:S], opY1, 0, 8), features(M[1][:, 0:S], opY1, 8, 10, kw=8),
                                features(bank(b + 3)[:, 0:S], opY1, 10, 16, kw=10)], it, 4)

            merge_round(0, 0)
            with pe.Fori(0, 15) as it:
                merge_round(it, 1)
            pe.wait_ge(h_ready, 1)

            def mixed_round(section, op, it, r, waits={}):
                b0, a0 = gb(section) + 4 * r, FIRST[section][2] + 4 * r
                for j in range(3):
                    gemm_T(b0 + j, op, it, 8, waits=waits if j == 0 else {})
                    ada(a0 + j, j, it, 8)
                ada(a0 + 3, 3, it, 8)
                gemm_T(b0 + 3, op, it, 8)
                turn(it + a0 // 4, modrow2)

            def plain_round(section, op, it, r, kt=KT, waits={}):
                for j in range(4):
                    gemm_T(gb(section) + 4 * r + j, op, it, 4, kt=kt, waits=waits if r == j == 0 else {})

            def normed(section, a_round, sq, first=0, also=lambda: None):
                for r in range(first):
                    a_round(section, 0, r)
                with pe.Fori(0, 3 - first) as it:
                    a_round(section, it, first)
                also()
                norm_parts(sq, (0, 1))
                a_round(section, 0, 3)
                norm_parts(sq, (2, 3))

            normed("w_o", lambda s, it, r: mixed_round(s, opG, it, r), sq1)
            norm_parts(sq1, range(4))
            mixed_round("up1_0", opH, 0, 0, waits=quarters(1))
            for q in range(QUARTER):
                section = f"up1_{q}"
                if q == 1:
                    pe.wait_ge(c_ready, 2)
                with pe.Fori(0, 3 if q == 0 else 4) as it:
                    if section in MIXED:
                        mixed_round(section, opH, it, 1 if q == 0 else 0)
                    else:
                        plain_round(section, opH, it, 0)
                last = 16 * (q + 1) + 2
                pe.wait_ge(up_ready, last - 1)
                waits = {KT - 1: (up_ready, last)}
                if q < 3:
                    plain_round(f"down1_{q}", opU1, 0, 0, waits=waits)
                    with pe.Fori(0, 3) as it:
                        plain_round(f"down1_{q}", opU1, it, 1)
            normed("down1_3", lambda s, it, r: plain_round(s, opU1, it, r, waits=waits), sqd1, first=1, also=lambda: norm(sqc, KT))
            norm_parts(sqx, range(4))
            for i in range(8):
                gemm_T(gb("m_q", i), opW, cols=slice(S, 512), waits=quarters(2) if i == 0 else {})
            with pe.Fori(0, 2) as it:
                for j in range(4):
                    gemm_T(gb("m_k") + j, opW, it, 4, slice(0, 512))
            gemm_T(gb("m_g"), opW, cols=slice(0, 512))
            for i in range(0, 8, 2):
                gemm_tokens(gb("m_v", i), opW, 4)
            pe.wait_ge(rows_ready, 1)
            for d in range(2):
                for t in range(4):
                    ins = pe.matmul(M[1][:, d * 32 + t * 8:d * 32 + t * 8 + 8], gG[0:8, 2 * d, t * P:(t + 1) * P],
                                    ident[0:8, 0:8], start=True, stop=True)
            ins.then_inc(at_mm, 1)
            pe.wait_ge(silu_done, 1)
            pe.wait_ge(at_ready, 1)
            for i in range(4):
                was_read(pe, gb("m_v", 4 + i))

            def scores(h, half):
                if 2 * h + half >= 3:
                    pe.wait_ge(ws_ready, 2 * (h - 1 + half))
                for t in range(2 * half, 2 * half + 2):
                    ins = pe.matmul(scores_of(h, half)[:, (t % 2) * S:(t % 2 + 1) * S],
                                    mk[:, h, t * P:(t + 1) * P], mq[:, h, :], start=True, stop=True)
                ins.then_inc(s_mm, 1)

            for u in range(17):
                if u < 16:
                    h, d = u // 2, u % 2
                    if d == 0:
                        scores(h, 0)
                    if u >= 2:
                        pe.wait_ge(floor_ready, u - 1)
                    beside("ada_m", (2 * u,), modrow_m, G[3], G[3])
                    pe.matmul(M[d][:, :], ident[0:8, h:h + 1].to_broadcast([8, P]),
                              grows[0:8, d, :, :].rearrange("p a b -> p (a b)"), start=True, stop=True).then_inc(bc_mm, 1)
                if u >= 1:
                    h, d = (u - 1) // 2, (u - 1) % 2
                    pe.wait_ge(ws_ready, u)
                    if u >= 3:
                        pe.wait_ge(fin_ready, u - 2)
                    last, half, cut = tiles_of(d)
                    for o, lhs in ((0, None), (S, ones[:, :])):
                        for t in (0, 1, last, half):
                            c = slice(0, S) if t != half else cut
                            ins = pe.matmul(M[2 + d][:, o + c.start:o + c.stop], mv[:, t, h * P:(h + 1) * P] if lhs is None else lhs,
                                            mW[d][:, t, c], start=(t == 0), stop=(t == half), skip_group_check=True)
                    ins.then_inc(nd_mm, 1)
                if u < 16:
                    if u % 2 == 0:
                        scores(u // 2, 1)
                    beside("ada_m", (2 * u + 1,), modrow_m, G[3], G[3])
            turn(FIRST["ada_m"][2] // 4 + 7, modrow_m, G[3])
            pe.wait_ge(fin_ready, 16)
            for i in range(8):
                gemm_T(gb("m_o", i), opW, cols=slice(S, 512))
            with pe.Fori(0, 2) as it:
                for j in range(4):
                    gemm_T(gb("d_q") + j, opW, it, 4, slice(S, 512))
            norm_heads(nsq)
            gemm_T(gb("d_k"), opW, cols=slice(0, 512))
            spread_heads(nrs[0:8, 0, :])
            for i in range(1, 8):
                gemm_T(gb("d_k", i), opW, cols=slice(0, 512))
            pe.wait_ge(lam_in, 1)
            pe.matmul(M[3][:, 0:2], ones[0:64, :], lamp[0:64, :], start=True, stop=True).then_inc(lam_mm, 1)
            for i in range(0, 8, 2):
                gemm_tokens(gb("d_v", i), opW, 4)
                if i == 0:
                    pe.wait_ge(tab_in, 48)
                    for n in range(4):
                        was_read(pe, gb("d_k", 4 + n))
                for c in range(i, i + 2):
                    if c >= 2:
                        pe.wait_ge(rope_done, c - 1)
                    for j in range(2):
                        src = dq[:, 2 * c + j, :] if c < 4 else dk[:, 2 * (c - 4) + j, S:512]
                        ins = pe.matmul(M[c % 2][:, j * S:(j + 1) * S], rtab[:, 0:P], src, start=True, stop=True)
                    ins.then_inc(rot_mm, 1)
            for i in range(4):
                was_read(pe, gb("d_v", 4 + i))
            pe.wait_ge(rope_done, 8)
            for u in range(18):
                if u < 16:
                    h, T = u // 2, u % 2
                    if u >= 2:
                        pe.wait_ge(dexp, u - 1)
                    for c in range(2):
                        ins = pe.matmul(scores_bank(u, c)[:, :], dq[64 * c:64 * c + 64, h, T * P:(T + 1) * P], dk[64 * c:64 * c + 64, h, :],
                                        start=True, stop=True)
                    ins.then_inc(dqk_mm, 1)
                if u >= 2:
                    e = u % 2
                    pe.wait_ge(dpd_ready, u - 1)
                    for t in range(4):
                        ins = pe.transpose(M[2][:, t * P:(t + 1) * P], dpd[e][:, t * P:(t + 1) * P], ident[:, :])
                    ins.then_inc(dpt_mm, 1)
                if u < 16:
                    beside("ada_d", (2 * u, 2 * u + 1), modrow_d, G[2], G[3])
                if u >= 2:
                    h, e = (u - 2) // 2, u % 2
                    pe.wait_ge(dpt_ready, u - 1)
                    pe.wait_ge(lam_exp, 1)
                    if u >= 3:
                        pe.wait_ge(dy_ready, u - 2)
                    for t in range(4):
                        ins = pe.matmul(M[3][:, 0:P], dv[:, t, h * P:(h + 1) * P], dPT[e][:, t, :], start=(t == 0), stop=(t == 3))
                    ins.then_inc(dpv_mm, 1)
            turn(FIRST["ada_d"][2] // 4 + 7, modrow_d, G[3])
            norm_heads(dq)
            spread_heads(dk[0:8, 0, 0:S])
            pe.wait_ge(h_ready, 2)
            normed("w_out", lambda s, it, r: plain_round(s, opY2, it, r), sq2, first=1)
            norm_parts(sq2, range(4))
            for j in range(4):
                gemm_T(gb("up2_0", j), opH, waits=quarters(3) if j == 0 else {})
            for q in range(QUARTER):
                with pe.Fori(0, 4 if q == 0 else 5) as it:
                    plain_round(f"up2_{q}", opH, it, 1 if q == 0 else 0)
                for j in range(20, 22):
                    gemm_T(gb(f"up2_{q}", j), opH)
                last = UP2 * (q + 1) + 2
                pe.wait_ge(ffn_done, last - 1)
                waits = {UP2 - 1: (ffn_done, last)}
                if q < 3:
                    plain_round(f"down2_{q}", opU2, 0, 0, UP2, waits)
                    with pe.Fori(0, 3) as it:
                        plain_round(f"down2_{q}", opU2, it, 1, UP2)
            normed("down2_3", lambda s, it, r: plain_round(s, opU2, it, r, UP2, waits), sq2, first=1)

        @block.vector
        def _(dve):
            step = Chain(dve, dve_step)
            norms, heads, splits = [0], [0], [0]

            def split_low(b, it=0, dn=0):
                if b >= len(G_AT):
                    return
                slot, _ = use(G_AT[b])
                kt = kt_of(b)
                dve.wait_ge(hi_ready, b + 1 + it * 4)
                if b >= 2:
                    done(dve, b - 2, it)
                dve.tensor_tensor(parts[:, b % 2, 1, 0:kt, :], raw[:, slot, 0:kt, :], parts[:, b % 2, 0, 0:kt, :].bitcast(F32),
                                  ALU.subtract).then_inc(taken[slot], 1)

            def rounds(section, body, first=0, chained=0, between=lambda: None):
                for r in range(first):
                    body(0, r)
                n = rounds_of(section) - 1 - first
                with dve.Fori(0, n) as it:
                    step.offset = it * chained
                    body(it, first)
                step.n += chained * (n - 1)
                step.offset = 0
                between()
                body(0, rounds_of(section) - 1)

            def in_round(section, it, r):
                b = gb(section) + 4 * r
                return b, lambda j: split_low(b + j + 2, it, steps_of(section))

            def only_split(section, first=0):
                def body(it, r):
                    _, ahead = in_round(section, it, r)
                    for j in range(4):
                        ahead(j)
                rounds(section, body, first)

            def low(dst, src, hi):
                splits[0] += 1
                dve.wait_ge(hh_ready, splits[0])
                dve.tensor_tensor(dst, src, hi.bitcast(F32), ALU.subtract).then_inc(h_ready, 1)

            def invert(t, scale, sums=M[2]):
                norms[0] += 1
                dve.wait_ge(ms_ready, norms[0])
                step(dve.tensor_scalar(t, sums[0:t.shape[0], 0:S], scale, EPS, ALU.mult, ALU.add))
                dve.reciprocal(t, t).then_inc(inv_ready, 1)
                dve.wait_ge(rstd_ready, norms[0])

            def norm_heads(y, t):
                invert(t, 1.0 / P, M[0])
                heads[0] += 1
                dve.wait_ge(heads_mm, heads[0])
                for n in range(4):
                    last = dve.tensor_tensor(y[:, 2 * n:2 * n + 2, :], y[:, 2 * n:2 * n + 2, :],
                                             M[n][:, :].rearrange("p (a b) -> p a b", a=2), ALU.mult)
                step(last)

            def over_tiles(t, n=KT):
                return t.unsqueeze(1).to_broadcast([P, n, t.shape[-1]])

            def modulate(dst, src, rs, mul, add):
                step(dve.tensor_tensor(dst, src, over_tiles(rs), ALU.mult))
                for k in range(KT):
                    last = dve.tensor_scalar(dst[:, k, :], dst[:, k, :], mul[:, k:k + 1], add[:, k:k + 1], ALU.mult, ALU.add)
                last.then_inc(hf_ready, 1)

            def modulate_parts(op, hf, src, rs, mul, add, n):
                for c in range(5):
                    if c < 4:
                        if rs is not None:
                            step(dve.tensor_tensor(quarter_of(hf, c), quarter_of(src, c), over_tiles(rs, 4), ALU.mult))
                        for k in range(4 * c, 4 * c + 4):
                            last = dve.tensor_scalar(hf[:, k, :], hf[:, k, :], mul[:, k:k + 1], add[:, k:k + 1], ALU.mult, ALU.add)
                        last.then_inc(hf_part, 1)
                    if c >= 1:
                        dve.wait_ge(hh_part, 4 * n + c)
                        dve.tensor_tensor(quarter_of(op[:, 1], c - 1), quarter_of(hf, c - 1), quarter_of(op[:, 0], c - 1).bitcast(F32),
                                          ALU.subtract).then_inc(h_part, 1)
                dve.wait_ge(h_part, 4 * n + 4)

            def residual(t, mul):
                for c in range(4):
                    step(dve.tensor_tensor(quarter_of(t, c), quarter_of(t, c), over_tiles(rstd[:, 0:S], 4), ALU.mult))
                    for k in range(4 * c, 4 * c + 4):
                        last = dve.scalar_tensor_tensor(xT[:, k, :], t[:, k, :], mul[:, k:k + 1], xT[:, k, :], ALU.mult, ALU.add)
                    last.then_inc(x_ready, 1)

            dve.wait_ge(brow_mm, 1)
            dve.wait_ge(boot, 112)
            dve.tensor_tensor(brow[0:12, :], M[3][0:12, 0:BPITCH], bmask[0:12, :], ALU.add).then_inc(brow_ready, 1)
            step(dve.tensor_copy(lvl_mask[:, :, :], lvl_f))
            dve.wait_ge(x_in, 16)
            invert(rstd[:, 0:S], 1.0 / D, M[1])
            step(dve.tensor_tensor(hf0, xT, over_tiles(rstd[:, 0:S]), ALU.mult))
            lg = v("lb", 0, 8)
            step(dve.tensor_tensor(sm_e, lg, lg, ALU.subtract))
            step(dve.tensor_scalar(lbc, sm_e, 0.0, TINY, ALU.max, ALU.add))
            step(dve.tensor_scalar(lb1, sm_e, 0.0, None, ALU.max))
            step(dve.tensor_scalar(lb1, lb1, -1.0, 1.0, ALU.mult, ALU.add))
            split_low(0)
            split_low(1)
            dve.wait_ge(ada_cols, 8)
            step(dve.tensor_tensor(mod1[:, 0:32], M[3][:, 0:64:2], v("b_ada", 0, 32), ALU.add))
            step(dve.scalar_tensor_tensor(amul, mod1[:, 16:32], 1.0, v("mix_pre", 0, 16), ALU.add, ALU.mult))
            modulate_parts(opH, hf0, None, None, amul, mod1, 0)
            for b in range(gb("c_a"), gb("c_g", 6)):
                split_low(b + 2)
            taps = 0
            for i in range(16):
                split_low(gb("a_f") + i + 2)
                if i == 0:
                    dve.wait_ge(conv_u, 2)
                for _ in range(min(6, C_TAPS * CONV_DVE - taps)):
                    t, j = taps % CONV_DVE, taps // CONV_DVE
                    if j == 0:
                        ins = dve.tensor_scalar(cy[:, t, :], upad[:, t, 0:S], conv_tap_of(t, 0), v("conv_b", t), ALU.mult, ALU.add)
                    else:
                        dve.wait_ge(conv_tap, taps - CONV_DVE + 1)
                        ins = dve.scalar_tensor_tensor(cy[:, t, :], upad[:, t, j:j + S], conv_tap_of(t, j), cy[:, t, :],
                                                       ALU.mult, ALU.add)
                    ins.then_inc(conv_tap, 1)
                    taps += 1
            assert taps == C_TAPS * CONV_DVE
            for i in range(8):
                was_read(dve, gb("a_f", i))
                was_read(dve, gb("a_q", i))
            for h in range(8):
                dve.tensor_scalar(fP[:, h, :], fP[:, h, :], lb1[:, h:h + 1], lbc[:, h:h + 1], ALU.mult, ALU.add)
                last = dve.tensor_scalar(kk[:, h, :], kk[:, h, :], lb1[:, h:h + 1], None, ALU.mult)
            step(last)
            for s in range(36):
                quarter, L = s // 9, s % 9
                hs = slice(2 * quarter, 2 * quarter + 2)
                f_, q_, k_ = fP[:, hs, :], qq[:, hs, :], kk[:, hs, :]
                if L == 0:
                    dve.memset(suf, 1.0).then_inc(lvl_prep, 1)
                    dve.wait_ge(lvl_prep, s + 1)
                else:
                    dve.wait_ge(lvl_mm, s)
                    dve.tensor_tensor(qs, q_, f_, ALU.mult)
                    dve.tensor_tensor(ks, k_, suf, ALU.mult).then_inc(lvl_prep, 1)
                    dve.wait_ge(lvl_prep, s + 1)
                    if L < 8:
                        w = 1 << (L - 1)
                        fv_ = f_.rearrange("p h (b two w) -> p (h b) two w", two=2, w=w)
                        sv_ = suf.rearrange("p h (b two w) -> p (h b) two w", two=2, w=w)
                        nb = 2 * S // (2 * w)
                        step(dve.tensor_tensor(sv_[:, :, 0, :], sv_[:, :, 0, :],
                                               fv_[:, :, 1, w - 1:w].to_broadcast([P, nb, w]), ALU.mult))
                        step(dve.tensor_tensor(fv_[:, :, 1, :], fv_[:, :, 1, :],
                                               fv_[:, :, 0, w - 1:w].to_broadcast([P, nb, w]), ALU.mult))
                if s == 15:
                    dve.wait_ge(mean_mm, 1)
                    step(dve.tensor_scalar(rstd[:, S:512], M[2][:, S:512], 1.0 / (C_TILES * P), None, ALU.mult))
                    dve.tensor_tensor(cy, cy, over_tiles(rstd[:, S:512], C_TILES), ALU.subtract).then_inc(conv_cent, 1)
                if s == 18:
                    invert(rstd[:, 0:S], 1.0 / (C_TILES * P))
                    dve.wait_ge(conv_cent, 1)
                    dve.tensor_tensor(cy, cy, over_tiles(rstd[:, 0:S], C_TILES), ALU.mult).then_inc(yc_in, 1)
                if s < 14:
                    for n in (s + 1, s + 2) if s % 2 else ():
                        split_low(gb("a_i") + n)
                elif s < 34:
                    split_low(gb("a_i") + s + 2)
                dve.wait_ge(lvl_mm, s + 1)
                if s % 9 == 0 and s:
                    dve.wait_ge(o_mm, quarter)
                bank4 = M[s % 2][:, :].rearrange("p (a b) -> p a b", a=4)
                if L == 0:
                    last = dve.tensor_tensor(attn, bank4, over_tiles(ident[:, :], 4), ALU.mult)
                elif L < 8:
                    last = dve.copy_predicated(attn, lvl_mask[:, L:L + 1, :].to_broadcast([P, 4, P]), bank4)
                else:
                    last = dve.tensor_copy(attx, bank4[:, 0:2, :])
                last.then_inc(lvl_read, 1)
                dve.wait_ge(lvl_read, s + 1)
            for i in range(8):
                was_read(dve, gb("a_g", i))
            norm_heads(qq, kk[0:8, 0, :])
            dve.scalar_tensor_tensor(og, qq, v("hgrn_w"), og, ALU.mult, ALU.mult).then_inc(ya_ready, 1)
            dve.wait_ge(bias_in, 16)
            for u in range(9):
                if u >= 1:
                    e = (u - 1) % 2
                    dve.wait_ge(exp_ready, u)
                    step(dve.reciprocal(rz[e][:, 0:1], zz[e][:, 0:1]))
                    dve.tensor_scalar(bdg[e], ident[:, :], rz[e][:, 0:1], None, ALU.mult).then_inc(dg_ready, 1)
                if u < 8:
                    T, slot, e = u // 4, u % 4, u % 2
                    w = P * (T + 1)
                    b0 = 0 if T else P
                    dve.wait_ge(qk_mm, u + 1)
                    if u >= 2:
                        dve.wait_ge(pt_mm, u - 1)
                    psum01 = M[0][:, :].rearrange("p (a b) -> p a b", a=2)
                    dve.scalar_tensor_tensor(blog[e][:, 0:2, 0:w], psum01[:, :, 0:w], 0.125,
                                             bias[:, slot:slot + 5:4, b0:b0 + w], ALU.mult, ALU.add)
                    step(dve.scalar_tensor_tensor(blog[e][:, 2, 0:w], M[1][:, 0:w], 0.125, bias[:, 8 + slot, b0:b0 + w],
                                                  ALU.mult, ALU.add))
                    step(dve.tensor_reduce(nm[e][:, 0:1], blog[e][:, :, 0:w], mybir.AxisListType.XY, ALU.max))
                    dve.tensor_scalar(nm[e][:, 0:1], nm[e][:, 0:1], -1.0, None, ALU.mult).then_inc(log_ready, 1)
                if u >= 1:
                    e, T = (u - 1) % 2, (u - 1) // 4
                    nch = 3 * (T + 1)
                    dve.wait_ge(pt_mm, u)
                    if u >= 3:
                        dve.wait_ge(pv_mm, u - 2)
                    last = dve.tensor_copy(bpt[e][:, 0:min(nch, 4), :],
                                           M[2][:, 0:min(nch, 4) * P].rearrange("p (a b) -> p a b", b=P))
                    if nch > 4:
                        last = dve.tensor_copy(bpt[e][:, 4:nch, :], M[3][:, 0:(nch - 4) * P].rearrange("p (a b) -> p a b", b=P))
                    last.then_inc(pt_ready, 1)
            dve.wait_ge(ada_cols, 16)
            step(dve.tensor_tensor(mod1[:, 32:64], G[3][:, 64:128:2], v("b_ada", 32, 32), ALU.add))
            dve.sem_inc(mod_read, 1)
            dve.wait_ge(y_hi, 1)
            for k0, k1, t in ((0, 8, og), (8, 10, yb), (10, 16, yc)):
                last = dve.tensor_tensor(opY1[:, 1, k0:k1, :], t, opY1[:, 0, k0:k1, :].bitcast(F32), ALU.subtract)
            last.then_inc(y_ready, 1)

            dve.wait_ge(y_ready, 1)
            dve.sem_inc(merged_part, 1)

            def merge_round(it, r):
                b0, ahead = in_round("merge", it, r)
                for j in range(3):
                    ahead(j)
                for g in range(3):
                    was_read(dve, b0 + g, it)
                done(dve, b0 + 3, it)
                g_ = gates[:, 0]
                t = bass.ds(it + r, 1)
                dve.tensor_tensor(mtmp[:, 0, :], M[0][:, 0:S], g_[:, 0, :], ALU.mult)
                step(dve.tensor_tensor(mtmp[:, 1, :], M[1][:, 0:S], g_[:, 1, :], ALU.mult))
                step(dve.tensor_tensor(mtmp[:, 0, :], mtmp[:, 0, :], mtmp[:, 1, :], ALU.add))
                step(dve.tensor_tensor(mtmp[:, 1, :], bank(b0 + 3)[:, 0:S], g_[:, 2, :], ALU.mult))
                dve.sem_inc(bank_read[(b0 + 3) % 4], 1)
                dve.sem_inc(merged_part, 1)
                step(dve.tensor_tensor(mfp[:, 0, :], mtmp[:, 0, :], mtmp[:, 1, :], ALU.add))
                gh, gl = (opG[:, p, t, :].rearrange("p a b -> p (a b)") for p in range(2))
                step(dve.tensor_copy(gh, mfp[:, 0, :]))
                step(dve.tensor_tensor(gl, mfp[:, 0, :], gh.bitcast(F32), ALU.subtract))
                ahead(3)

            rounds("merge", merge_round, 1, chained=6)
            dve.sem_inc(h_ready, 1)
            only_split("w_o")
            step(dve.tensor_tensor(gmul, mod1[:, 32:48], v("mix_post", 0, 16), ALU.mult))
            dve.wait_ge(ada_cols, 20)
            step(dve.tensor_tensor(mod1[:, 64:80], M[3][:, 128:160:2], v("b_ada", 64, 16), ALU.add))
            step(dve.scalar_tensor_tensor(amul, mod1[:, 64:80], 1.0, v("mlp_pre", 0, 16), ALU.add, ALU.mult))
            invert(rstd[:, 0:S], 1.0 / D, M[1])
            residual(proj1, gmul)
            invert(rstd[:, 0:S], 1.0 / D, M[1])
            modulate_parts(opH, hf1, xT, rstd[:, 0:S], amul, mod1[:, 48:64], 1)
            dve.sem_inc(up_ready, 2)

            def norm_context():
                step(dve.scalar_tensor_tensor(cmul, mod2[:, 1, 16:32], 1.0, v("g_pre_mix", 0, 16), ALU.add, ALU.mult))
                invert(rstd[:, 0:S], 1.0 / D)
                modulate(hfc, hfc, rstd[:, 0:S], cmul, mod2[:, 1, 0:16])

            def add_round(section, acc, **more):
                def body(it, r):
                    b0, ahead = in_round(section, it, r)
                    for j in range(4):
                        done(dve, b0 + j, it)
                        t = acc[:, bass.ds(j + it * 4 + 4 * r, 1), :].rearrange("p a b -> p (a b)")
                        dve.tensor_tensor(t, bank(b0 + j)[:, 0:S], t, ALU.add).then_inc(bank_read[(b0 + j) % 4], 1)
                        ahead(j)
                rounds(section, body, **more)

            for q in range(QUARTER):
                def up_round(it, r, section=f"up1_{q}"):
                    b0, ahead = in_round(section, it, r)
                    for j in range(4):
                        was_read(dve, b0 + j, it)
                        t = bass.ds(j + it * 4 + 4 * r, 1)
                        uh, ul = (opU1[:, p, t, :].rearrange("p a b -> p (a b)") for p in range(2))
                        relu, sq = ut[:, j % 2, 0, :], ut[:, j % 2, 1, :]
                        dve.tensor_tensor(sq, relu, relu, ALU.mult)
                        step(dve.tensor_tensor(uh, relu, relu, ALU.mult))
                        dve.tensor_tensor(ul, sq, uh.bitcast(F32), ALU.subtract).then_inc(up_ready, 1)
                        ahead(j)
                rounds(f"up1_{q}", up_round, chained=4)
                if q == 0:
                    only_split("down1_0")
                elif q < 3:
                    add_round(f"down1_{q}", down1)
                else:
                    dve.wait_ge(ada_cols, 32)
                    step(dve.tensor_tensor(mod1[:, 80:96], M[3][:, 160:192:2], v("b_ada", 80, 16), ALU.add))
                    step(dve.tensor_tensor(gmul, mod1[:, 80:96], v("mlp_post", 0, 16), ALU.mult))
                    for r in range(2):
                        last = dve.tensor_tensor(mod2[:, r, 0:32], M[3][:, 192 + r:256:2], v("b_mod", 0, 32), ALU.add)
                    step(last)
                    step(dve.scalar_tensor_tensor(amul, mod2[:, 0, 16:32], 1.0, v("g_pre_mix", 0, 16), ALU.add, ALU.mult))
                    add_round("down1_3", down1, between=norm_context)
            invert(rstd[:, 0:S], 1.0 / D, M[1])
            residual(down1, gmul)
            splits[0] += 1
            dve.wait_ge(hh_ready, splits[0])
            step(dve.tensor_tensor(opW[:, 1, :, 0:S], hfc, opW[:, 0, :, 0:S].bitcast(F32), ALU.subtract))
            invert(rstd[:, S:512], 1.0 / D, M[1])
            modulate_parts(opW[:, :, :, S:512], hfx, xT, rstd[:, S:512], amul, mod2[:, 0, 0:16], 2)

            def outer_taps(part, i, dst, tile0, wide, seen):
                b = gb(part, i)
                t = tile0 + i
                src, y = bank(b)[:, 0:512 if wide else S], dst[:, i, :]
                if wide:
                    src, y = (a.rearrange("p (s t) -> p s t", s=2) for a in (src, y))
                else:
                    src, y = src.unsqueeze(1), y.unsqueeze(1)
                dve.wait_ge(conv3_in, seen + 1)
                step(dve.scalar_tensor_tensor(y[:, :, 1:S], src[:, :, 0:S - 1], v("qk_w", t), y[:, :, 1:S], ALU.mult, ALU.add))
                dve.scalar_tensor_tensor(y[:, :, 0:S - 1], src[:, :, 1:S], v("qk_w", 32 + t), y[:, :, 0:S - 1],
                                         ALU.mult, ALU.add).then_inc(conv3_done, 1)
                dve.wait_ge(conv3_done, seen + 1)
                dve.sem_inc(bank_read[b % 4], 1)
                split_low(b + 2)

            for i in range(8):
                outer_taps("m_q", i, mq, 0, False, i)
            for i in range(8):
                outer_taps("m_k", i, mk, 8, True, 8 + i)
            for i in range(5):
                split_low(gb("m_g") + i + 2)
            dve.wait_ge(ln_ready, 1)
            one = ones[0:8, 0:1].to_broadcast([8, 512])
            one_s = ones[0:8, 0:1].to_broadcast([8, S])
            g8 = gG[0:8]
            step(dve.scalar_tensor_tensor(g8[:, 1:4:2, :], g8[:, 1:4:2, :], 0.0, gtmp[0:8, :, :], ALU.min, ALU.subtract))
            B8, M8 = gB[0:8], gM[0:8]
            last_c = slice(0, 1)
            dve.tensor_tensor_scan(B8[:, 0, :], one, g8[:, 1, :], 0.0, ALU.mult, ALU.add)
            step(dve.tensor_tensor_scan(B8[:, 1, 0:S][:, ::-1], one_s, g8[:, 3, 0:S][:, ::-1], 0.0, ALU.mult, ALU.add))
            step(dve.tensor_tensor_scan(B8[:, 1, S:512][:, ::-1], one_s, g8[:, 3, S:512][:, ::-1], B8[:, 1, last_c],
                                        ALU.mult, ALU.add))
            step(dve.tensor_tensor(g8[:, 0:4:2, :], g8[:, 0:4:2, :], B8[:, :, :], ALU.subtract))
            dve.tensor_tensor_scan(M8[:, 0, :], one, g8[:, 0, :], 0.0, ALU.mult, ALU.max)
            step(dve.tensor_tensor_scan(M8[:, 1, 0:S][:, ::-1], one_s, g8[:, 2, 0:S][:, ::-1], 0.0, ALU.mult, ALU.max))
            step(dve.tensor_tensor_scan(M8[:, 1, S:512][:, ::-1], one_s, g8[:, 2, S:512][:, ::-1], M8[:, 1, last_c],
                                        ALU.mult, ALU.max))
            r8 = grows[0:8]
            dve.tensor_scalar(r8[:, :, 0, :], M8[:, :, S:512], -1.0, None, ALU.mult)
            dve.scalar_tensor_tensor(r8[:, :, 1, :], B8[:, :, S:512], -1.0, M8[:, :, S:512], ALU.mult, ALU.subtract)\
               .then_inc(rows_ready, 1)
            for i in range(5, 9):
                split_low(gb("m_g") + i + 2)
            dve.wait_ge(at_mm, 1)
            step(dve.tensor_copy(aT.rearrange("p a b c -> p (a b c)"), M[1][:, 0:64]))
            dve.sem_inc(at_ready, 1)
            dve.wait_ge(tab_in, 32)
            scale = float(P) ** -0.5
            for u in range(18):
                if 1 <= u <= 16:
                    h, d = (u - 1) // 2, (u - 1) % 2
                    dve.wait_ge(w_ready, u)
                    dve.wait_ge(s_mm, 2 * h + 2)
                    whole, half, cut = tiles_of(d)
                    for t0, t1, c in ((0, 2, slice(0, S)), (whole, whole + 1, slice(0, S)), (half, half + 1, cut)):
                        sc = scores_of(h, t0 // 2)[:, :].rearrange("p (a b) -> p a b", a=2)[:, t0 % 2:t0 % 2 + t1 - t0, c]
                        last = dve.scalar_tensor_tensor(mW[d][:, t0:t1, c], sc, scale, mW[d][:, t0:t1, c], ALU.mult, ALU.mult)
                    last.then_inc(ws_ready, 1)
                if u < 16:
                    h, d = u // 2, u % 2
                    dve.wait_ge(bc_mm, u + 1)
                    if u >= 2:
                        dve.wait_ge(nd_mm, u - 1)
                    half = tiles_of(d)[1]
                    for t in range(2):
                        dve.tensor_scalar(mW[d][:, t, :], M[d][:, 0:S], aT[:, d, t, h:h + 1], 0.0, ALU.add, ALU.min)
                    for t in (2, 3):
                        a = aT[:, d, t, h:h + 1]
                        c = slice((t - 2) * P, (t - 1) * P)
                        last = dve.scalar_tensor_tensor(mW[d][:, t, c], M[d][:, c], a, tri[d], ALU.add, ALU.min)
                        if t != half:
                            c = slice(P, S) if d == 0 else slice(0, P)
                            last = dve.tensor_scalar(mW[d][:, t, c], M[d][:, c], a, 0.0, ALU.add, ALU.min)
                    last.then_inc(w_arg, 1)
                if u >= 2:
                    h, d = (u - 2) // 2, (u - 2) % 2
                    dve.wait_ge(den_ready, u - 1)
                    if u == 17:
                        dve.wait_ge(ada_cols, 40)
                        step(dve.tensor_tensor(mod2[:, 0, 32:64], G[3][:, 256:320:2], v("b_mod", 32, 32), ALU.add))
                    step(dve.tensor_tensor(mfl[d], mfl[d], mden, ALU.max))
                    step(dve.reciprocal(mfl[d], mfl[d]))
                    num = M[2 + d][:, 0:S]
                    if d == 0:
                        dve.tensor_tensor(ym[:, h, :], num, mfl[d], ALU.mult).then_inc(fin_ready, 1)
                    else:
                        step(dve.tensor_tensor(mfl[d], num, mfl[d], ALU.mult))
                        dve.wait_ge(fin_ready, u - 2)
                        dve.tensor_tensor(ym[:, h, :], ym[:, h, :], mfl[d], ALU.add).then_inc(fin_ready, 1)
            for b in range(gb("m_o"), gb("d_q", 8)):
                split_low(b + 2)
            for i in range(8):
                was_read(dve, gb("m_o", i))
            norm_heads(ym, nrs[0:8, 0, :])
            for h in range(8):
                last = dve.scalar_tensor_tensor(ym[:, h, :], ym[:, h, :], v("g_mlstm", h), mo[:, h, :], ALU.mult, ALU.mult)
            last.then_inc(ym_ready, 1)
            dve.wait_ge(ym_ready, 1)
            lv = v("lam", 0, 4)[0:64, :]
            dve.tensor_tensor(lamp[0:64, :], lv[:, 0:4:2], lv[:, 1:4:2], ALU.mult).then_inc(lam_in, 1)
            for i in range(8):
                split_low(gb("d_k", i) + 2)
            for i in range(8):
                was_read(dve, gb("d_q", i))
                was_read(dve, gb("d_k", i))
            dve.wait_ge(tab_in, 48)
            cos = rtab[:, P:P + S].unsqueeze(1).to_broadcast([P, 2, S])
            sin = rtab[:, P + S:P + 2 * S].unsqueeze(1).to_broadcast([P, 2, S])
            for c in range(8):
                split_low(gb("d_v", c) + 2)
                dve.wait_ge(rot_mm, c + 1)
                t = dq[:, 2 * c:2 * c + 2, :] if c < 4 else dk[:, 2 * (c - 4):2 * (c - 4) + 2, S:512]
                dve.tensor_tensor(rtmp, M[c % 2][:, :].rearrange("p (a b) -> p a b", a=2), sin, ALU.mult)
                step(dve.tensor_tensor(t, t, cos, ALU.mult))
                dve.tensor_tensor(t, t, rtmp, ALU.add).then_inc(rope_done, 1)
                dve.wait_ge(rope_done, c + 1)
            dve.wait_ge(lam_exp, 1)
            step(dve.tensor_tensor(lamn, lame[:, 1:2], lame[:, 0:1], ALU.subtract))
            step(dve.tensor_scalar(lamn, lamn, -LAM_INIT, None, ALU.add))
            for u in range(17):
                if u < 16:
                    e = u % 2
                    dve.wait_ge(dqk_mm, u + 1)
                    dve.tensor_reduce(nm[e][:, 0:1], scores_bank(u, 0)[:, :], AX_X, ALU.max)
                    step(dve.tensor_reduce(nm[e][:, 1:2], scores_bank(u, 1)[:, :], AX_X, ALU.max))
                    dve.tensor_scalar(nm[e], nm[e], -0.125, None, ALU.mult).then_inc(dmax, 1)
                if u >= 1:
                    e = (u - 1) % 2
                    dve.wait_ge(dexp, u)
                    step(dve.reciprocal(rz[e], zz[e]))
                    step(dve.tensor_tensor(rz[e][:, 1:2], rz[e][:, 1:2], lamn, ALU.mult))
                    if u >= 3:
                        dve.wait_ge(dpt_mm, u - 2)
                    step(dve.tensor_scalar(dpd[e], dE[e][:, 0, :], rz[e][:, 0:1], None, ALU.mult))
                    dve.scalar_tensor_tensor(dpd[e], dE[e][:, 1, :], rz[e][:, 1:2], dpd[e], ALU.mult, ALU.add)\
                       .then_inc(dpd_ready, 1)
            dve.wait_ge(ada_cols, 48)
            step(dve.tensor_tensor(mod2[:, 0, 64:96], G[3][:, 320:384:2], v("b_mod", 64, 32), ALU.add))
            norm_heads(yd, dk[0:8, 0, 0:S])
            dve.tensor_scalar(yd, yd, v("g_diff"), 1.0 - LAM_INIT, ALU.mult, ALU.mult).then_inc(hf_ready, 1)
            low(opY2[:, 1], region(0, KT, S), opY2[:, 0])
            only_split("w_out", 1)
            step(dve.tensor_tensor(gmul, mod2[:, 0, 32:48], v("g_post_mix", 0, 16), ALU.mult))
            step(dve.scalar_tensor_tensor(amul, mod2[:, 0, 64:80], 1.0, v("g_pre_ffn", 0, 16), ALU.add, ALU.mult))
            dve.wait_ge(x_back, 16)
            invert(rstd[:, 0:S], 1.0 / D, M[1])
            residual(proj2, gmul)
            invert(rstd[:, 0:S], 1.0 / D, M[1])
            modulate_parts(opH, hf2, xT, rstd[:, 0:S], amul, mod2[:, 0, 48:64], 3)
            dve.sem_inc(ffn_done, 2)
            for q in range(QUARTER):
                def pair(b, pos, tile, local, it, ahead):
                    for c in range(2):
                        dve.wait_ge(taps_in, pos * 2 + c + 1)
                        src, y = bank(b + c)[:, 0:S], fv[:, buffer_of(b), c, :]
                        w0, w2 = (vec[:, bass.ds(tile + VEC["ffn_w"] + side * 4 * FF2 + c * FF2, 1)] for side in range(2))
                        step(dve.scalar_tensor_tensor(y[:, 1:S], src[:, 0:S - 1], w0, y[:, 1:S], ALU.mult, ALU.add))
                        step(dve.scalar_tensor_tensor(y[:, 0:S - 1], src[:, 1:S], w2, y[:, 0:S - 1], ALU.mult, ALU.add))
                        dve.sem_inc(bank_read[(b + c) % 4], 1)
                        ahead(c)
                    dve.wait_ge(gate_silu, pos + 1)
                    e = buffer_of(b)
                    step(dve.tensor_tensor(ftm[:, e, :], fv[:, e, 0, :], fv[:, e, 1, :], ALU.mult))
                    uh, ul = (opU2[:, p, bass.ds(local, 1), :].rearrange("p a b -> p (a b)") for p in range(2))
                    step(dve.tensor_copy(uh, ftm[:, e, :]))
                    dve.tensor_tensor(ul, ftm[:, e, :], uh.bitcast(F32), ALU.subtract).then_inc(ffn_done, 1)

                b0, t0 = gb(f"up2_{q}"), q * UP2
                with dve.Fori(0, 5) as it:
                    step.offset = it * 12
                    for j in range(2):
                        pair(b0 + 2 * j, t0 + j + it * 2, t0 + j + it * 2, j + it * 2, it,
                             lambda c, j=j: split_low(b0 + 2 * j + c + 2, it, 4))
                step.n += 12 * 4
                step.offset = 0
                pair(b0 + 20, t0 + 10, t0 + 10, 10, 0, lambda c: split_low(b0 + 20 + c + 2))
                if q == 0:
                    only_split("down2_0")
                else:
                    add_round(f"down2_{q}", down2)
            step(dve.tensor_tensor(gmul, mod2[:, 0, 80:96], v("g_post_ffn", 0, 16), ALU.mult))
            invert(rstd[:, 0:S], 1.0 / D, M[1])
            residual(down2, gmul)


def constant_arrays():
    import math
    import numpy as np

    f = np.float32
    consts = np.zeros((P, NCONST), f)
    freqs, grid_w, base = 16, 64, 10000.0
    inv = (f(base) ** (-np.arange(freqs, dtype=f) / f(freqs))).astype(f)
    tok = np.arange(S)
    axis = np.stack([(tok // grid_w).astype(f), (tok % grid_w).astype(f)])
    perm = np.zeros((P, P), f)
    for p in range(P):
        ax, half, fr = (p // 32) % 2, (p // 16) % 2, p % 16
        ang = (axis[ax] * inv[fr]).astype(f)
        consts[p, CONST["cos"]:CONST["cos"] + S] = np.cos(ang)
        consts[p, CONST["sin"]:CONST["sin"] + S] = np.sin(ang)
        perm[p + 16 if half == 0 else p - 16, p] = -1.0 if half == 0 else 1.0
    consts[:, 0:P] = perm
    p, j = np.arange(P)[:, None], np.arange(P)[None, :]
    consts[:, CONST["tri_f"]:CONST["tri_f"] + P] = np.where(j >= p, 0.0, MASK_VALUE)
    consts[:, CONST["tri_b"]:CONST["tri_b"] + P] = np.where(j <= p, 0.0, MASK_VALUE)
    exact, buckets, far = 16, 32, 2048
    for i in range(BROW):
        d = 255 - i
        if d >= 0:
            if d < exact:
                b = d
            else:
                large = exact + int(np.float32(np.log(f(d) / f(exact)) / f(math.log(far / exact))) * f(buckets - exact))
                b = min(max(large, exact), buckets - 1)
            consts[b, CONST["onehot"] + i] = 1.0
    for g, (window, dil) in enumerate(((128, 1), (512, 4), (2048, 16))):
        for i in range(BPITCH):
            d = 255 - i
            ok = 0 <= d <= window and d % dil == 0
            consts[4 * g:4 * g + 4, CONST["bmask"] + i] = 0.0 if ok else MASK_VALUE
    s, t = np.arange(P)[:, None], np.arange(P)[None, :]
    lvl = np.zeros((P, 8, P), f)
    lvl[:, 0] = s == t
    for n in range(1, 8):
        w = 1 << (n - 1)
        lvl[:, n] = (s // (2 * w) == t // (2 * w)) & ((s // w) % 2 == 0) & ((t // w) % 2 == 1)
    ident = np.zeros((P, P + 8), f)
    ident[:, 0:P] = np.eye(P, dtype=f)
    for r in range(8):
        ident[r::32, P + r] = 1.0
    return consts, lvl, ident


def kernel(**inputs):
    import numpy as _np
    import concourse.bacc as _bacc
    from concourse.bass_utils import run_bass_kernel_spmd as _run

    a = {k: _np.asarray(x) for k, x in inputs.items()}

    def columns(x):
        return _np.ascontiguousarray(x.reshape(-1, P).T)

    def blocks(w):
        k, n = w.shape
        return w.reshape(k // P, P, n // P, P).transpose(2, 1, 0, 3)

    w_in, w_in_2 = blocks(a["w_in"][0]), a["w_in_2"][0]
    cuts = dict(a_q=(0, 8), a_f=(8, 16), a_i=(16, 24), a_g=(24, 32), b_q=(32, 38), b_k=(38, 44), b_v=(44, 50),
                c_a=(50, 56), c_g=(56, 62))
    parts = {k: w_in[i:j] for k, (i, j) in cuts.items()}
    gate = blocks(a["w_gate"][0]).reshape(3, KT, P, KT, P)
    branches = blocks(_np.concatenate([a["w_a_out"][0], a["w_b_out"][0], a["w_c_out"][0]]))
    parts["merge"] = [x for j in range(KT) for x in (gate[0, j], gate[1, j], gate[2, j], branches[j])]
    parts["w_o"], parts["w_out"] = blocks(a["w_o"][0]), blocks(a["w_out_2"][0])
    mg = 4 * 1024
    for name, at in (("m_q", 0), ("m_k", 1024), ("m_v", 2048), ("m_o", 3072), ("d_q", mg + 32), ("d_k", mg + 1056), ("d_v", mg + 2080)):
        parts[name] = blocks(w_in_2[:, at:at + 1024])
    for name in ("m_v", "d_v"):
        parts[name] = parts[name].reshape(4, 2, P, KT, P)[:, ::-1].reshape(8, P, KT, P)
    parts["m_g"] = blocks(_np.pad(w_in_2[:, mg:mg + 32], ((0, 0), (0, P - 32))))
    up1, up2 = blocks(a["w_up"][0]), blocks(a["w_up_2"][0])
    for q in range(QUARTER):
        n1, n2 = FF1 // QUARTER, UP2
        parts[f"up1_{q}"] = up1[q * n1:(q + 1) * n1]
        parts[f"down1_{q}"] = blocks(a["w_down"][0][q * n1 * P:(q + 1) * n1 * P])
        parts[f"up2_{q}"] = [x for j in range(q * n2, (q + 1) * n2) for x in (up2[j], up2[FF2 + j])]
        parts[f"down2_{q}"] = blocks(a["w_down_2"][0][q * n2 * P:(q + 1) * n2 * P])
    stream = _np.zeros((N_STREAM, P, KT, P), _np.float32)
    g_blocks = [x for name, n in BLOCKS.items() if n for x in parts[name]]
    a_blocks = [x for w in (a["w_ada"][0], a["w_mod_2"][0]) for x in blocks(w)]
    for at, some in ((G_AT, g_blocks), (A_AT, a_blocks)):
        assert len(at) == len(some)
        for n, x in zip(at, some):
            stream[n, :, 0:x.shape[1], :] = x

    vectors = dict(
        c1=a["c"][0], c2=a["c_2"][0], cctx=a["c_ctx_2"], b_ada=a["b_ada"][0], mix_pre=a["mix_norm_pre"][0],
        mix_post=a["mix_norm_post"][0], mlp_pre=a["mlp_norm_pre"][0], mlp_post=a["mlp_norm_post"][0],
        b_gate=a["b_gate"][0], lb=a["hgrn_lb_logits"][0], hgrn_w=a["hgrn_norm_w"][0],
        conv_w=a["conv_w"][0].reshape(C_TAPS, C_TILES, P).transpose(1, 0, 2), conv_b=a["conv_b"][0],
        ln_g=a["conv_ln_g"][0], ln_b=a["conv_ln_b"][0], b_mod=a["b_mod_2"][0], g_pre_mix=a["g_pre_mix_2"][0],
        g_post_mix=a["g_post_mix_2"][0], g_pre_ffn=a["g_pre_ffn_2"][0], g_post_ffn=a["g_post_ffn_2"][0],
        qk_w=a["conv_qk_w_2"][0], qk_b=a["conv_qk_b_2"][0], g_mlstm=a["g_mlstm_2"][0], g_diff=a["g_diff_2"][0],
        ffn_w=a["conv_ffn_w_2"][0], ffn_b=a["conv_ffn_b_2"][0])
    vec = _np.zeros((P, NVEC), _np.float32)
    for name, x in vectors.items():
        c = columns(x)
        vec[:, VEC[name]:VEC[name] + c.shape[1]] = c
    vec[0:32, VEC["mg_b"]] = a["b_gate_2"][0].reshape(-1)
    for i, name in enumerate(("lambda_q1_2", "lambda_k1_2", "lambda_q2_2", "lambda_k2_2")):
        vec[0:64, VEC["lam"] + i] = a[name][0]

    def tokens_last(x):
        return _np.ascontiguousarray(x.reshape(S, KT, P).transpose(2, 1, 0))

    consts, lvl, ident = constant_arrays()
    arrays = dict(
        stream=stream, x_t=tokens_last(a["x"][0]), ctx_t=tokens_last(a["ctx_2"][0]), vec=vec, consts=consts, lvl_mask=lvl, ident=ident,
        rel_bias=a["rel_bias"])

    nc = _bacc.Bacc("TRN2", target_bir_lowering=False, num_devices=1)
    aps = [nc.dram_tensor(k, x.shape, mybir.dt.from_np(x.dtype), kind="ExternalInput").ap() for k, x in arrays.items()]
    scratch = nc.dram_tensor("bias_rows", (B_HEADS, P * BPITCH), F32, kind="Internal").ap()
    x_keep = nc.dram_tensor("x_keep", (P, KT, S), F32, kind="Internal").ap()
    out = nc.dram_tensor("out_t", (P, KT, S), F32, kind="ExternalOutput").ap()
    two_blocks_kernel(nc, *aps, scratch, x_keep, out)
    got = _run(nc, [arrays], core_ids=[0]).results[0]["out_t"]
    return _np.ascontiguousarray(got.transpose(2, 1, 0)).reshape(1, S, D)
```
